# Optimizing a Trainium2 kernel written in Bass

```python
import jax
import jax.numpy as jnp
from jax import lax
import numpy as np

D_MODEL = 1024
BATCH = 1
SEQ = 512
DEPTH = 2

GRID_W = 64
CTX_LEN = 256
NORM_EPS = 1e-6
ROPE_BASE = 10000.0
N_MOD = 6

MLA_HEADS = 8
MLA_Q_LORA = 384
MLA_KV_LORA = 256
MLA_NOPE = 64
MLA_ROPE = 32
MLA_V = 64
MLA_WIDTH = MLA_HEADS * MLA_V
MLA_SCALE = (MLA_NOPE + MLA_ROPE) ** -0.5
ATTN_Q_BLOCK = 128

POOL_WINDOWS = (2, 4, 8, 16)
POOL_GROUPS = 4
POOL_GROUP_DIM = 128
POOL_WIDTH = POOL_GROUPS * POOL_GROUP_DIM

SWA_Q_HEADS = 8
SWA_KV_HEADS = 2
SWA_HEAD_DIM = 64
SWA_WINDOW = 128
SWA_BLOCK = 128
SWA_WIDTH = SWA_Q_HEADS * SWA_HEAD_DIM
SWA_SCALE = SWA_HEAD_DIM ** -0.5

N_BRANCHES = 3
IN_SPLITS = (MLA_Q_LORA, MLA_KV_LORA, MLA_ROPE, POOL_WIDTH, SWA_Q_HEADS * SWA_HEAD_DIM, SWA_KV_HEADS * SWA_HEAD_DIM, SWA_KV_HEADS * SWA_HEAD_DIM, N_BRANCHES * D_MODEL)
IN_OFFSETS = tuple(sum(IN_SPLITS[:j]) for j in range(len(IN_SPLITS) + 1))
IN_WIDTH = IN_OFFSETS[-1]

N_EXPERTS = 64
TOP_K = 8
N_GROUPS = 8
TOPK_GROUPS = 4
EXPERTS_PER_GROUP = N_EXPERTS // N_GROUPS
D_EXPERT = 256
D_SHARED = 256
ROUTED_SCALE = 2.5
MOE_BLOCK = 128

kernel_name = "hybrid_mla_pool_swa_moe_dit"

def rmsnorm(x, g):
    xf = x.astype(jnp.float32)
    y = xf * lax.rsqrt(jnp.mean(xf * xf, axis=-1, keepdims=True) + NORM_EPS)
    return (y * g.astype(jnp.float32)).astype(x.dtype)

def axial_rope_tables(n_tokens, rot_dim):
    rows = n_tokens // GRID_W
    t = jnp.arange(rows * GRID_W)
    row = (t // GRID_W).astype(jnp.float32)
    col = (t % GRID_W).astype(jnp.float32)
    n_freq = rot_dim // 4
    inv_freq = ROPE_BASE ** (-jnp.arange(n_freq, dtype=jnp.float32) / n_freq)
    ang_r = row[:, None] * inv_freq[None, :]
    ang_c = col[:, None] * inv_freq[None, :]
    return (jnp.cos(ang_r), jnp.sin(ang_r), jnp.cos(ang_c), jnp.sin(ang_c))

def apply_axial_rope(x, tabs):
    cos_r, sin_r, cos_c, sin_c = (t[None, :, None, :].astype(x.dtype) for t in tabs)
    r1, r2, c1, c2 = jnp.split(x, 4, axis=-1)
    return jnp.concatenate([r1 * cos_r - r2 * sin_r, r2 * cos_r + r1 * sin_r,
                            c1 * cos_c - c2 * sin_c, c2 * cos_c + c1 * sin_c], axis=-1)

def in_proj(h, w_in, first, last):
    y = h @ w_in[:, IN_OFFSETS[first]:IN_OFFSETS[last]]
    cuts = [IN_OFFSETS[j] - IN_OFFSETS[first] for j in range(first + 1, last)]
    return jnp.split(y, cuts, axis=-1)

def mla_queries(cq, g_q, w_uq):
    B, L, _ = cq.shape
    q = (rmsnorm(cq, g_q) @ w_uq).reshape(B, L, MLA_HEADS, MLA_NOPE + MLA_ROPE)
    return q[..., :MLA_NOPE], q[..., MLA_NOPE:]

def mla_keys(ckv, g_kv, w_ukv):
    B, L, _ = ckv.shape
    kv = (rmsnorm(ckv, g_kv) @ w_ukv).reshape(B, L, MLA_HEADS, MLA_NOPE + MLA_V)
    return kv[..., :MLA_NOPE], kv[..., MLA_NOPE:]

def mla_attend(q_nope, q_rope, k_nope, k_rope, v):
    s = jnp.einsum('bqhd,bkhd->bhqk', q_nope, k_nope) + jnp.einsum('bqhd,bkd->bhqk', q_rope, k_rope)
    p = jax.nn.softmax(s.astype(jnp.float32) * MLA_SCALE, axis=-1).astype(v.dtype)
    return jnp.einsum('bhqk,bkhd->bqhd', p, v)

def mla_latent_attention(q_nope, q_rope, k_nope, k_rope, v, ck_nope, ck_rope, cv):
    B, S = q_nope.shape[:2]
    nb = S // ATTN_Q_BLOCK
    kn = jnp.concatenate([ck_nope, k_nope], axis=1)
    kr = jnp.concatenate([ck_rope, k_rope], axis=1)
    vv = jnp.concatenate([cv, v], axis=1)

    def to_blocks(t):
        return jnp.moveaxis(t.reshape((B, nb, ATTN_Q_BLOCK) + t.shape[2:]), 1, 0)

    out = lax.map(lambda qb: mla_attend(qb[0], qb[1], kn, kr, vv), (to_blocks(q_nope), to_blocks(q_rope)))
    return jnp.moveaxis(out, 0, 1).reshape(B, S, MLA_WIDTH)

def multiscale_pool(u, w_pool, pool_scale):
    B, L, _ = u.shape
    uf = u.astype(jnp.float32)
    cs = jnp.pad(jnp.cumsum(uf, axis=1), ((0, 0), (1, 0), (0, 0)))
    t = jnp.arange(L)
    outs = []
    for j, w in enumerate(POOL_WINDOWS):
        lo = jnp.clip(t - w // 2, 0, L)
        hi = jnp.clip(t + w - w // 2, 0, L)
        cnt = (hi - lo).astype(jnp.float32)[None, :, None]
        sl = slice(j * POOL_GROUP_DIM, (j + 1) * POOL_GROUP_DIM)
        cs_g = cs[:, :, sl]
        outs.append((cs_g[:, hi] - cs_g[:, lo]) / cnt - uf[:, :, sl])
    pooled = jnp.concatenate(outs, axis=-1).astype(u.dtype).reshape(B, L, POOL_GROUPS, POOL_GROUP_DIM)
    mixed = jnp.einsum('blgc,gcd->blgd', pooled, w_pool).reshape(B, L, POOL_WIDTH)
    return mixed * pool_scale

def swa_latent_attention(q, k, v, kc, vc, sink):
    B, S = q.shape[:2]
    G = SWA_Q_HEADS // SWA_KV_HEADS
    nb = S // SWA_BLOCK
    qb = q.reshape(B, nb, SWA_BLOCK, SWA_KV_HEADS, G, SWA_HEAD_DIM)

    def band(t):
        tp = jnp.pad(t, ((0, 0), (SWA_BLOCK, SWA_BLOCK), (0, 0), (0, 0)))
        tp = tp.reshape(B, nb + 2, SWA_BLOCK, SWA_KV_HEADS, SWA_HEAD_DIM)
        return jnp.concatenate([tp[:, :-2], tp[:, 1:-1], tp[:, 2:]], axis=2)

    kb, vb = band(k), band(v)
    blk = jnp.arange(nb)[:, None, None]
    qpos = blk * SWA_BLOCK + jnp.arange(SWA_BLOCK)[None, :, None]
    kpos = (blk - 1) * SWA_BLOCK + jnp.arange(3 * SWA_BLOCK)[None, None, :]
    mask = (jnp.abs(qpos - kpos) <= SWA_WINDOW) & (kpos >= 0) & (kpos < S)
    s_band = jnp.einsum('bnqhgd,bnkhd->bnhgqk', qb, kb).astype(jnp.float32) * SWA_SCALE
    s_band = jnp.where(mask[None, :, None, None], s_band, -jnp.inf)
    s_ctx = jnp.einsum('bnqhgd,bchd->bnhgqc', qb, kc).astype(jnp.float32) * SWA_SCALE
    s_sink = jnp.broadcast_to(sink.astype(jnp.float32).reshape(1, 1, SWA_KV_HEADS, G, 1, 1), s_band.shape[:-1] + (1,))
    p = jax.nn.softmax(jnp.concatenate([s_band, s_ctx, s_sink], axis=-1), axis=-1).astype(v.dtype)
    n_band = 3 * SWA_BLOCK
    n_ctx = kc.shape[1]
    out = (jnp.einsum('bnhgqk,bnkhd->bnqhgd', p[..., :n_band], vb)
           + jnp.einsum('bnhgqc,bchd->bnqhgd', p[..., n_band:n_band + n_ctx], vc))
    return out.reshape(B, S, SWA_WIDTH)

def swa_context_attention(q, k, v, sink):
    B, C = q.shape[:2]
    G = SWA_Q_HEADS // SWA_KV_HEADS
    qg = q.reshape(B, C, SWA_KV_HEADS, G, SWA_HEAD_DIM)
    s = jnp.einsum('bqhgd,bkhd->bhgqk', qg, k).astype(jnp.float32) * SWA_SCALE
    s_sink = jnp.broadcast_to(sink.astype(jnp.float32).reshape(1, SWA_KV_HEADS, G, 1, 1), s.shape[:-1] + (1,))
    p = jax.nn.softmax(jnp.concatenate([s, s_sink], axis=-1), axis=-1)[..., :-1].astype(v.dtype)
    return jnp.einsum('bhgqk,bkhd->bqhgd', p, v).reshape(B, C, SWA_WIDTH)

def merge_branches(gate_logits, y_mla, y_pool, y_swa, w_br_mla, w_br_pool, w_br_swa, w_out):
    g_mla, g_pool, g_swa = jnp.split(jax.nn.sigmoid(gate_logits), N_BRANCHES, axis=-1)
    merged = g_mla * (y_mla @ w_br_mla) + g_pool * (y_pool @ w_br_pool) + g_swa * (y_swa @ w_br_swa)
    return merged @ w_out

def token_mixers(h_lat, h_ctx, ctx_out, w_in, g_mla_q, g_mla_kv, w_mla_uq, w_mla_ukv, w_pool, pool_scale,
                 swa_sink, w_br_mla, w_br_pool, w_br_swa, w_out, rope_mla, rope_swa):
    B, S, _ = h_lat.shape
    C = h_ctx.shape[1]
    cq, ckv, kr, u, qs, ks, vs, gl = in_proj(h_lat, w_in, 0, 8)
    q_nope, q_rope = mla_queries(cq, g_mla_q, w_mla_uq)
    k_nope, v_mla = mla_keys(ckv, g_mla_kv, w_mla_ukv)
    q_rope = apply_axial_rope(q_rope, rope_mla)
    k_rope = apply_axial_rope(kr[:, :, None, :], rope_mla)[:, :, 0, :]
    qs = apply_axial_rope(qs.reshape(B, S, SWA_Q_HEADS, SWA_HEAD_DIM), rope_swa)
    ks = apply_axial_rope(ks.reshape(B, S, SWA_KV_HEADS, SWA_HEAD_DIM), rope_swa)
    vs = vs.reshape(B, S, SWA_KV_HEADS, SWA_HEAD_DIM)
    if ctx_out:
        ccq, cckv, ckr, cu, cqs, cks, cvs, cgl = in_proj(h_ctx, w_in, 0, 8)
    else:
        cckv, ckr = in_proj(h_ctx, w_in, 1, 3)
        cks, cvs = in_proj(h_ctx, w_in, 5, 7)
    ck_nope, cv_mla = mla_keys(cckv, g_mla_kv, w_mla_ukv)
    cks = cks.reshape(B, C, SWA_KV_HEADS, SWA_HEAD_DIM)
    cvs = cvs.reshape(B, C, SWA_KV_HEADS, SWA_HEAD_DIM)
    y_mla = mla_latent_attention(q_nope, q_rope, k_nope, k_rope, v_mla, ck_nope, ckr, cv_mla)
    y_pool = multiscale_pool(u, w_pool, pool_scale)
    y_swa = swa_latent_attention(qs, ks, vs, cks, cvs, swa_sink)
    y_lat = merge_branches(gl, y_mla, y_pool, y_swa, w_br_mla, w_br_pool, w_br_swa, w_out)
    if not ctx_out:
        return y_lat, None
    cq_nope, cq_rope = mla_queries(ccq, g_mla_q, w_mla_uq)
    cy_mla = mla_attend(cq_nope, cq_rope, ck_nope, ckr, cv_mla).reshape(B, C, MLA_WIDTH)
    cy_pool = multiscale_pool(cu, w_pool, pool_scale)
    cy_swa = swa_context_attention(cqs.reshape(B, C, SWA_Q_HEADS, SWA_HEAD_DIM), cks, cvs, swa_sink)
    y_ctx = merge_branches(cgl, cy_mla, cy_pool, cy_swa, w_br_mla, w_br_pool, w_br_swa, w_out)
    return y_lat, y_ctx

def moe_ffn(h, w_router, router_bias, w_eg, w_eu, w_ed, w_sg, w_su, w_sd):
    T, D = h.shape
    scores = jax.nn.sigmoid((h @ w_router).astype(jnp.float32))
    sel = scores + router_bias.astype(jnp.float32)
    grp_score = lax.top_k(sel.reshape(T, N_GROUPS, EXPERTS_PER_GROUP), 2)[0].sum(-1)
    grp_idx = lax.top_k(grp_score, TOPK_GROUPS)[1]
    grp_mask = jnp.any(grp_idx[:, :, None] == jnp.arange(N_GROUPS)[None, None, :], axis=1)
    sel = jnp.where(jnp.repeat(grp_mask, EXPERTS_PER_GROUP, axis=1), sel, -jnp.inf)
    idx = lax.top_k(sel, TOP_K)[1]
    wts = jnp.take_along_axis(scores, idx, axis=1)
    wts = wts / jnp.sum(wts, axis=-1, keepdims=True) * ROUTED_SCALE
    A = T * TOP_K
    flat_e = idx.reshape(-1)
    flat_w = wts.reshape(-1)
    order = jnp.argsort(flat_e)
    sorted_e = flat_e[order]
    counts = jnp.bincount(flat_e, length=N_EXPERTS)
    padded = (counts + MOE_BLOCK - 1) // MOE_BLOCK * MOE_BLOCK
    pad_end = jnp.cumsum(padded)
    pad_start = pad_end - padded
    start = jnp.cumsum(counts) - counts
    dest = pad_start[sorted_e] + jnp.arange(A) - start[sorted_e]
    n_rows = -(-(A + N_EXPERTS * (MOE_BLOCK - 1)) // MOE_BLOCK) * MOE_BLOCK
    n_blocks = n_rows // MOE_BLOCK
    row_tok = jnp.full((n_rows,), T, jnp.int32).at[dest].set((order // TOP_K).astype(jnp.int32))
    row_w = jnp.zeros((n_rows,), h.dtype).at[dest].set(flat_w[order].astype(h.dtype))
    block_e = jnp.minimum(jnp.searchsorted(pad_end, jnp.arange(n_blocks) * MOE_BLOCK, side='right'), N_EXPERTS - 1)
    h_pad = jnp.concatenate([h, jnp.zeros((1, D), h.dtype)], axis=0)

    def expert_block(args):
        tok, e = args
        xb = h_pad[tok]
        return (jax.nn.silu(xb @ w_eg[e]) * (xb @ w_eu[e])) @ w_ed[e]

    y = lax.map(expert_block, (row_tok.reshape(n_blocks, MOE_BLOCK), block_e)).reshape(n_rows, D)
    routed = jnp.zeros((T + 1, D), h.dtype).at[row_tok].add(y * row_w[:, None])[:T]
    shared = (jax.nn.silu(h @ w_sg) * (h @ w_su)) @ w_sd
    return routed + shared

def setup_inputs(seed: int = 0) -> dict:
    key = jax.random.key(seed)
    ks = jax.random.split(key, 32)
    f32 = jnp.float32

    def nrm(k, shape, scale):
        return jax.random.normal(k, shape, f32) * scale

    L = DEPTH
    return {
        "x": nrm(ks[0], (BATCH, SEQ, D_MODEL), 1.0),
        "c": nrm(ks[1], (BATCH, D_MODEL), 1.0),
        "ctx": nrm(ks[2], (BATCH, CTX_LEN, D_MODEL), 1.0),
        "c_ctx": nrm(ks[3], (D_MODEL,), 1.0),
        "w_mod": nrm(ks[4], (L, D_MODEL, N_MOD * D_MODEL), 0.5 * D_MODEL ** -0.5),
        "b_mod": nrm(ks[5], (L, N_MOD * D_MODEL), 0.02),
        "g_mix": 1.0 + nrm(ks[6], (L, D_MODEL), 0.05),
        "g_ffn": 1.0 + nrm(ks[7], (L, D_MODEL), 0.05),
        "w_in": nrm(ks[8], (L, D_MODEL, IN_WIDTH), D_MODEL ** -0.5),
        "g_mla_q": 1.0 + nrm(ks[9], (L, MLA_Q_LORA), 0.05),
        "g_mla_kv": 1.0 + nrm(ks[10], (L, MLA_KV_LORA), 0.05),
        "w_mla_uq": nrm(ks[11], (L, MLA_Q_LORA, MLA_HEADS * (MLA_NOPE + MLA_ROPE)), MLA_Q_LORA ** -0.5),
        "w_mla_ukv": nrm(ks[12], (L, MLA_KV_LORA, MLA_HEADS * (MLA_NOPE + MLA_V)), MLA_KV_LORA ** -0.5),
        "w_pool": nrm(ks[13], (L, POOL_GROUPS, POOL_GROUP_DIM, POOL_GROUP_DIM), POOL_GROUP_DIM ** -0.5),
        "pool_scale": 1.0 + nrm(ks[14], (L, POOL_WIDTH), 0.1),
        "swa_sink": nrm(ks[15], (L, SWA_Q_HEADS), 0.5),
        "w_br_mla": nrm(ks[16], (L, MLA_WIDTH, D_MODEL), MLA_WIDTH ** -0.5),
        "w_br_pool": nrm(ks[17], (L, POOL_WIDTH, D_MODEL), POOL_WIDTH ** -0.5),
        "w_br_swa": nrm(ks[18], (L, SWA_WIDTH, D_MODEL), SWA_WIDTH ** -0.5),
        "w_out": nrm(ks[19], (L, D_MODEL, D_MODEL), D_MODEL ** -0.5),
        "w_router": nrm(ks[20], (L, D_MODEL, N_EXPERTS), D_MODEL ** -0.5),
        "router_bias": nrm(ks[21], (L, N_EXPERTS), 0.01),
        "w_exp_gate": nrm(ks[22], (L, N_EXPERTS, D_MODEL, D_EXPERT), D_MODEL ** -0.5),
        "w_exp_up": nrm(ks[23], (L, N_EXPERTS, D_MODEL, D_EXPERT), D_MODEL ** -0.5),
        "w_exp_down": nrm(ks[24], (L, N_EXPERTS, D_EXPERT, D_MODEL), D_EXPERT ** -0.5),
        "w_sh_gate": nrm(ks[25], (L, D_MODEL, D_SHARED), D_MODEL ** -0.5),
        "w_sh_up": nrm(ks[26], (L, D_MODEL, D_SHARED), D_MODEL ** -0.5),
        "w_sh_down": nrm(ks[27], (L, D_SHARED, D_MODEL), D_SHARED ** -0.5),
        "g_final": 1.0 + nrm(ks[28], (D_MODEL,), 0.05),
    }

def reference(x, c, ctx, c_ctx, w_mod, b_mod, g_mix, g_ffn, w_in, g_mla_q, g_mla_kv, w_mla_uq, w_mla_ukv,
              w_pool, pool_scale, swa_sink, w_br_mla, w_br_pool, w_br_swa, w_out, w_router, router_bias,
              w_exp_gate, w_exp_up, w_exp_down, w_sh_gate, w_sh_up, w_sh_down, g_final):
    B, S, D = x.shape
    C = ctx.shape[1]
    rope_mla = axial_rope_tables(S, MLA_ROPE)
    rope_swa = axial_rope_tables(S, SWA_HEAD_DIM)
    xc = ctx
    for i in range(DEPTH):
        last = i == DEPTH - 1
        mod_lat = (jax.nn.silu(c) @ w_mod[i] + b_mod[i])[:, None, :]
        mod_ctx = (jax.nn.silu(c_ctx) @ w_mod[i] + b_mod[i])[None, None, :]
        sh1, sc1, gt1, sh2, sc2, gt2 = jnp.split(mod_lat, N_MOD, axis=-1)
        csh1, csc1, cgt1, csh2, csc2, cgt2 = jnp.split(mod_ctx, N_MOD, axis=-1)
        h_lat = rmsnorm(x, g_mix[i]) * (1 + sc1) + sh1
        h_ctx = rmsnorm(xc, g_mix[i]) * (1 + csc1) + csh1
        y_lat, y_ctx = token_mixers(h_lat, h_ctx, not last, w_in[i], g_mla_q[i], g_mla_kv[i], w_mla_uq[i],
                                    w_mla_ukv[i], w_pool[i], pool_scale[i], swa_sink[i], w_br_mla[i],
                                    w_br_pool[i], w_br_swa[i], w_out[i], rope_mla, rope_swa)
        x = x + gt1 * y_lat
        f_lat = (rmsnorm(x, g_ffn[i]) * (1 + sc2) + sh2).reshape(B * S, D)
        moe_args = (w_router[i], router_bias[i], w_exp_gate[i], w_exp_up[i], w_exp_down[i],
                    w_sh_gate[i], w_sh_up[i], w_sh_down[i])
        if last:
            x = x + gt2 * moe_ffn(f_lat, *moe_args).reshape(B, S, D)
        else:
            xc = xc + cgt1 * y_ctx
            f_ctx = (rmsnorm(xc, g_ffn[i]) * (1 + csc2) + csh2).reshape(B * C, D)
            f_out = moe_ffn(jnp.concatenate([f_lat, f_ctx], axis=0), *moe_args)
            x = x + gt2 * f_out[:B * S].reshape(B, S, D)
            xc = xc + cgt2 * f_out[B * S:].reshape(B, C, D)
    return rmsnorm(x, g_final)


_drawn_inputs = setup_inputs


def setup_inputs(seed=0):
    import zlib

    import numpy as np

    out = dict(_drawn_inputs(seed))
    spreads = {}
    factors = {'g_mla_q': 8.0, 'g_mla_kv': 3.198, 'swa_sink': 24.019}
    for name, (base, spread) in spreads.items():
        noise = np.random.default_rng([zlib.crc32(name.encode()), seed]).standard_normal(out[name].shape)
        drawn = base * np.exp(spread * noise) if base else spread * noise
        out[name] = jnp.asarray(drawn.astype(out[name].dtype))
    for name, factor in factors.items():
        out[name] = (out[name] * factor).astype(out[name].dtype)
    return out
```

```python
from contextlib import ExitStack

import concourse.bass as bass
from concourse import mybir

F32, BF16, I32 = mybir.dt.float32, mybir.dt.bfloat16, mybir.dt.int32
ALU, ACT, AX = mybir.AluOpType, mybir.ActivationFunctionType, mybir.AxisListType

P = 128
D, DEPTH, SEQ, CTX = 1024, 2, 512, 256
DK = D // P
TOK = CTX + SEQ
NT, CT = TOK // P, CTX // P
EPS = 1e-6
QL, KVL, ROPE, POOLW, SWQ, SWKV = 384, 256, 32, 512, 512, 128
OFF_CQ, OFF_CKV, OFF_U, OFF_QS, OFF_KS, OFF_G = 0, 384, 672, 1184, 1696, 1952
HEADS, NOPE, VD, HD = 8, 64, 64, 64
MLA_SCALE, SWA_SCALE = (NOPE + ROPE) ** -0.5, HD ** -0.5
E, DE, TOPK, GROUPS, KEEP = 64, 256, 8, 8, 4
ROUTED = 2.5
NEG = -1e30
UW = 800
UC, UL = 8, 8 + CTX + 16
MAXB = TOK // P
TABN = 120
UNROLL = 4
HROW = D + E
RING, SLOT = 3, 4096
NVEC = 73
V_B, V_GM, V_GF, V_PS, V_GQ, V_GKV = 0, 48, 56, 64, 68, 71

CONSTS = {}
_at = 0
for _name, _n in (("ident", 128), ("ones", 128), ("perm16", 128), ("perm8", 128), ("tri", 128), ("tokid", 3 * NT),
                  ("thr", MAXB), ("iotan", TABN), ("dummy", 1), ("negdummy", 1), ("edges", 64), ("lower", 64),
                  ("slot1", TOK)):
    CONSTS[_name] = (_at, _at + _n)
    _at += _n
NCONST = _at
MASK, MASK2 = 640, 512


def active(l):
    return list(range(NT)) if l < DEPTH - 1 else list(range(CT, NT))


def max_blocks(l):
    n = (len(active(l)) * P * TOPK + E * (P - 1)) // P
    return -(-n // UNROLL) * UNROLL


class Job:
    def __init__(self, kind, args, drain, slot, fill, count):
        self.kind, self.args, self.drain, self.slot, self.fill, self.count = kind, args, drain, slot, fill, count


def make_plan():
    jobs, names, panels = [], {}, []
    counts = {"act": 0, "dve": 0}

    def add(kind, *args, drain=None, panel=None):
        if drain is None:
            jobs.append(Job(kind, args, None, None, None, None))
            return
        counts[drain] += 1
        n = counts["act"] + counts["dve"]
        job = Job(kind, args, drain, (n - 1) % 3, n, counts[drain])
        jobs.append(job)
        names[(kind,) + args] = job
        for p in (panel if isinstance(panel, list) else [panel] if panel else []):
            if not panels or all(q[0] != p for q in panels):
                panels.append([p, job])
            for q in panels:
                if q[0] == p:
                    q[1] = job

    def attention(l, br):
        items = [(t, h) for t in active(l) for h in range(HEADS)]
        late = []
        add("S", l, br, 0, drain="act" if br == "m" else "dve")
        for i in range(len(items) + 2):
            if i + 1 < len(items):
                add("S", l, br, i + 1, drain="act" if br == "m" else "dve")
            if i < len(items):
                add("T", l, br, i, drain="act" if i % 2 else "dve")
            for t in late:
                add("yT", l, br, t, drain="act")
            late = []
            if 1 <= i <= len(items):
                add("PV", l, br, i - 1)
                if items[i - 1][1] == HEADS - 1:
                    late.append(items[i - 1][0])

    alt = ["act", "dve"]
    add("cvec", drain="act")
    for l in range(DEPTH):
        add("vec", l, drain="dve")
    for l in range(DEPTH):
        for p in range(12):
            add("mod", l, p, drain="dve", panel=("mod", l, p))
    for l in range(DEPTH):
        A = active(l)
        for k in range(DK):
            add("h", l, k, drain=alt[k % 2])
        for c in range(3):
            add("cq", l, c, drain="act", panel=("cq", l))
        for c in range(2):
            add("ckv", l, c, drain="act", panel=("ckv", l))
        add("kr", l, drain="act", panel=("ckv", l))
        add("rq", l, drain="dve")
        add("rk", l, drain="dve")
        add("krp", l, drain="dve")
        for j in range(2):
            add("qr", l, j, drain="act", panel=("uq", l))
            add("qrp", l, j, drain="dve")
        for j in range(4):
            add("qn", l, j, drain=alt[j % 2], panel=("uq", l))
        for j in range(4):
            add("kn", l, j, drain=alt[j % 2], panel=("ukv", l))
        for t in range(NT):
            add("v", l, t, drain=alt[t % 2], panel=("ukv", l))
        attention(l, "m")
        for c in range(4):
            add("qs", l, c, drain="act", panel=("qs", l))
            add("qsp", l, c, drain="dve")
        add("ks", l, drain="act", panel=("ks", l))
        add("ksp", l, drain="dve")
        add("vs", l, drain="act", panel=("ks", l))
        for c in range(4):
            add("u", l, c, drain="act", panel=("u", l))
        attention(l, "s")
        for g in range(4):
            add("pm", l, g, drain="dve", panel=("pm", l))
        for n2 in range(DK // 2):
            for b in range(3):
                for c in range(2):
                    add("g", l, n2, b, c, drain="act", panel=("merge", l, n2, b))
                    add("b", l, n2, b, c, drain="dve", panel=("merge", l, n2, b))
        streams = (0, 1) if l < DEPTH - 1 else (0,)
        for which in ("gt1", "A2", "B2"):
            for s in streams:
                add("bc", l, which, s, drain="act")
        for i, t in enumerate(A):
            add("o", l, t, drain="dve", panel=[("wo", l, 0), ("wo", l, 1)])
            if i:
                add("f", l, A[i - 1], drain="act")
        for s in streams:
            add("bc", l, "gt2", s, drain="act")
        add("f", l, A[-1], drain="act")
        for t in A:
            add("r", l, t, drain="act", panel=("router", l))
        for i, t in enumerate(A):
            add("sg", l, t, drain="dve", panel=("shgu", l))
            add("sT", l, t, drain="act")
            add("sd", l, t, drain="act", panel=("shd", l))
        for t in A:
            add("pos", l, t, drain="dve")
        add("cnt", l, drain="dve")
        add("end", l, drain="dve")
        add("tab", l, drain="dve")
        add("moe", l)
    return jobs, names, panels


def build(nc, x, c, ctx, c_ctx, w_mod, b_mod, g_mix, g_ffn, w_in, g_mla_q, g_mla_kv, w_mla_uq, w_mla_ukv, w_pool,
          pool_scale, swa_sink, w_br_mla, w_br_pool, w_br_swa, w_out, w_router, router_bias, w_exp_gate, w_exp_up,
          w_exp_down, w_sh_gate, w_sh_up, w_sh_down, g_final, consts, mask, rope_mla, rope_swa, out):
    H = nc.dram_tensor("h_rows", [TOK + P, HROW], F32, kind="Internal").ap()
    ACC = [nc.dram_tensor(f"acc{i}", [TOK + P, D], F32, kind="Internal").ap() for i in range(2)]
    XS = nc.dram_tensor("x_saved", [TOK, D], F32, kind="Internal").ap()
    jobs, names, panels = make_plan()
    panel_no = {p[0]: n for n, p in enumerate(panels)}

    with ExitStack() as stack:
        def sb(name, n, dt=F32, rows=P):
            return stack.enter_context(nc.sbuf_tensor(name, [rows, n], dt))

        def sem(name):
            return stack.enter_context(nc.semaphore(name))

        XA = sb("region_x", 6144)
        HT = sb("region_h", 6144)
        Q = sb("region_q", 6144)
        K = sb("region_k", 6144)
        VY = sb("region_v", 6144)
        C = sb("region_c", 4608)
        ring = sb("ring", RING * SLOT)
        con = sb("con", NCONST)
        masks = sb("masks", MASK + MASK2, BF16)

        def cst(name, rows=P):
            a, b = CONSTS[name]
            return con[0:rows, a:b]
        ident = cst("ident")
        vecs = sb("vecs", P)
        cT = sb("cT", 16)
        vecT = sb("vecT", DEPTH * NVEC)
        modT = sb("modT", DEPTH * 96)
        AB = sb("AB", DEPTH * 32)
        ssq, rstd = sb("ssq", 8), sb("rstd", 8)
        zero = sb("zero", 256)
        scores = sb("scores", NT * E)
        posm = sb("posm", NT * E)
        rt = sb("rt", 6 * E)
        rsm = sb("rsm", 64)
        Mb = sb("Mb", NT * E, BF16)
        onesb, trib, tokb = sb("onesb", P, BF16), sb("trib", P, BF16), sb("tokb", 3 * NT, BF16)
        nbb, Gb = sb("nbb", 2, BF16), sb("Gb", TABN, BF16)
        endc = sb("endc", 16)
        tab = sb("tab", 2 * TABN + 8, I32, 1)
        idx = sb("idx", 4, I32)
        idxf = sb("idxf", 2)
        pcol = sb("pcol", 3)
        bias = sb("bias", DEPTH * E)
        sink = sb("sink", 2 * DEPTH * HEADS)
        mx, nb = sb("mx", 4), sb("nb", 32)
        den, rden = sb("den", 16), sb("rden", 16)

        XT = XA[:].rearrange("p (t d) -> p t d", t=NT)
        hT = HT[:].rearrange("p (k n) -> p k n", k=DK)
        cqT = C[:, 0:2304].rearrange("p (c n) -> p c n", c=3)
        ckvT = C[:, 2304:3840].rearrange("p (c n) -> p c n", c=2)
        tmpr = C[:, 3840:4608]
        sq = XA[:, 0:3840].rearrange("p (c n) -> p c n", c=5)
        qr = XA[:, 3840:5376].rearrange("p (c n) -> p c n", c=2)
        kr = XA[0:32, 5376:6144]
        rb = K[:, 0:1536].rearrange("p (c n) -> p c n", c=2)
        QT = Q[:].rearrange("p (h n) -> p h n", h=HEADS)
        KT = K[:].rearrange("p (h n) -> p h n", h=HEADS)
        V = VY[:, 0:3072].rearrange("p (t n) -> p t n", t=NT)
        Ym = VY[:, 3072:6144].rearrange("p (c n) -> p c n", c=4)
        cs_m = VY[:, 3072:4096].rearrange("p (a n) -> p a n", a=2)
        cs_s = VY[:, 0:1024].rearrange("p (a n) -> p a n", a=2)
        Ys = XA[:, 0:3072].rearrange("p (c n) -> p c n", c=4)
        Yp = XA[:, 3072:6144].rearrange("p (c n) -> p c n", c=4)
        Y = {"m": Ym, "s": Ys}
        Pb = C[:, 0:1536].rearrange("p (a n) -> p a n", a=2)
        PTb = C[:, 1536:3072].rearrange("p (a n) -> p a n", a=2)
        ytok = C[:, 3072:4096].rearrange("p (a n) -> p a n", a=2)
        QS = Q[:, 0:3072].rearrange("p (c n) -> p c n", c=4)
        KK = Q[:, 3072:4608].rearrange("p (c n) -> p c n", c=2)
        VS = Q[:, 4608:5376].rearrange("p (t n) -> p t n", t=NT)
        KS = Q[:, 5376:6144]
        U = K[:, 0:4 * UW].rearrange("p (c n) -> p c n", c=4)
        UT = K[:, 4 * UW:6 * UW].rearrange("p (c n) -> p c n", c=2)
        MG = K[:].rearrange("p (k n) -> p k n", k=DK)
        SG = C[:, 0:1536].rearrange("p (a n) -> p a n", a=2)
        mtmp = C[:, 1536:3072].rearrange("p (a n) -> p a n", a=2)
        BC = {("A2", 0): Q[:, 0:1024], ("A2", 1): Q[:, 1024:2048], ("B2", 0): Q[:, 2048:3072],
              ("B2", 1): Q[:, 3072:4096], ("gt1", 0): Q[:, 4096:5120], ("gt1", 1): Q[:, 5120:6144]}
        BC["gt2", 0], BC["gt2", 1] = BC["gt1", 0], BC["gt1", 1]
        fb = C[:, 0:2048].rearrange("p (a n) -> p a n", a=2)
        junk = C[:, 2048:3072]
        otmp = C[:, 3072:4096]
        Wt = rt[:, 4 * E:6 * E].rearrange("p (a n) -> p a n", a=2)
        tabf = rt[0:1, 0:2 * TABN + 8]
        xg = C[:, 0:2 * HROW].rearrange("p (a n) -> p a n", a=2)
        s1 = C[:, 2176:2688].rearrange("p (a n) -> p a n", a=2)
        hb = C[:, 2688:3200].rearrange("p (a n) -> p a n", a=2)
        hTb = C[:, 3200:3712].rearrange("p (a n) -> p a n", a=2)
        oh = C[:, 3712:4480].bitcast(BF16).rearrange("p (a t s) -> p a t s", a=2, t=NT)
        xgT = Q[:, 0:2048].rearrange("p (a k s) -> p a k s", a=2, k=DK)
        yb = Q[:, 2048:4096].rearrange("p (a n) -> p a n", a=2)
        WSL = [K, VY]
        wgu = [w[:, 0:4096].rearrange("p (g k n) -> p g k n", g=2, k=DK) for w in WSL]
        wdn = [w[:, 4096:6144].rearrange("p (c n) -> p c n", c=2) for w in WSL]
        comb = [VY[:, 0:2048].rearrange("p (a n) -> p a n", a=2), VY[:, 2048:4096].rearrange("p (a n) -> p a n", a=2)]

        PS = stack.enter_context(nc.psum_tensor("ps", [P, 4096], F32))
        slot = [PS[:, 1024 * i:1024 * i + 1024] for i in range(3)]
        OB = [PS[:, 3072:3584], PS[:, 3584:4096]]
        m_gu = [PS[:, 0:512], PS[:, 512:1024]]
        m_tr, m_y = PS[:, 1024:2048], PS[:, 2048:3072]
        m_h, m_i = PS[:, 3072:3328], PS[:, 3584:3587]

        s_con, s_vec, s_mask = sem("s_con"), sem("s_vec"), sem("s_mask")
        s_panel = [sem(f"s_panel{i}") for i in range(RING)]
        filled = sem("filled")
        drained = {"act": sem("drained_act"), "dve": sem("drained_dve")}
        s_x, s_xs, s_xr = sem("s_x"), sem("s_xs"), sem("s_xr")
        s_csm, s_css = sem("s_csm"), sem("s_css")
        ssq_ready, var_ready, rstd_ready, xn_ready = sem("ssq_ready"), sem("var_ready"), sem("rstd_ready"), sem("xn_ready")
        rms_rec, rms_sqrt, cn_ready = sem("rms_rec"), sem("rms_sqrt"), sem("cn_ready")
        roped, rope_copied = sem("roped"), sem("rope_copied")
        max_ready, exp_ready, o_full, o_drained = sem("max_ready"), sem("exp_ready"), sem("o_full"), sem("o_drained")
        sink_sum, sink_exp = sem("sink_sum"), sem("sink_exp")
        kk_ready, u_zero, pooled = sem("kk_ready"), sem("u_zero"), sem("pooled")
        x_new, f_ready, s_h = sem("x_new"), sem("f_ready"), [sem("s_h0"), sem("s_h1")]
        w_ready, s_w = sem("w_ready"), [sem("s_w0"), sem("s_w1")]
        sh_silu, sh_ready, s_sh = sem("sh_silu"), sem("sh_ready"), [sem("s_sh0"), sem("s_sh1")]
        setup_dve, s_zero, tab_ready = sem("setup_dve"), sem("s_zero"), sem("tab_ready")
        s_turns = sem("s_turns")
        s_row, s_hz, s_acc1, sink_neg = sem("s_row"), sem("s_hz"), sem("s_acc1"), sem("sink_neg")
        s_comb, combined, s_out = [sem("s_comb0"), sem("s_comb1")], sem("combined"), sem("s_out")
        s_gfin, fin_ready = sem("s_gfin"), sem("fin_ready")
        loops_done, layer_done = sem("loops_done"), sem("layer_done")
        L = [{n: sem(f"{n}_{l}") for n in ("wgu0", "wgu1", "wdn0", "wdn1", "gu_done", "tr_done", "hT_done", "idx_done",
                                             "dn_done", "silu_done", "h_ready", "xgT_a", "xgT_b", "hT_ev", "idx_ready",
                                             "oh_ready", "y_a", "y_b", "gat0", "gat1", "scat0", "scat1", "idx_copied", "idx_low")}
             for l in range(DEPTH)]
        chain = {e: [sem(f"chain_{e}"), 0] for e in ("act", "dve", "pool")}

        def step(e, eng, ins):
            chain[e][1] += 1
            ins.then_inc(chain[e][0], 1)
            eng.wait_ge(chain[e][0], chain[e][1])

        def after(eng, *name):
            j = names[name]
            eng.wait_ge(drained[j.drain], j.count)

        def full(l, kind):
            return l < DEPTH - 1 or kind in ("ckv", "kr", "ks")

        def pview(ps, everything, rows=P):
            return ps[0:rows, :].rearrange("p (b n) -> p b n", b=2)[:, :, 0:TOK // 2] if everything else ps[0:rows, 0:SEQ]

        def sview(buf, everything):
            return buf.rearrange("p (b n) -> p b n", b=2) if everything else buf[:, CTX:TOK]

        def attn(l, br, i):
            t, h = active(l)[i // HEADS], i % HEADS
            if br == "m":
                return t, h, 0, [(0, 0, 512), (512, 512, 256)] if t >= CT else [(0, 0, CTX)]
            if t < CT:
                return t, h, 512, [(512, 0, CTX)]
            a, b = max(CT, t - 1), min(NT - 1, t + 1)
            n = (b - a + 1) * P
            return t, h, 512 - n, [(512 - n, a * P, n), (512, 0, CTX)]

        def key_tiles(l, br, i):
            return [k // P + j for _, k, n in attn(l, br, i)[3] for j in range(n // P)]

        def exp_no(l, i):
            return (HEADS * NT if l else 0) + i + 1

        def tile_no(l, br, t):
            return (2 * NT if l else 0) + (len(active(l)) if br == "s" else 0) + active(l).index(t)

        def column(l, which, s, k):
            if which in ("A1", "A2"):
                at = l * 32 + (16 if which == "A2" else 0) + 2 * k + s
                return AB[:, at:at + 1]
            at = l * 96 + 2 * (8 * {"sh1": 0, "gt1": 2, "B2": 3, "gt2": 5}[which] + k) + s
            return modT[:, at:at + 1]

        def norm_no(l, i):
            return [0, 1 + NT, 2 + NT + len(active(1))][l] + i + 1

        def roped_no(l, what):
            return 8 * l + {"k": 1, 0: 2, 1: 3, "s": 8}[what]

        def max_no(l, br, i):
            return (2 * HEADS * NT if l else 0) + (HEADS * len(active(l)) if br == "s" else 0) + i + 1

        def sink_no(l, t):
            return (NT if l else 0) + active(l).index(t) + 1

        def gate_no(n2, b, cc):
            return 6 * n2 + 2 * b + cc

        def gate_args(i):
            return i // 6, i % 6 // 2, i % 2

        def store_no(l, n):
            return 16 * ((NT // 2 if l else 0) + n // 2 + 1)

        block = stack.enter_context(nc.Block())

        def loop_end(eng):
            eng.drain().then_inc(loops_done, 1)

        @block.sync
        def _(sp):
            sp.dma_start(con[:], consts).then_inc(s_con, 16)
            sp.dma_start(K[:, 0:MASK + MASK2], mask).then_inc(s_mask, 16)
            sp.dma_start(vecs[0:8, :], c.rearrange("a (k p) -> (a k) p", p=P)).then_inc(s_vec, 16)
            sp.dma_start(vecs[8:16, :], c_ctx.rearrange("(k p) -> k p", p=P)).then_inc(s_vec, 16)
            for l in range(DEPTH):
                sp.wait_ge(filled, l + 1)
                at = 0
                for v in (b_mod, g_mix, g_ffn, pool_scale, g_mla_q, g_mla_kv):
                    rows = v.shape[1] // P
                    sp.dma_start(vecs[at:at + rows, :], v[l].rearrange("(k p) -> k p", p=P)).then_inc(s_vec, 16)
                    at += rows
                assert at == NVEC

            def kpn(w, a, b):
                return w[:, a:b].rearrange("(k p) n -> p k n", p=P)

            def panel_parts(key):
                kind, l = key[0], key[1]
                if kind == "mod":
                    return [(0, DK, kpn(w_mod[l], 512 * key[2], 512 * key[2] + 512))]
                if kind == "cq":
                    return [(0, DK, kpn(w_in[l], OFF_CQ, OFF_CKV))]
                if kind == "ckv":
                    return [(0, DK, kpn(w_in[l], OFF_CKV, OFF_U))]
                if kind == "qs":
                    return [(0, DK, kpn(w_in[l], OFF_QS, OFF_KS))]
                if kind == "ks":
                    return [(0, DK, kpn(w_in[l], OFF_KS, OFF_G))]
                if kind == "u":
                    return [(0, DK, kpn(w_in[l], OFF_U, OFF_QS))]
                if kind == "uq":
                    v = w_mla_uq[l].rearrange("(k p) (h n) -> k p h n", p=P, h=HEADS)
                    return [(512 * k, HEADS, v[k, :, :, 0:NOPE]) for k in range(3)] + \
                        [(1536 + 256 * k, HEADS, v[k, :, :, NOPE:NOPE + ROPE]) for k in range(3)]
                if kind == "ukv":
                    v = w_mla_ukv[l].rearrange("(k p) (h n) -> k p h n", p=P, h=HEADS)
                    return [(1024 * i + 512 * k, HEADS, v[k, :, :, 64 * i:64 * i + 64]) for i in range(2) for k in range(2)]
                if kind == "pm":
                    return [(0, 4, w_pool[l].rearrange("g c d -> c g d"))]
                if kind == "merge":
                    n, b = key[2], key[3]
                    g0 = OFF_G + b * D + 256 * n
                    br = (w_br_mla, w_br_pool, w_br_swa)[b]
                    return [(0, DK, kpn(w_in[l], g0, g0 + 256)), (2048, 4, kpn(br[l], 256 * n, 256 * n + 256))]
                if kind == "wo":
                    return [(0, DK, kpn(w_out[l], 512 * key[2], 512 * key[2] + 512))]
                if kind == "router":
                    return [(0, DK, kpn(w_router[l], 0, E))]
                if kind == "shgu":
                    return [(0, DK, kpn(w_sh_gate[l], 0, DE)), (2048, DK, kpn(w_sh_up[l], 0, DE))]
                return [(0, 2, kpn(w_sh_down[l], 0, D))]

            def load_panel(n):
                key, _ = panels[n]
                if n >= RING:
                    sp.wait_ge(filled, panels[n - RING][1].fill)
                for at, ks, src in panel_parts(key):
                    w = src.shape[2]
                    dst = ring[:, SLOT * (n % RING) + at:SLOT * (n % RING) + at + ks * w]
                    sp.dma_start(dst.rearrange("p (k n) -> p k n", k=ks), src).then_inc(s_panel[n % RING], 16)

            done = [0]

            def load_until(key):
                while done[0] <= panel_no[key]:
                    load_panel(done[0])
                    done[0] += 1

            load_until(("mod", DEPTH - 1, 8))
            for l in range(DEPTH):
                A = active(l)
                if l == 0:
                    sp.dma_start(XT[:, 0:CT, :], ctx[0].rearrange("(t p) d -> p t d", p=P)).then_inc(s_x, 16)
                    sp.dma_start(XT[:, CT:NT, :], x[0].rearrange("(t p) d -> p t d", p=P)).then_inc(s_x, 16)
                sp.dma_start(cs_m, rope_mla).then_inc(s_csm, 16)
                load_until(("ukv", l))
                sp.wait_ge(filled, names["yT", l, "m", NT - 1].fill)
                sp.dma_start(cs_s, rope_swa).then_inc(s_css, 16)
                load_until(("wo", l, 1))
                sp.wait_ge(filled, names["b", l, 3, 2, 1].fill)
                if l == 0:
                    sp.dma_start(XT[:, 0:CT, :], ctx[0].rearrange("(t p) d -> p t d", p=P)).then_inc(s_xr, 16)
                    sp.dma_start(XT[:, CT:NT, :], x[0].rearrange("(t p) d -> p t d", p=P)).then_inc(s_xr, 16)
                else:
                    sp.dma_start(XT[:, CT:NT, :], XS[CTX:TOK, :].rearrange("(t p) d -> p t d", p=P)).then_inc(s_xr, 16)
                load_until(("shd", l))
                sl = L[l]
                sp.wait_ge(filled, names["o", l, A[-1]].fill)
                sp.wait_ge(tab_ready, l + 1)
                n_blocks = sp.value_load(tab[0:1, 2 * TABN:2 * TABN + 1], min_val=1, max_val=max_blocks(l))

                def load_gate_up(n, s):
                    e = sp.value_load(tab[0:1, bass.ds(n, 1)], min_val=0, max_val=E - 1)
                    for g, w in enumerate((w_exp_gate, w_exp_up)):
                        sp.dma_start(wgu[s][:, g, :, :].rearrange("p k n -> p (k n)"),
                                     w[l][bass.ds(e, 1), :, :].rearrange("e (p k) n -> (e p) (k n)", p=P))\
                            .then_inc(sl[f"wgu{s}"], 16)
                    return e

                def load_down(e, s):
                    sp.dma_start(wdn[s].rearrange("p c n -> p (c n)"),
                                 w_exp_down[l][bass.ds(e, 1), :, :].rearrange("e (p c) n -> (e p) (c n)", p=P))\
                        .then_inc(sl[f"wdn{s}"], 16)

                for n in range(2):
                    load_down(load_gate_up(n, n), n)
                with sp.Fori(0, max_blocks(l) // UNROLL) as m:
                    for r in range(UNROLL):
                        n = UNROLL * m + r
                        with sp.If(n + 2 < n_blocks):
                            sp.wait_ge(sl["gu_done"], n + 1)
                            e = load_gate_up(n + 2, r % 2)
                            sp.wait_ge(sl["dn_done"], n + 1)
                            load_down(e, r % 2)
                loop_end(sp)
                sp.wait_ge(loops_done, 5 * (l + 1))
                if l == DEPTH - 1:
                    sp.dma_start(BC["A2", 0], g_final.partition_broadcast(P)).then_inc(s_gfin, 16)
                for i, t in enumerate(A):
                    g = i + (len(active(0)) if l else 0)
                    if i >= 2:
                        sp.wait_ge(combined, g - 1)
                    for a in range(2):
                        sp.dma_start(comb[i % 2][:, a, :], ACC[a][t * P:t * P + P, :]).then_inc(s_comb[i % 2], 16)
                if l < DEPTH - 1:
                    for i, t in enumerate(A):
                        sp.wait_ge(combined, i + 1)
                        sp.dma_start(XS[t * P:t * P + P, :], XT[:, t, :]).then_inc(s_xs, 16)
                else:
                    for i, t in enumerate(A):
                        sp.wait_ge(fin_ready, i + 1)
                        sp.dma_start(out[0, (t - CT) * P:(t - CT + 1) * P, :], XT[:, t, :]).then_inc(s_out, 16)
                    sp.wait_ge(s_out, 16 * len(A))

        @block.tensor
        def _(pe):
            mm = nc.tensor.matmul

            def panel(key):
                n = panel_no[key]
                per = {"merge": 2, "shgu": 2, "uq": 6, "ukv": 4}
                loads = sum(16 * per.get(panels[i][0][0], 1) for i in range(n % RING, n + 1, RING))
                pe.wait_ge(s_panel[n % RING], loads)
                return ring[:, SLOT * (n % RING):SLOT * (n % RING + 1)]

            def chunks(buf, k, w):
                return buf[:, 0:k * w].rearrange("p (k n) -> p k n", k=k)

            def project(ps, weight, src, everything, rows=P):
                pieces = [(0, 0, TOK // 2), (512, TOK // 2, TOK // 2)] if everything else [(0, CTX, SEQ)]
                for at, tok, n in pieces:
                    for k in range(len(weight)):
                        last = mm(ps[0:rows, at:at + n], weight[k], src[k][:, tok:tok + n],
                                  start=k == 0, stop=k == len(weight) - 1)
                return last

            def turn(ps, tiles):
                for at, t in tiles:
                    last = nc.tensor.transpose(ps[0:t.shape[1], at:at + t.shape[0]], t, ident[0:t.shape[0], 0:t.shape[0]])
                return last

            tiles_done = [0]

            def moe(l):
                sl = L[l]
                pe.wait_ge(tab_ready, l + 1)
                n_blocks = pe.value_load(tab[0:1, 2 * TABN:2 * TABN + 1], min_val=1, max_val=max_blocks(l))
                A = active(l)

                def slots_of(n, count):
                    pe.wait_ge(sl["oh_ready"], count)
                    for i, t in enumerate(A):
                        last = mm(m_i, oh[:, n % 2, t, :], tokb[:, 3 * t:3 * t + 3], start=i == 0, stop=i == len(A) - 1)
                    last.then_inc(sl["idx_done"], 1)

                def turn_tokens(s, gathered):
                    pe.wait_ge(sl[f"gat{s}"], gathered)
                    v = xg[:, s, 0:D].rearrange("s (p k) -> s k p", k=DK)
                    turn(m_tr, [(k * P, v[:, k, :]) for k in range(DK)]).then_inc(sl["tr_done"], 1)

                slots_of(0, 1)
                pe.wait_ge(sl["idx_ready"], 1)
                slots_of(1, 2)
                turn_tokens(0, 16)
                with pe.Fori(0, max_blocks(l) // UNROLL) as m:
                    for r in range(UNROLL):
                        n, s = UNROLL * m + r, r % 2
                        with pe.If(n < n_blocks):
                            turns = (UNROLL // 2) * m + r // 2 + 1
                            pe.wait_ge(sl[f"wgu{s}"], 32 * turns)
                            pe.wait_ge(sl["xgT_a"], n + 1)
                            pe.wait_ge(sl["xgT_b"], n + 1)
                            for k in range(DK):
                                last = mm(m_gu[s], xgT[:, s, k, :], wgu[s][:, :, k, :], start=k == 0, stop=k == DK - 1)
                            last.then_inc(sl["gu_done"], 1)
                            turn_tokens(1 - s, 16 * ((UNROLL // 2) * m + (r + 1) // 2 + 1))
                            pe.wait_ge(sl["h_ready"], n + 1)
                            hv = hb[:, s, :].rearrange("s (p c) -> s c p", c=2)
                            turn(m_h, [(cc * P, hv[:, cc, :]) for cc in range(2)]).then_inc(sl["hT_done"], 1)
                            pe.wait_ge(sl["idx_ready"], n + 2)
                            slots_of(r, n + 3)
                            pe.wait_ge(sl[f"wdn{s}"], 16 * turns)
                            pe.wait_ge(sl["hT_ev"], n + 1)
                            pe.wait_ge(sl["y_a"], n + 1)
                            pe.wait_ge(sl["y_b"], n + 1)
                            for half in range(2):
                                for cc in range(2):
                                    last = mm(m_y[:, 512 * half:512 * half + 512], hTb[:, s, cc * P:cc * P + P],
                                              wdn[s][:, cc, 512 * half:512 * half + 512], start=cc == 0, stop=cc == 1)
                            last.then_inc(sl["dn_done"], 1)

            pe.wait_ge(s_con, 16)
            fills = []
            for job in jobs:
                kind, a = job.kind, job.args
                if job.drain:
                    ps = slot[job.slot]
                    if len(fills) >= 3:
                        pe.wait_ge(drained[fills[-3].drain], fills[-3].count)
                    fills.append(job)
                if kind == "cvec":
                    pe.wait_ge(s_vec, 32)
                    last = turn(ps, [(0, vecs[0:16, :])])
                elif kind == "vec":
                    pe.wait_ge(s_vec, 32 + 96 * (a[0] + 1))
                    last = turn(ps, [(0, vecs[0:NVEC, :])])
                elif kind == "mod":
                    w = chunks(panel(("mod",) + a), DK, 512)
                    after(pe, "cvec")
                    for j in range(4):
                        for k in range(DK):
                            last = mm(ps[:, 2 * j:2 * j + 2], w[:, k, j * P:j * P + P], cT[:, k::8],
                                      start=k == 0, stop=k == DK - 1)
                elif kind == "h":
                    l, k = a
                    pe.wait_ge(xn_ready, NT * (l + 1))
                    tiles = [((t - CT) * P, t) for t in range(CT, NT)] + [(SEQ + t * P, t) for t in range(CT)]
                    last = turn(ps, [(at, XT[:, t, k * P:k * P + P]) for at, t in tiles])
                elif kind in ("cq", "ckv", "kr", "qs", "ks"):
                    l = a[0]
                    col, width, key = {"cq": (0, 384, "cq"), "ckv": (0, 288, "ckv"), "kr": (256, 288, "ckv"),
                                       "qs": (0, 512, "qs"), "ks": (0, 256, "ks")}[kind]
                    col += P * a[1] if len(a) > 1 else 0
                    w = chunks(panel((key, l)), DK, width)
                    rows = ROPE if kind == "kr" else P
                    after(pe, "h", l, DK - 2)
                    after(pe, "h", l, DK - 1)
                    last = project(ps, [w[:, k, col:col + rows] for k in range(DK)], [hT[:, k, :] for k in range(DK)],
                                   full(l, kind), rows)
                elif kind in ("rq", "rk"):
                    l = a[0]
                    cs = (0, 1, 2) if kind == "rq" else (3, 4)
                    after(pe, "ckv", l, 1)
                    last = project(ps, [cst("ones") for _ in cs], [sq[:, i, :] for i in cs], full(l, kind) or kind == "rk")
                elif kind == "krp":
                    after(pe, "kr", a[0])
                    last = mm(ps[0:32, 0:SEQ], cst("perm8")[0:32, 0:32], kr[:, CTX:TOK], start=True, stop=True)
                elif kind in ("qr", "qn"):
                    l, j = a
                    pe.wait_ge(cn_ready, 2 * l + 1)
                    w = panel(("uq", l))
                    at, per = (P * j, 512) if kind == "qn" else (1536 + P * j, 256)
                    ws = [w[:, at + per * k:at + per * k + P] for k in range(3)]
                    last = project(ps, ws, [cqT[:, k, :] for k in range(3)], full(l, kind))
                elif kind == "qrp":
                    l, j = a
                    after(pe, "qr", l, j)
                    last = mm(ps[:, 0:SEQ], cst("perm8"), qr[:, j, CTX:TOK], start=True, stop=True)
                elif kind == "kn":
                    l, j = a
                    pe.wait_ge(cn_ready, 2 * l + 2)
                    w = panel(("ukv", l))
                    ws = [w[:, 512 * k + P * j:512 * k + P * j + P] for k in range(2)]
                    last = project(ps, ws, [ckvT[:, k, :] for k in range(2)], True)
                elif kind == "v":
                    l, t = a
                    w = panel(("ukv", l))
                    for k in range(2):
                        last = mm(ps[:, 0:512], ckvT[:, k, t * P:t * P + P], w[:, 1024 + 512 * k:1536 + 512 * k],
                                  start=k == 0, stop=k == 1)
                elif kind == "S":
                    l, br, i = a
                    t, h, _, parts = attn(l, br, i)
                    if i == 0:
                        if br == "m":
                            pe.wait_ge(rope_copied, 3 * (l + 1))
                            for j in range(4):
                                after(pe, "kn", l, j)
                            after(pe, "v", l, NT - 1)
                            after(pe, "v", l, NT - 2)
                        else:
                            pe.wait_ge(kk_ready, l + 1)
                            after(pe, "vs", l)
                    if br == "m":
                        q = QT[0:96, h, t * P:t * P + P]
                    else:
                        q = QS[64 * (h % 2):64 * (h % 2) + 64, h // 2, t * P:t * P + P]
                    for at, key, n in parts:
                        k = KT[0:96, h, key:key + n] if br == "m" else KK[64 * (h % 2):64 * (h % 2) + 64, h // 4, key:key + n]
                        last = mm(ps[:, at:at + n], q, k, start=True, stop=True)
                elif kind == "T":
                    l, br, i = a
                    if br == "m":
                        after(pe, "S", l, br, i)
                    else:
                        pe.wait_ge(exp_ready, exp_no(l, i))
                    n = len(key_tiles(l, br, i))
                    last = turn(ps, [(j * P, Pb[:, i % 2, j * P:j * P + P]) for j in range(n)])
                elif kind == "PV":
                    l, br, i = a
                    t, h = attn(l, br, i)[:2]
                    g = tiles_done[0]
                    after(pe, "T", l, br, i)
                    if h == 0 and g >= 2:
                        pe.wait_ge(o_drained, g - 1)
                    ks = key_tiles(l, br, i)
                    for j, kt in enumerate(ks):
                        v = V[:, kt, VD * h:VD * h + VD] if br == "m" else VS[:, kt, HD * (h // 4):HD * (h // 4) + HD]
                        last = mm(OB[g % 2][:, VD * h:VD * h + VD], PTb[:, i % 2, j * P:j * P + P], v,
                                  start=j == 0, stop=j == len(ks) - 1)
                    if h == HEADS - 1:
                        last.then_inc(o_full, 1)
                        tiles_done[0] += 1
                elif kind == "yT":
                    l, br, t = a
                    g = tile_no(l, br, t)
                    pe.wait_ge(o_drained, g + 1)
                    last = turn(ps, [(j * P, ytok[:, g % 2, j * P:j * P + P]) for j in range(4)])
                elif kind in ("qsp", "ksp"):
                    l = a[0]
                    after(pe, kind[:2], *a)
                    src = QS[:, a[1], :] if kind == "qsp" else KS
                    last = mm(ps[:, 0:SEQ], cst("perm16"), src[:, CTX:TOK], start=True, stop=True)
                elif kind == "vs":
                    w = chunks(panel(("ks", a[0])), DK, 256)
                    for t in range(NT):
                        for k in range(DK):
                            last = mm(ps[:, t * P:t * P + P], hT[:, k, t * P:t * P + P], w[:, k, SWKV:2 * SWKV],
                                      start=k == 0, stop=k == DK - 1)
                elif kind in ("u", "pm"):
                    l, j = a
                    if kind == "u":
                        w = chunks(panel(("u", l)), DK, 512)
                        ws, xs = [w[:, k, j * P:j * P + P] for k in range(DK)], [hT[:, k, :] for k in range(DK)]
                        at = {0: CTX, 512: 0}
                    else:
                        pe.wait_ge(pooled, 4 * l + j + 1)
                        ws, xs = [chunks(panel(("pm", l)), 4, P)[:, j, :]], [U[:, j, :]]
                        at = {0: UL, 512: UC}
                    for col, n in ((0, SEQ), (512, CTX))[:2 if l < DEPTH - 1 else 1]:
                        for k in range(len(ws)):
                            last = mm(ps[:, col:col + n], ws[k], xs[k][:, at[col]:at[col] + n],
                                      start=k == 0, stop=k == len(ws) - 1)
                elif kind in ("g", "b"):
                    l, n2, b, cc = a
                    buf = panel(("merge", l, n2, b))
                    if kind == "g":
                        w = chunks(buf, DK, 256)
                        ws, xs = [w[:, k, cc * P:cc * P + P] for k in range(DK)], [hT[:, k, :] for k in range(DK)]
                    else:
                        w = chunks(buf[:, 2048:3072], 4, 256)
                        src = (Ym, Yp, Ys)[b]
                        if n2 == 0 and cc == 0:
                            if b == 1:
                                after(pe, "pm", l, 3)
                            else:
                                after(pe, "yT", l, "ms"[b // 2], NT - 1)
                        ws, xs = [w[:, k, cc * P:cc * P + P] for k in range(4)], [src[:, k, :] for k in range(4)]
                    last = project(ps, ws, xs, full(l, kind))
                elif kind == "bc":
                    l, which, s = a
                    for k in range(DK):
                        last = mm(ps[:, k * P:k * P + P], column(l, which, s, k).broadcast_to([P, P]), ident,
                                  start=True, stop=True)
                elif kind == "o":
                    l, t = a
                    for half in range(2):
                        w = chunks(panel(("wo", l, half)), DK, 512)
                        if t == active(l)[0]:
                            after(pe, "b", l, 3, 2, 1)
                        for k in range(DK):
                            last = mm(ps[:, 512 * half:512 * half + 512], MG[:, k, t * P:t * P + P], w[:, k, :],
                                      start=k == 0, stop=k == DK - 1)
                elif kind == "f":
                    l, t = a
                    n = active(l).index(t)
                    pe.wait_ge(f_ready, n + 1 + (NT if l else 0))
                    last = turn(ps, [(k * P, fb[:, n % 2, k * P:k * P + P]) for k in range(DK)])
                elif kind == "r":
                    l, t = a
                    w = chunks(panel(("router", l)), DK, E)
                    after(pe, "f", l, t)
                    for k in range(DK):
                        last = mm(ps[:, 0:E], hT[:, k, t * P:t * P + P], w[:, k, :], start=k == 0, stop=k == DK - 1)
                elif kind == "sg":
                    l, t = a
                    w = panel(("shgu", l)).rearrange("p (g k n) -> p g k n", g=2, k=DK)
                    for k in range(DK):
                        last = mm(ps[:, 0:512], hT[:, k, t * P:t * P + P], w[:, :, k, :], start=k == 0, stop=k == DK - 1)
                elif kind == "sT":
                    l, t = a
                    after(pe, "sg", l, t)
                    n = active(l).index(t)
                    last = turn(ps, [(cc * P, hb[:, n % 2, cc * P:cc * P + P]) for cc in range(2)])
                elif kind == "sd":
                    l, t = a
                    w = chunks(panel(("shd", l)), 2, D)
                    n = active(l).index(t)
                    after(pe, "sT", l, t)
                    for half in range(2):
                        for cc in range(2):
                            last = mm(ps[:, 512 * half:512 * half + 512], hTb[:, n % 2, cc * P:cc * P + P],
                                      w[:, cc, 512 * half:512 * half + 512], start=cc == 0, stop=cc == 1)
                elif kind == "pos":
                    l, t = a
                    A = active(l)
                    pe.wait_ge(w_ready, A.index(t) + 1 + (NT if l else 0))
                    for u in [v for v in A if v <= t]:
                        last = mm(ps[:, 0:E], (trib if u == t else onesb)[:], Mb[:, u * E:u * E + E], start=u == A[0], stop=u == t)
                elif kind == "cnt":
                    A = active(a[0])
                    for u in A:
                        last = mm(ps[0:E, 0:1], Mb[:, u * E:u * E + E], onesb[:, 0:1], start=u == A[0], stop=u == A[-1])
                elif kind == "end":
                    after(pe, "cnt", a[0])
                    last = mm(ps[0:E, 0:1], trib[0:E, 0:E], nbb[0:E, 0:1], start=True, stop=True)
                elif kind == "tab":
                    after(pe, "end", a[0])
                    mm(ps[0:1, 0:TABN], onesb[0:E, 0:1], Gb[0:E, :], start=True, stop=True)
                    mm(ps[0:1, 128:128 + TABN], nbb[0:E, 0:1], Gb[0:E, :], start=True, stop=True)
                    last = mm(ps[0:1, 256:257], nbb[0:E, 0:1], onesb[0:E, 0:1], start=True, stop=True)
                elif kind == "moe":
                    moe(a[0])
                    loop_end(pe)
                if job.drain:
                    last.then_inc(filled, 1)

        @block.scalar
        def _(act):
            A_ = nc.scalar.activation

            def copy(o, i):
                return A_(o, i, ACT.Copy)

            def moe(l):
                sl = L[l]
                act.wait_ge(tab_ready, l + 1)
                n_blocks = act.value_load(tab[0:1, 2 * TABN:2 * TABN + 1], min_val=1, max_val=max_blocks(l))

                def tokens(s, count):
                    act.wait_ge(sl["tr_done"], count)
                    copy(xgT[:, s, 0:4, :], m_tr[:, 0:512].rearrange("p (k s) -> p k s", k=4)).then_inc(sl["xgT_a"], 1)

                tokens(0, 1)
                act.sem_inc(sl["y_a"], 1)
                with act.Fori(0, max_blocks(l) // UNROLL) as m:
                    for r in range(UNROLL):
                        n, s = UNROLL * m + r, r % 2
                        with act.If(n < n_blocks):
                            act.wait_ge(sl["gu_done"], n + 1)
                            A_(s1[:, s, :], m_gu[s][:, 0:DE], ACT.Silu).then_inc(sl["silu_done"], 1)
                            tokens(1 - s, n + 2)
                            act.wait_ge(sl["dn_done"], n + 1)
                            act.wait_ge(sl[f"scat{s}"], 16 * ((UNROLL // 2) * m + r // 2 + 1))
                            copy(yb[:, s, 0:512], m_y[:, 0:512]).then_inc(sl["y_a"], 1)

            for job in jobs:
                kind, a, ps = job.kind, job.args, slot[job.slot] if job.drain else None
                mine = job.drain == "act"
                l = a[0] if a else 0
                last = None
                if kind == "h" and a[1] == 0:
                    if l == 0:
                        act.wait_ge(s_x, 32)
                    else:
                        act.wait_ge(combined, NT)
                    for t in range(NT):
                        ins = A_(HT[:, t * D:t * D + D], XT[:, t, :], ACT.Square, accum_out=ssq[:, t:t + 1])
                    ins.then_inc(ssq_ready, 1)
                    act.wait_ge(var_ready, norm_no(l, 0))
                    A_(rstd[:, 0:NT], ssq[:, 0:NT], ACT.Sqrt).then_inc(rstd_ready, 1)
                if mine:
                    act.wait_ge(filled, job.fill)
                if kind == "cvec":
                    last = A_(cT[:], ps[:, 0:16], ACT.Silu)
                elif kind == "h" and mine:
                    k = a[1]
                    if k == 0:
                        act.wait_ge(setup_dve, DEPTH)
                    for at, tok, n, s in ((0, CTX, SEQ, 0), (512, 0, CTX, 1)):
                        last = A_(hT[:, k, tok:tok + n], ps[:, at:at + n], ACT.Identity,
                                  scale=column(l, "A1", s, k), bias=column(l, "sh1", s, k))
                elif kind in ("cq", "ckv"):
                    ev = full(l, kind)
                    i = a[1] + (3 if kind == "ckv" else 0)
                    dst = cqT[:, a[1], :] if kind == "cq" else ckvT[:, a[1], :]
                    copy(sview(dst, ev), pview(ps, ev))
                    last = A_(sview(sq[:, i, :], ev), pview(ps, ev), ACT.Square)
                elif kind == "kr":
                    last = copy(sview(kr, True), pview(ps, True, 32))
                elif kind in ("rq", "rk"):
                    i = int(kind == "rk")
                    act.wait_ge(rms_rec, 2 * l + i + 1)
                    v = sview(rb[:, i, :], full(l, kind) or i)
                    A_(v, v, ACT.Sqrt).then_inc(rms_sqrt, 1)
                elif kind == "krp":
                    act.wait_ge(roped, roped_no(l, "k"))
                    act.wait_ge(cn_ready, 2 * l + 2)
                    for h in range(HEADS):
                        ins = copy(KT[64:96, h, :], kr)
                    ins.then_inc(rope_copied, 1)
                elif kind == "qr":
                    ev = full(l, kind)
                    last = copy(sview(qr[:, a[1], :], ev), pview(ps, ev))
                elif kind == "qrp":
                    j = a[1]
                    act.wait_ge(roped, roped_no(l, j))
                    for h in range(4 * j, 4 * j + 4):
                        ins = copy(sview(QT[64:96, h, :], full(l, kind)),
                                   sview(qr[32 * (h % 4):32 * (h % 4) + 32, j, :], full(l, kind)))
                    ins.then_inc(rope_copied, 1)
                elif kind in ("qn", "kn") and mine:
                    T_, ev = (QT, full(l, kind)) if kind == "qn" else (KT, True)
                    for hh in range(2):
                        last = copy(sview(T_[0:64, 2 * a[1] + hh, :], ev), pview(ps[64 * hh:64 * hh + 64, :], ev, 64))
                elif kind == "v" and mine:
                    last = copy(V[:, a[1], :], ps[:, 0:512])
                elif kind == "S":
                    _, br, i = a
                    t, h, at, parts = attn(l, br, i)
                    w = sum(n for _, _, n in parts)
                    g = tile_no(l, br, t)
                    act.wait_ge(max_ready, max_no(l, br, i))
                    if br == "m":
                        last = A_(Pb[:, i % 2, 0:w], ps[:, 0:w], ACT.Exp, scale=MLA_SCALE, bias=nb[:, 8 * (g % 2) + h:8 * (g % 2) + h + 1],
                                  accum_out=den[:, 8 * (g % 2) + h:8 * (g % 2) + h + 1])
                    else:
                        A_(Pb[:, i % 2, 0:w], Pb[:, i % 2, 0:w], ACT.Exp, scale=SWA_SCALE, bias=nb[:, 8 * (g % 2) + h:8 * (g % 2) + h + 1],
                           accum_out=den[:, 8 * (g % 2) + h:8 * (g % 2) + h + 1]).then_inc(exp_ready, 1)
                        if h == HEADS - 1:
                            act.wait_ge(sink_sum, sink_no(l, t))
                            A_(nb[:, 16 + 8 * (g % 2):24 + 8 * (g % 2)], nb[:, 16 + 8 * (g % 2):24 + 8 * (g % 2)], ACT.Exp)\
                                .then_inc(sink_exp, 1)
                elif kind == "T" and mine:
                    n = P * len(key_tiles(l, a[1], a[2]))
                    last = copy(PTb[:, a[2] % 2, 0:n], ps[:, 0:n])
                elif kind == "yT":
                    t = a[2]
                    last = copy(Y[a[1]][:, :, t * P:t * P + P], ps[:, 0:512].rearrange("p (c n) -> p c n", c=4))
                elif kind == "qs":
                    last = copy(sview(QS[:, a[1], :], full(l, kind)), pview(ps, full(l, kind)))
                elif kind == "ks":
                    last = copy(sview(KS, True), pview(ps, True))
                elif kind == "ksp":
                    act.wait_ge(roped, roped_no(l, "s"))
                    for kv in range(2):
                        for half in range(2):
                            ins = copy(KK[64 * half:64 * half + 64, kv, :], KS[64 * kv:64 * kv + 64, :])
                    ins.then_inc(kk_ready, 1)
                elif kind == "vs":
                    last = copy(VS, ps[:, 0:TOK].rearrange("p (t n) -> p t n", t=NT))
                elif kind == "u":
                    if a[1] == 0:
                        act.wait_ge(u_zero, l + 1)
                    last = copy(U[:, a[1], UL:UL + SEQ], ps[:, 0:SEQ])
                    if l < DEPTH - 1:
                        last = copy(U[:, a[1], UC:UC + CTX], ps[:, 512:512 + CTX])
                elif kind == "g":
                    i = gate_no(*a[1:])
                    if i >= 2:
                        after(act, "b", l, *gate_args(i - 2))
                    ev = full(l, kind)
                    last = A_(sview(SG[:, i % 2, :], ev), pview(ps, ev), ACT.Sigmoid)
                elif kind == "bc":
                    if a[1] == "gt2":
                        after(act, "o", l, active(l)[-1])
                    last = copy(BC[a[1], a[2]], ps)
                elif kind == "o":
                    n = active(l).index(a[1])
                    after(act, "o", l, a[1])
                    A_(junk, XT[:, a[1], :], ACT.Square, accum_out=ssq[:, a[1]:a[1] + 1]).then_inc(ssq_ready, 1)
                    act.wait_ge(var_ready, norm_no(l, n + 1))
                    A_(rstd[:, a[1]:a[1] + 1], ssq[:, a[1]:a[1] + 1], ACT.Sqrt).then_inc(rstd_ready, 1)
                elif kind == "f":
                    last = copy(hT[:, :, a[1] * P:a[1] * P + P], ps.rearrange("p (k n) -> p k n", k=DK))
                elif kind == "r":
                    last = A_(scores[:, a[1] * E:a[1] * E + E], ps[:, 0:E], ACT.Sigmoid)
                elif kind == "sg":
                    n = active(l).index(a[1])
                    act.wait_ge(filled, job.fill)
                    A_(s1[:, n % 2, :], ps[:, 0:DE], ACT.Silu).then_inc(sh_silu, 1)
                elif kind == "sT":
                    n = active(l).index(a[1])
                    last = copy(hTb[:, n % 2, :], ps[:, 0:DE])
                elif kind == "sd":
                    n = active(l).index(a[1])
                    if n >= 2:
                        act.wait_ge(s_sh[n % 2], store_no(l, n) - 16)
                    last = copy(yb[:, n % 2, :], ps)
                elif kind == "moe":
                    moe(l)
                    loop_end(act)
                    if l == DEPTH - 1:
                        for i, t in enumerate(active(l)):
                            act.wait_ge(combined, NT + i + 1)
                            A_(junk, XT[:, t, :], ACT.Square, accum_out=ssq[:, t:t + 1]).then_inc(ssq_ready, 1)
                            act.wait_ge(var_ready, norm_no(l + 1, i))
                            A_(rstd[:, t:t + 1], ssq[:, t:t + 1], ACT.Sqrt).then_inc(rstd_ready, 1)
                if last is not None:
                    last.then_inc(drained["act"], 1)

        @block.vector
        def _(dve):
            vec = nc.vector
            tt, ts, stt = vec.tensor_tensor, vec.tensor_scalar, vec.scalar_tensor_tensor

            def link(ins):
                step("dve", dve, ins)

            def rotate(rows, ps, tables, n_rows=P):
                lat, tmp = rows[:, CTX:TOK], tmpr[0:n_rows, 0:SEQ]
                tt(tmp, ps[0:n_rows, 0:SEQ], tables[0:n_rows, 1, :], ALU.mult)
                ins = tt(lat, lat, tables[0:n_rows, 0, :], ALU.mult)
                link(ins)
                return tt(lat, lat, tmp, ALU.add)

            def inv_mean(out_, in_, n):
                link(ts(out_, in_, 1.0 / n, EPS, ALU.mult, ALU.add))
                return vec.reciprocal(out_, out_)

            def route(l, t):
                sc = scores[:, t * E:t * E + E]
                sel, t1, t2, t3 = (rt[:, i * E:i * E + E] for i in range(4))
                n = active(l).index(t)
                g8 = t1.rearrange("p (g j) -> p g j", g=GROUPS)
                gs, rank, pen, v8 = (rsm[:, 8 * i:8 * i + 8] for i in range(4))
                total, inv = rsm[:, 32:33], rsm[:, 33:34]
                after(dve, "r", l, t)
                link(tt(sel, sc, bias[:, l * E:l * E + E], ALU.add))
                for g in range(GROUPS):
                    ins = vec.max(g8[:, g, :], sel[:, 8 * g:8 * g + 8])
                link(ins)
                link(tt(gs, g8[:, :, 0], g8[:, :, 1], ALU.add))
                gj = gs.unsqueeze(1).broadcast_to([P, GROUPS, GROUPS])
                gi = gs.unsqueeze(2).broadcast_to([P, GROUPS, GROUPS])
                v2, v3 = (v.rearrange("p (g j) -> p g j", g=GROUPS) for v in (t2, t3))
                tt(v2, gj, gi, ALU.is_gt)
                link(tt(v3, gj, gi, ALU.is_equal))
                link(tt(t3, t3, cst("lower"), ALU.mult))
                link(tt(t2, t2, t3, ALU.add))
                link(vec.tensor_reduce(rank, v2, AX.X, ALU.add))
                link(ts(rank, rank, float(KEEP), None, ALU.is_lt))
                link(ts(pen, rank, -NEG, NEG, ALU.mult, ALU.add))
                vs_ = sel.rearrange("p (g j) -> p g j", g=GROUPS)
                link(tt(vs_, vs_, rank.unsqueeze(2).broadcast_to([P, GROUPS, 8]), ALU.mult))
                link(tt(vs_, vs_, pen.unsqueeze(2).broadcast_to([P, GROUPS, 8]), ALU.add))
                link(vec.max(v8, sel))
                link(vec.match_replace(t1, v8, sel, -3e38))
                link(tt(t2, t1, sel, ALU.not_equal))
                vec.tensor_copy(Mb[:, t * E:t * E + E], t2)
                link(tt(t3, sc, t2, ALU.mult))
                link(vec.tensor_reduce(total, t3, AX.X, ALU.add))
                link(vec.reciprocal(inv, total))
                if n >= 2:
                    dve.wait_ge(s_w[n % 2], store_no(l, n) - 16)
                ts(Wt[:, n % 2, :], t3, inv, ROUTED, ALU.mult, ALU.mult).then_inc(w_ready, 1)

            def moe(l):
                sl = L[l]
                A = active(l)
                a0 = A[0]
                n_blocks = dve.value_load(tab[0:1, 2 * TABN:2 * TABN + 1], min_val=1, max_val=max_blocks(l))

                def one_hot(n, s):
                    e = dve.value_load(tab[0:1, bass.ds(n, 1)], min_val=0, max_val=E - 1)
                    b = dve.value_load(tab[0:1, bass.ds(n + TABN, 1)], min_val=0, max_val=MAXB - 1)
                    a, _ = CONSTS["slot1"]
                    slots = con[:, bass.ds(a + b * P, P)].unsqueeze(1).broadcast_to([P, len(A), P])
                    rows = posm[:, a0 * E:NT * E].rearrange("p (t e) -> p t e", e=E)[:, :, bass.ds(e, 1)]
                    tt(oh[:, s, a0:NT, :], slots, rows.broadcast_to([P, len(A), P]), ALU.is_equal)\
                        .then_inc(sl["oh_ready"], 1)
                    return e

                def take_index(count, i4):
                    dve.wait_ge(sl["idx_done"], count)
                    vec.tensor_copy(pcol[:], m_i).then_inc(sl["idx_copied"], 1)
                    dve.wait_ge(sl["idx_copied"], count)
                    stt(idxf[:, 0:1], pcol[:, 2:3], cst("negdummy"), pcol[:, 0:1], ALU.mult, ALU.add)\
                        .then_inc(sl["idx_low"], 1)
                    dve.wait_ge(sl["idx_low"], count)
                    stt(idx[:, i4:i4 + 1], idxf[:, 0:1], cst("dummy"), pcol[:, 1:2], ALU.add, ALU.add)\
                        .then_inc(sl["idx_ready"], 1)

                def tokens(s, count):
                    dve.wait_ge(sl["tr_done"], count)
                    vec.tensor_copy(xgT[:, s, 4:8, :], m_tr[:, 512:1024].rearrange("p (k s) -> p k s", k=4))\
                        .then_inc(sl["xgT_b"], 1)

                dve.sem_inc(sl["y_b"], 1)
                one_hot(0, 0)
                one_hot(1, 1)
                take_index(1, 0)
                take_index(2, 1)
                one_hot(2, 0)
                tokens(0, 1)
                with dve.Fori(0, max_blocks(l) // UNROLL) as m:
                    for r in range(UNROLL):
                        n, s = UNROLL * m + r, r % 2
                        with dve.If(n < n_blocks):
                            e = dve.value_load(tab[0:1, bass.ds(n, 1)], min_val=0, max_val=E - 1)
                            dve.wait_ge(sl["silu_done"], n + 1)
                            stt(hb[:, s, :], s1[:, s, :], xg[:, s, bass.ds(e + D, 1)], m_gu[s][:, DE:2 * DE],
                                ALU.mult, ALU.mult).then_inc(sl["h_ready"], 1)
                            dve.wait_ge(sl["hT_done"], n + 1)
                            vec.tensor_copy(hTb[:, s, :], m_h).then_inc(sl["hT_ev"], 1)
                            tokens(1 - s, n + 2)
                            dve.wait_ge(sl[f"scat{s}"], 16 * ((UNROLL // 2) * m + r // 2 + 1))
                            take_index(n + 3, (r + 2) % 4)
                            one_hot(n + 3, 1 - s)
                            dve.wait_ge(sl["dn_done"], n + 1)
                            vec.tensor_copy(yb[:, s, 512:1024], m_y[:, 512:1024]).then_inc(sl["y_b"], 1)

            def combine(l):
                A = active(l)
                dve.wait_ge(loops_done, 5 * (l + 1))
                for i, t in enumerate(A):
                    a = comb[i % 2]
                    per = NT // 2 if l else 0
                    dve.wait_ge(s_comb[i % 2], 32 * (per + i // 2 + 1))
                    link(tt(a[:, 0, :], a[:, 0, :], a[:, 1, :], ALU.add))
                    link(tt(a[:, 0, :], a[:, 0, :], BC["gt2", 0 if t >= CT else 1], ALU.mult))
                    tt(XT[:, t, :], XT[:, t, :], a[:, 0, :], ALU.add).then_inc(combined, 1)
                if l == DEPTH - 1:
                    dve.wait_ge(s_gfin, 16)
                    for i, t in enumerate(A):
                        dve.wait_ge(ssq_ready, norm_no(l + 1, i))
                        inv_mean(ssq[:, t:t + 1], ssq[:, t:t + 1], D).then_inc(var_ready, 1)
                        dve.wait_ge(rstd_ready, norm_no(l + 1, i))
                        stt(XT[:, t, :], XT[:, t, :], rstd[:, t:t + 1], BC["A2", 0], ALU.mult, ALU.mult)\
                            .then_inc(fin_ready, 1)

            dve.wait_ge(s_con, 16)
            vec.tensor_copy(onesb[:], cst("ones"))
            vec.tensor_copy(trib[:], cst("tri"))
            vec.tensor_copy(tokb[:], cst("tokid"))
            dve.wait_ge(s_mask, 16)
            dve.wait_ge(sink_neg, 1)
            vec.tensor_copy(masks[:], K[:, 0:MASK + MASK2])
            vec.memset(zero[:], 0.0).then_inc(s_zero, 1)
            for job in jobs:
                kind, a, ps = job.kind, job.args, slot[job.slot] if job.drain else None
                mine = job.drain == "dve"
                l = a[0] if a else 0
                last = None
                if kind == "h" and a[1] == 0:
                    dve.wait_ge(ssq_ready, norm_no(l, 0))
                    inv_mean(ssq[:, 0:NT], ssq[:, 0:NT], D).then_inc(var_ready, 1)
                    dve.wait_ge(rstd_ready, norm_no(l, 0))
                    if l:
                        dve.wait_ge(s_xs, 16 * NT)
                    for t in range(NT):
                        ts(XT[:, t, :], XT[:, t, :], rstd[:, t:t + 1], None, ALU.mult).then_inc(xn_ready, 1)
                if mine:
                    dve.wait_ge(filled, job.fill)
                if kind == "vec":
                    last = vec.tensor_copy(vecT[:, l * NVEC:l * NVEC + NVEC], ps[:, 0:NVEC])
                elif kind == "mod":
                    if a[1] == 0:
                        after(dve, "vec", l)
                    at = l * 96 + 8 * a[1]
                    b4 = vecT[:, l * NVEC + V_B + 4 * a[1]:l * NVEC + V_B + 4 * a[1] + 4]
                    last = tt(modT[:, at:at + 8].rearrange("p (j s) -> p j s", s=2),
                              ps[:, 0:8].rearrange("p (j s) -> p j s", s=2), b4.unsqueeze(2).broadcast_to([P, 4, 2]), ALU.add)
                    if a[1] == 11:
                        last.then_inc(drained["dve"], 1)
                        last = None
                        dve.wait_ge(drained["dve"], job.count)
                        for i, (g, m) in enumerate(((V_GM, 1), (V_GF, 4))):
                            gain = vecT[:, l * NVEC + g:l * NVEC + g + DK].unsqueeze(2).broadcast_to([P, DK, 2])
                            ins = stt(AB[:, l * 32 + 16 * i:l * 32 + 16 * i + 16].rearrange("p (k s) -> p k s", s=2),
                                      modT[:, l * 96 + 16 * m:l * 96 + 16 * m + 16].rearrange("p (k s) -> p k s", s=2),
                                      1.0, gain, ALU.add, ALU.mult)
                        ins.then_inc(setup_dve, 1)
                elif kind == "h" and mine:
                    k = a[1]
                    if k == 1:
                        dve.wait_ge(setup_dve, DEPTH)
                    for at, tok, n, s in ((0, CTX, SEQ, 0), (512, 0, CTX, 1)):
                        last = ts(hT[:, k, tok:tok + n], ps[:, at:at + n], column(l, "A1", s, k), column(l, "sh1", s, k),
                                  ALU.mult, ALU.add)
                elif kind in ("rq", "rk"):
                    i = int(kind == "rk")
                    ev = full(l, kind) or bool(i)
                    v = sview(rb[:, i, :], ev)
                    ts(v, pview(ps, ev), 1.0 / (KVL if i else QL), EPS, ALU.mult, ALU.add).then_inc(drained["dve"], 1)
                    dve.wait_ge(drained["dve"], job.count)
                    vec.reciprocal(v, v).then_inc(rms_rec, 1)
                    dve.wait_ge(rms_sqrt, 2 * l + i + 1)
                    n, buf, g0 = (2, ckvT, V_GKV) if i else (3, cqT, V_GQ)
                    for k in range(n):
                        y = sview(buf[:, k, :], ev)
                        ins = stt(y, y, vecT[:, l * NVEC + g0 + k:l * NVEC + g0 + k + 1], v, ALU.mult, ALU.mult)
                    ins.then_inc(cn_ready, 1)
                elif kind == "krp":
                    dve.wait_ge(s_csm, 16 * (l + 1))
                    rotate(kr, ps, cs_m, 32).then_inc(roped, 1)
                    dve.wait_ge(roped, roped_no(l, "k"))
                elif kind == "qrp":
                    rotate(qr[:, a[1], :], ps, cs_m).then_inc(roped, 1)
                    dve.wait_ge(roped, roped_no(l, a[1]))
                elif kind in ("qsp", "ksp"):
                    if kind == "qsp" and a[1] == 0:
                        dve.wait_ge(s_css, 16 * (l + 1))
                    rotate(QS[:, a[1], :] if kind == "qsp" else KS, ps, cs_s).then_inc(roped, 1)
                    dve.wait_ge(roped, 8 * l + (4 + a[1] if kind == "qsp" else 8))
                elif kind in ("qn", "kn") and mine:
                    T_, ev = (QT, full(l, kind)) if kind == "qn" else (KT, True)
                    for hh in range(2):
                        last = vec.tensor_copy(sview(T_[0:64, 2 * a[1] + hh, :], ev), pview(ps[64 * hh:64 * hh + 64, :], ev, 64))
                elif kind == "v" and mine:
                    last = vec.tensor_copy(V[:, a[1], :], ps[:, 0:512])
                elif kind == "S":
                    _, br, i = a
                    t, h, at, parts = attn(l, br, i)
                    w = sum(n for _, _, n in parts)
                    g = tile_no(l, br, t)
                    dve.wait_ge(filled, job.fill)
                    m1, b1 = mx[:, i % 2:i % 2 + 1], nb[:, 8 * (g % 2) + h:8 * (g % 2) + h + 1]
                    if br == "m":
                        link(vec.tensor_reduce(m1, ps[:, 0:w], AX.X, ALU.max))
                        ts(b1, m1, -MLA_SCALE, None, ALU.mult).then_inc(max_ready, 1)
                    else:
                        if t < CT:
                            band = masks[:, MASK - CTX:MASK]
                        elif t == NT - 1:
                            band = masks[:, MASK:MASK + MASK2]
                        else:
                            band = masks[:, MASK - w:MASK]
                        vec.tensor_tensor_reduce(Pb[:, i % 2, 0:w], ps[:, at:at + w], band, 1.0, -3e38, ALU.add, ALU.max,
                                                 m1).then_inc(drained["dve"], 1)
                        dve.wait_ge(drained["dve"], job.count)
                        ns = sink[:, (2 * l + 1) * HEADS + h:(2 * l + 1) * HEADS + h + 1]
                        ts(b1, m1, -SWA_SCALE, ns, ALU.mult, ALU.min).then_inc(max_ready, 1)
                        if h == HEADS - 1:
                            dve.wait_ge(max_ready, max_no(l, br, i))
                            tt(nb[:, 16 + 8 * (g % 2):24 + 8 * (g % 2)], nb[:, 8 * (g % 2):8 * (g % 2) + 8],
                               sink[:, 2 * l * HEADS:(2 * l + 1) * HEADS], ALU.add).then_inc(sink_sum, 1)
                elif kind == "T" and mine:
                    n = P * len(key_tiles(l, a[1], a[2]))
                    last = vec.tensor_copy(PTb[:, a[2] % 2, 0:n], ps[:, 0:n])
                elif kind == "PV" and a[2] % HEADS == HEADS - 1:
                    _, br, i = a
                    t = attn(l, br, i)[0]
                    g = tile_no(l, br, t)
                    dve.wait_ge(o_full, g + 1)
                    d8, r8 = den[:, 8 * (g % 2):8 * (g % 2) + 8], rden[:, 8 * (g % 2):8 * (g % 2) + 8]
                    if br == "s":
                        dve.wait_ge(sink_exp, sink_no(l, t))
                        link(tt(d8, d8, nb[:, 16 + 8 * (g % 2):24 + 8 * (g % 2)], ALU.add))
                    link(vec.reciprocal(r8, d8))
                    tt(ytok[:, g % 2, :].rearrange("p (h n) -> p h n", h=HEADS), OB[g % 2].rearrange("p (h n) -> p h n", h=HEADS),
                       r8.unsqueeze(2).broadcast_to([P, HEADS, VD]), ALU.mult).then_inc(o_drained, 1)
                elif kind == "pm":
                    g = a[1]
                    sc = vecT[:, l * NVEC + V_PS + g:l * NVEC + V_PS + g + 1]
                    last = ts(Yp[:, g, CTX:TOK], ps[:, 0:SEQ], sc, None, ALU.mult)
                    if l < DEPTH - 1:
                        last = ts(Yp[:, g, 0:CTX], ps[:, 512:512 + CTX], sc, None, ALU.mult)
                elif kind == "b":
                    _, n2, b, cc = a
                    i = gate_no(n2, b, cc)
                    after(dve, "g", *a)
                    ev = full(l, kind)
                    gate, mrow = sview(SG[:, i % 2, :], ev), sview(MG[:, 2 * n2 + cc, :], ev)
                    if b == 0:
                        last = tt(mrow, gate, pview(ps, ev), ALU.mult)
                    else:
                        tmp = sview(mtmp[:, i % 2, :], ev)
                        link(tt(tmp, gate, pview(ps, ev), ALU.mult))
                        last = tt(mrow, mrow, tmp, ALU.add)
                elif kind == "o":
                    t = a[1]
                    n = active(l).index(t)
                    s = 0 if t >= CT else 1
                    if n == 0:
                        dve.wait_ge(s_xr, 32 if l == 0 else 48)
                        for which in ("gt1", "A2", "B2"):
                            after(dve, "bc", l, which, 0)
                            if l < DEPTH - 1:
                                after(dve, "bc", l, which, 1)
                    link(tt(otmp, ps, BC["gt1", s], ALU.mult))
                    tt(XT[:, t, :], XT[:, t, :], otmp, ALU.add).then_inc(drained["dve"], 1)
                    dve.wait_ge(ssq_ready, norm_no(l, n + 1))
                    inv_mean(ssq[:, t:t + 1], ssq[:, t:t + 1], D).then_inc(var_ready, 1)
                    dve.wait_ge(rstd_ready, norm_no(l, n + 1))
                    if n >= 2:
                        after(dve, "f", l, active(l)[n - 2])
                        dve.wait_ge(s_h[n % 2], store_no(l, n) - 16)
                    fr = fb[:, n % 2, :]
                    link(stt(fr, XT[:, t, :], rstd[:, t:t + 1], BC["A2", s], ALU.mult, ALU.mult))
                    tt(fr, fr, BC["B2", s], ALU.add).then_inc(f_ready, 1)
                elif kind == "r":
                    pass
                elif kind == "sg":
                    n = active(l).index(a[1])
                    dve.wait_ge(sh_silu, n + 1 + (NT if l else 0))
                    last = tt(hb[:, n % 2, :], s1[:, n % 2, :], ps[:, DE:2 * DE], ALU.mult)
                    last.then_inc(drained["dve"], 1)
                    last = None
                    route(l, a[1])
                elif kind == "pos":
                    t = a[1]
                    last = tt(posm[:, t * E:t * E + E], ps[:, 0:E], Mb[:, t * E:t * E + E], ALU.mult)
                elif kind == "cnt":
                    link(vec.tensor_copy(endc[0:E, 0:1], ps[0:E, 0:1]))
                    link(ts(endc[0:E, 1:1 + MAXB], cst("thr", E), endc[0:E, 0:1], None, ALU.is_lt))
                    link(vec.tensor_reduce(endc[0:E, 8:9], endc[0:E, 1:1 + MAXB], AX.X, ALU.add))
                    last = vec.tensor_copy(nbb[0:E, 0:1], endc[0:E, 8:9])
                elif kind == "end":
                    link(vec.tensor_copy(endc[0:E, 9:10], ps[0:E, 0:1]))
                    last = ts(Gb[0:E, :], cst("iotan", E), endc[0:E, 9:10], None, ALU.is_ge)
                elif kind == "tab":
                    ts(tabf[0:1, 0:TABN], ps[0:1, 0:TABN], float(E - 1), None, ALU.min)
                    link(tt(tabf[0:1, TABN:2 * TABN], cst("iotan", 1), ps[0:1, 128:128 + TABN], ALU.subtract))
                    ts(tabf[0:1, TABN:2 * TABN], tabf[0:1, TABN:2 * TABN], float(MAXB - 1), None, ALU.min)
                    link(vec.tensor_copy(tabf[0:1, 2 * TABN:2 * TABN + 1], ps[0:1, 256:257]))
                    last = vec.tensor_copy(tab[0:1, 0:2 * TABN + 1], tabf[0:1, 0:2 * TABN + 1])
                    last.then_inc(drained["dve"], 1)
                    last = None
                    dve.wait_ge(drained["dve"], job.count)
                    dve.sem_inc(tab_ready, 1)
                elif kind == "moe":
                    moe(l)
                    loop_end(dve)
                    combine(l)
                if last is not None:
                    last.then_inc(drained["dve"], 1)
                elif kind in ("krp", "qrp", "qsp", "ksp"):
                    dve.sem_inc(drained["dve"], 1)

        @block.gpsimd
        def _(pool):
            gp = nc.gpsimd

            turns = s_turns

            def link(ins):
                step("pool", pool, ins)

            for l in range(DEPTH):
                pool.dma_start(bias[:, l * E:l * E + E], router_bias[l].partition_broadcast(P)).then_inc(s_row, 16)
                pool.dma_start(sink[:, 2 * l * HEADS:(2 * l + 1) * HEADS], swa_sink[l].partition_broadcast(P)).then_inc(s_row, 16)
            pool.wait_ge(s_con, 16)
            pool.wait_ge(s_row, 32 * DEPTH)
            for l in range(DEPTH):
                ins = gp.tensor_scalar(sink[:, (2 * l + 1) * HEADS:(2 * l + 2) * HEADS],
                                       sink[:, 2 * l * HEADS:(2 * l + 1) * HEADS], -1.0, None, ALU.mult)
            ins.then_inc(sink_neg, 1)
            pool.wait_ge(s_zero, 1)
            zr = zero[:].unsqueeze(1).broadcast_to([P, 4, 256])
            pool.dma_start(H[TOK:TOK + P, 0:D].rearrange("p (a n) -> p a n", a=4), zr).then_inc(s_hz, 16)
            pool.dma_start(H[TOK:TOK + P, D:HROW], zero[:, 0:E]).then_inc(s_hz, 16)
            pool.wait_ge(s_hz, 32)
            for l in range(DEPTH):
                A, sl = active(l), L[l]
                pool.wait_ge(filled, names["yT", l, "m", NT - 1].fill)
                gp.memset(K[:, 0:4 * UW], 0.0).then_inc(u_zero, 1)
                pool.wait_ge(u_zero, l + 1)
                lo, hi = (0, UW) if l < DEPTH - 1 else (UL - 8, UW)
                for g in range(4):
                    after(pool, "u", l, g)
                    u, bufs = U[:, g, :], [UT[:, 0, :], UT[:, 1, :]]
                    link(gp.tensor_tensor(bufs[0][:, lo + 1:hi], u[:, lo:hi - 1], u[:, lo + 1:hi], ALU.add))
                    src, a, b = 0, lo + 1, hi
                    for d in (1, 2, 4)[:g]:
                        a, b = a + d, b - d
                        link(gp.tensor_tensor(bufs[1 - src][:, a:b], bufs[src][:, a - d:b - d], bufs[src][:, a + d:b + d], ALU.add))
                        src = 1 - src
                    w = bufs[src]
                    link(gp.tensor_scalar(w[:, a:b], w[:, a:b], 1.0 / (2 << g), None, ALU.mult))
                    e0 = CONSTS["edges"][0] + 16 * g
                    edge = con[:, e0:e0 + 16].rearrange("p (a n) -> p a n", a=2)
                    for start, n in ((UL, SEQ), (UC, CTX))[:2 if l < DEPTH - 1 else 1]:
                        for side in range(2):
                            v = w[:, start + side * (n - 8):start + side * (n - 8) + 8]
                            ins = gp.tensor_tensor(v, v, edge[:, side, :], ALU.mult)
                        link(ins)
                    for start, n in ((UL, SEQ), (UC, CTX))[:2 if l < DEPTH - 1 else 1]:
                        ins = gp.tensor_tensor(u[:, start:start + n], w[:, start:start + n], u[:, start:start + n], ALU.subtract)
                    ins.then_inc(pooled, 1)
                    pool.wait_ge(pooled, 4 * l + g + 1)
                for n, t in enumerate(A):
                    pool.wait_ge(f_ready, n + 1 + (NT if l else 0))
                    pool.dma_start(H[t * P:t * P + P, 0:D], fb[:, n % 2, :]).then_inc(s_h[n % 2], 16)
                    pool.dma_start(ACC[1][t * P:t * P + P, :].rearrange("p (a n) -> p a n", a=4), zr).then_inc(s_acc1, 16)
                for n, t in enumerate(A):
                    pool.wait_ge(w_ready, n + 1 + (NT if l else 0))
                    pool.dma_start(H[t * P:t * P + P, D:HROW], Wt[:, n % 2, :]).then_inc(s_w[n % 2], 16)
                    after(pool, "sd", l, t)
                    pool.dma_start(ACC[0][t * P:t * P + P, :], yb[:, n % 2, :]).then_inc(s_sh[n % 2], 16)
                for s in range(2):
                    for q in (s_h, s_w, s_sh):
                        pool.wait_ge(q[s], store_no(l, len(A) - 2 + s))
                pool.wait_ge(s_acc1, 16 * (NT + (len(A) if l else 0)))
                for s in range(2):
                    pool.dma_start(ACC[s][TOK:TOK + P, :].rearrange("p (a n) -> p a n", a=4), zr).then_inc(sl[f"scat{s}"], 16)
                pool.wait_ge(tab_ready, l + 1)
                n_blocks = pool.value_load(tab[0:1, 2 * TABN:2 * TABN + 1], min_val=1, max_val=max_blocks(l))

                def gather(s, i4, count):
                    pool.wait_ge(sl["idx_ready"], count)
                    pool.sem_inc(turns, 1)
                    pool.indirect_dma_start(xg[:, s, :], None, H, bass.IndirectOffsetOnAxis(ap=idx[:, i4:i4 + 1], axis=0))\
                        .then_inc(sl[f"gat{s}"], 16)

                for s in range(2):
                    gather(s, s, s + 1)
                with pool.Fori(0, max_blocks(l) // UNROLL) as m:
                    for r in range(UNROLL):
                        n, s = UNROLL * m + r, r % 2
                        with pool.If(n < n_blocks):
                            pool.wait_ge(sl["h_ready"], n + 1)
                            gather(s, (r + 2) % 4, n + 3)
                            pool.wait_ge(sl["y_a"], n + 2)
                            pool.wait_ge(sl["y_b"], n + 2)
                            pool.wait_ge(sl[f"scat{s}"], 16 * ((UNROLL // 2) * m + r // 2 + 1))
                            pool.sem_inc(turns, 1)
                            pool.indirect_dma_start(ACC[s], bass.IndirectOffsetOnAxis(ap=idx[:, r:r + 1], axis=0),
                                                    yb[:, s, :], None, compute_op=ALU.add).then_inc(sl[f"scat{s}"], 16)
                pool.wait_ge(sl["scat0"], 16 * ((n_blocks + 1) // 2) + 16)
                pool.wait_ge(sl["scat1"], 16 * (n_blocks // 2) + 16)
                pool.wait_ge(sl["gat0"], 16 * ((n_blocks + 1) // 2) + 16)
                pool.wait_ge(sl["gat1"], 16 * (n_blocks // 2) + 16)
                pool.sem_inc(turns, 1)
                loop_end(pool)


def constants():
    import numpy as np
    con = np.zeros((P, NCONST), np.float32)

    def put(name, v):
        a, b = CONSTS[name]
        con[:, a:b] = v
    i = np.arange(P)
    put("ident", np.eye(P))
    put("ones", 1.0)
    put("perm16", (i[:, None] ^ 16) == i[None, :])
    put("perm8", (i[:, None] ^ 8) == i[None, :])
    put("tri", i[:, None] <= i[None, :])
    put("tokid", np.stack([np.stack([i, np.full(P, P * t), np.ones(P)], 1) for t in range(NT)], 1).reshape(P, -1))
    put("thr", P * np.arange(MAXB))
    put("iotan", np.arange(TABN))
    put("dummy", (TOK + i)[:, None])
    put("negdummy", -(TOK + i)[:, None])
    edges = np.ones((4, 2, 8))
    for g in range(4):
        w = 2 << g
        for j in range(8):
            edges[g, 0, j] = w / (j + w // 2 - max(j - w // 2, 0))
            edges[g, 1, j] = w / (min(w // 2, 8 - j) + w // 2)
    put("edges", edges.reshape(1, -1))
    put("lower", (np.arange(8)[None, :] < np.arange(8)[:, None]).reshape(1, -1))
    put("slot1", 1 + np.arange(TOK))
    prev = np.where(i[None, :] >= i[:, None], 0.0, NEG)
    nxt = np.where(i[None, :] <= i[:, None], 0.0, NEG)
    mask = np.concatenate([prev, np.zeros((P, P)), nxt, np.zeros((P, CTX)), prev, np.zeros((P, 3 * P))], 1)

    def rope(dim):
        n = dim // 4
        t = np.arange(SEQ)
        inv = np.float32(10000.0) ** (-np.arange(n, dtype=np.float32) / np.float32(n))
        table = np.zeros((P, 2, SEQ), np.float32)
        for p in range(P):
            part, f = p % dim // n, p % n
            pos = (t // 64 if part < 2 else t % 64).astype(np.float32)
            ang = pos * inv[f]
            table[p, 0] = np.cos(ang)
            table[p, 1] = np.sin(ang) * (-1 if part % 2 == 0 else 1)
        return table
    return {"consts": con, "mask": mask.astype(np.float32), "rope_mla": rope(ROPE), "rope_swa": rope(HD)}


_INS = ['x', 'c', 'ctx', 'c_ctx', 'w_mod', 'b_mod', 'g_mix', 'g_ffn', 'w_in', 'g_mla_q', 'g_mla_kv', 'w_mla_uq',
        'w_mla_ukv', 'w_pool', 'pool_scale', 'swa_sink', 'w_br_mla', 'w_br_pool', 'w_br_swa', 'w_out', 'w_router',
        'router_bias', 'w_exp_gate', 'w_exp_up', 'w_exp_down', 'w_sh_gate', 'w_sh_up', 'w_sh_down', 'g_final']


def kernel(**inputs):
    import numpy as np
    import concourse.bacc as bacc
    from concourse.bass_utils import run_bass_kernel_spmd
    nc = bacc.Bacc("TRN2", target_bir_lowering=False, num_devices=1)
    arrays, args = {}, []
    for name, a in [(n, inputs[n]) for n in _INS] + list(constants().items()):
        a = np.ascontiguousarray(a)
        arrays[f"in_{name}"] = a
        args.append(nc.dram_tensor(f"in_{name}", a.shape, mybir.dt.from_np(a.dtype), kind="ExternalInput").ap())
    args.append(nc.dram_tensor("out_0", (1, SEQ, D), F32, kind="ExternalOutput").ap())
    build(nc, *args)
    r = run_bass_kernel_spmd(nc, [arrays], core_ids=[0])
    return r.results[0]["out_0"]
```

```python
from contextlib import ExitStack

import concourse.bass as bass
from concourse import mybir

F32, BF16, I32 = mybir.dt.float32, mybir.dt.bfloat16, mybir.dt.int32
ALU, ACT, AX = mybir.AluOpType, mybir.ActivationFunctionType, mybir.AxisListType

P = 128
D, DEPTH, SEQ, CTX = 1024, 2, 512, 256
DK = D // P
TOK = CTX + SEQ
NT, CT = TOK // P, CTX // P
EPS = 1e-6
QL, KVL, ROPE, POOLW, SWQ, SWKV = 384, 256, 32, 512, 512, 128
OFF_CQ, OFF_CKV, OFF_U, OFF_QS, OFF_KS, OFF_G = 0, 384, 672, 1184, 1696, 1952
HEADS, NOPE, VD, HD = 8, 64, 64, 64
MLA_SCALE, SWA_SCALE = (NOPE + ROPE) ** -0.5, HD ** -0.5
E, DE, TOPK, GROUPS, KEEP = 64, 256, 8, 8, 4
ROUTED = 2.5
NEG = -1e30
UW = 800
UC, UL = 8, 8 + CTX + 16
MAXB = TOK // P
TABN = 120
UNROLL = 4
HROW = D + E
RING, SLOT = 3, 4096
NVEC = 73
V_B, V_GM, V_GF, V_PS, V_GQ, V_GKV = 0, 48, 56, 64, 68, 71

CONSTS = {}
_at = 0
for _name, _n in (("ident", 128), ("ones", 128), ("perm16", 128), ("perm8", 128), ("tri", 128), ("tokid", 3 * NT), ("sel2", 2),
                  ("thr", MAXB), ("iotan", TABN), ("dummy", 1), ("negdummy", 1), ("edges", 64), ("lower", 64),
                  ("slot1", TOK)):
    CONSTS[_name] = (_at, _at + _n)
    _at += _n
NCONST = _at
MASK, MASK2 = 640, 512


def active(l):
    return list(range(NT)) if l < DEPTH - 1 else list(range(CT, NT))


def max_blocks(l):
    return (len(active(l)) * P * TOPK + E * (P - 1)) // P


def max_turns(l):
    return -(-max_blocks(l) // UNROLL) * UNROLL


class Job:
    def __init__(self, kind, args, drain, slot, fill, count):
        self.kind, self.args, self.drain, self.slot, self.fill, self.count = kind, args, drain, slot, fill, count


def make_plan():
    jobs, names, panels = [], {}, []
    counts = {"act": 0, "dve": 0}

    def add(kind, *args, drain=None, panel=None):
        if drain is None:
            jobs.append(Job(kind, args, None, None, None, None))
            return
        counts[drain] += 1
        n = counts["act"] + counts["dve"]
        job = Job(kind, args, drain, (n - 1) % 3, n, counts[drain])
        jobs.append(job)
        names[(kind,) + args] = job
        for p in (panel if isinstance(panel, list) else [panel] if panel else []):
            if not panels or all(q[0] != p for q in panels):
                panels.append([p, job])
            for q in panels:
                if q[0] == p:
                    q[1] = job

    def modulation(l, p, *between):
        add("modr", l, p, drain="act", panel=("mod", l, p))
        for kind, args, kw in between:
            add(kind, *args, **kw)
        add("mod", l, p, drain="dve")

    rest = [(0, p) for p in range(4, 12)] + [(l, p) for l in range(1, DEPTH) for p in range(12)]

    def more_modulation(*between):
        if rest:
            modulation(*rest.pop(0), *between)
        else:
            for kind, args, kw in between:
                add(kind, *args, **kw)

    def attention(l, br):
        items = [(t, h) for t in active(l) for h in range(HEADS)]
        late = []
        add("S", l, br, 0, drain="act" if br == "m" else "dve")
        for i in range(len(items) + 2):
            if l == 0 and br == "s" and i in (16, 32):
                more_modulation()
            if i + 1 < len(items):
                add("S", l, br, i + 1, drain="act" if br == "m" else "dve")
            if i < len(items):
                add("T", l, br, i, drain="act" if i % 2 else "dve")
            for t in late:
                add("yT", l, br, t, drain="act")
            late = []
            if 1 <= i <= len(items):
                add("PV", l, br, i - 1)
                if items[i - 1][1] == HEADS - 1:
                    late.append(items[i - 1][0])

    alt = ["act", "dve"]
    add("cvec", drain="act")
    for l in range(DEPTH):
        add("vec", l, drain="dve")
    for p in range(4):
        modulation(0, p)
    for l in range(DEPTH):
        A = active(l)

        for k in range(DK):
            add("h", l, k, drain=alt[k % 2])
        for c in range(2):
            add("ckv", l, c, drain="act", panel=("ckv", l))
        add("kr", l, drain="act", panel=("ckv", l))
        more_modulation(("rk", (l,), dict(drain="dve")))
        add("krp", l, drain="dve")
        for c in range(3):
            add("cq", l, c, drain="act", panel=("cq", l))
        more_modulation(("rq", (l,), dict(drain="dve")))
        for j in range(4):
            add("kn", l, j, drain=alt[j % 2], panel=("ukv", l))
        for t in range(NT):
            add("v", l, t, drain=alt[t % 2], panel=("ukv", l))
        more_modulation()
        for j in range(2):
            add("qr", l, j, drain="act", panel=("uq", l))
            add("qrp", l, j, drain="dve")
        for j in range(4):
            add("qn", l, j, drain=alt[j % 2], panel=("uq", l))
        attention(l, "m")
        for c in range(4):
            add("qs", l, c, drain="act", panel=("qs", l))
            add("qsp", l, c, drain="dve")
        more_modulation()
        add("ks", l, drain="act", panel=("ks", l))
        more_modulation(("ksp", (l,), dict(drain="dve")), ("vs", (l,), dict(drain="act", panel=("ks", l))))
        for c in range(3):
            add("u", l, c, drain="act", panel=("u", l))
        more_modulation(("u", (l, 3), dict(drain="act", panel=("u", l))))
        attention(l, "s")
        for g in range(4):
            add("pm", l, g, drain="dve", panel=("pm", l))
        for n2 in range(DK // 2):
            for b in range(3):
                jobs4 = [(k, (l, n2, b, c), dict(drain=e, panel=("merge", l, n2, b)))
                         for c in range(2) for k, e in (("g", "act"), ("b", "dve"))]
                add(jobs4[0][0], *jobs4[0][1], **jobs4[0][2])
                more_modulation(*jobs4[1:3])
                add(jobs4[3][0], *jobs4[3][1], **jobs4[3][2])
        assert not rest
        streams = (0, 1) if l < DEPTH - 1 else (0,)
        for which in ("gt1", "A2", "B2"):
            for s in streams:
                add("bc", l, which, s, drain="act")
        for i, t in enumerate(A):
            add("o", l, t, drain="dve", panel=[("wo", l, 0), ("wo", l, 1)])
            if i:
                add("f", l, A[i - 1], drain="act")
        for s in streams:
            add("bc", l, "gt2", s, drain="act")
        add("f", l, A[-1], drain="act")
        for t in A:
            add("r", l, t, drain="act", panel=("router", l))
        for i, t in enumerate(A):
            if i == len(A) - 1:
                for u in A:
                    add("pos", l, u, drain="dve")
                add("cnt", l, drain="dve")
                add("end", l, drain="dve")
                add("tab", l, drain="dve")
                add("first", l)
            add("sg", l, t, drain="dve", panel=("shgu", l))
            add("sT", l, t, drain="act")
            add("sd", l, t, drain="act", panel=("shd", l))
        add("moe", l)
    return jobs, names, panels


def build(nc, x, c, ctx, c_ctx, w_mod, b_mod, g_mix, g_ffn, w_in, g_mla_q, g_mla_kv, w_mla_uq, w_mla_ukv, w_pool,
          pool_scale, swa_sink, w_br_mla, w_br_pool, w_br_swa, w_out, w_router, router_bias, w_exp_gate, w_exp_up,
          w_exp_down, w_sh_gate, w_sh_up, w_sh_down, g_final, consts, mask, rope_mla, rope_swa, out):
    H = nc.dram_tensor("h_rows", [TOK + P, HROW], F32, kind="Internal").ap()
    ACC = [nc.dram_tensor(f"acc{i}", [TOK + P, D], F32, kind="Internal").ap() for i in range(2)]
    XS = nc.dram_tensor("x_saved", [TOK, D], F32, kind="Internal").ap()
    jobs, names, panels = make_plan()
    panel_no = {p[0]: n for n, p in enumerate(panels)}

    with ExitStack() as stack:
        def sb(name, n, dt=F32, rows=P):
            return stack.enter_context(nc.sbuf_tensor(name, [rows, n], dt))

        def sem(name):
            return stack.enter_context(nc.semaphore(name))

        XA = sb("region_x", 6144)
        HT = sb("region_h", 6144)
        Q = sb("region_q", 6144)
        K = sb("region_k", 6144)
        VY = sb("region_v", 6144)
        C = sb("region_c", 4608)
        ring = sb("ring", RING * SLOT)
        con = sb("con", NCONST)
        masks = sb("masks", MASK + MASK2, BF16)

        def cst(name, rows=P):
            a, b = CONSTS[name]
            return con[0:rows, a:b]
        ident = cst("ident")
        vecs = sb("vecs", P)
        cT = sb("cT", DK * 32)
        cTk = cT[:].rearrange("p (k m) -> p k m", k=DK)
        vecT = sb("vecT", DEPTH * NVEC)
        modT = sb("modT", DEPTH * 96)
        AB = sb("AB", DEPTH * 32)
        ssq, rstd = sb("ssq", 8), sb("rstd", 8)
        zero = sb("zero", 256)
        scores = sb("scores", NT * E)
        posm = sb("posm", NT * E)
        rt = sb("rt", 6 * E)
        rsm = sb("rsm", 64)
        Mb = sb("Mb", NT * E, BF16)
        onesb, trib, tokb = sb("onesb", P, BF16), sb("trib", P, BF16), sb("tokb", 3 * NT, BF16)
        nbb, Gb = sb("nbb", 2, BF16), sb("Gb", TABN, BF16)
        endc = sb("endc", 16)
        tab = sb("tab", 2 * TABN + 8, I32, 1)
        idx = sb("idx", 4, I32)
        idxf = sb("idxf", 2)
        pcol = sb("pcol", 3)
        bias = sb("bias", DEPTH * E)
        sink = sb("sink", 2 * DEPTH * HEADS)
        mx, nb = sb("mx", 4), sb("nb", 32)
        den, rden = sb("den", 16), sb("rden", 16)

        XT = XA[:].rearrange("p (t d) -> p t d", t=NT)
        hT = HT[:].rearrange("p (k n) -> p k n", k=DK)
        cqT = C[:, 0:2304].rearrange("p (c n) -> p c n", c=3)
        ckvT = C[:, 2304:3840].rearrange("p (c n) -> p c n", c=2)
        tmpr = C[:, 3840:4352]

        def modrow(l, p):
            return VY[:, 4096:4608] if (l, p) < (0, 7) else VY[:, 1024:1536]
        XN = Q[:].rearrange("p (t d) -> p t d", t=NT)
        sq = XA[:, 0:3840].rearrange("p (c n) -> p c n", c=5)
        qr = XA[:, 3840:5376].rearrange("p (c n) -> p c n", c=2)
        kr = XA[0:32, 5376:6144]
        rb = Q[:, 0:1536].rearrange("p (c n) -> p c n", c=2)
        QT = Q[:].rearrange("p (h n) -> p h n", h=HEADS)
        KT = K[:].rearrange("p (h n) -> p h n", h=HEADS)
        V = VY[:, 0:3072].rearrange("p (t n) -> p t n", t=NT)
        Ym = VY[:, 3072:6144].rearrange("p (c n) -> p c n", c=4)
        cs_m = VY[:, 3072:4096].rearrange("p (a n) -> p a n", a=2)
        cs_s = VY[:, 0:1024].rearrange("p (a n) -> p a n", a=2)
        Ys = XA[:, 0:3072].rearrange("p (c n) -> p c n", c=4)
        Yp = XA[:, 3072:6144].rearrange("p (c n) -> p c n", c=4)
        Y = {"m": Ym, "s": Ys}
        Pb = C[:, 0:1536].rearrange("p (a n) -> p a n", a=2)
        PTb = C[:, 1536:3072].rearrange("p (a n) -> p a n", a=2)
        ytok = C[:, 3072:4096].rearrange("p (a n) -> p a n", a=2)
        QS = Q[:, 0:3072].rearrange("p (c n) -> p c n", c=4)
        KK = Q[:, 3072:4608].rearrange("p (c n) -> p c n", c=2)
        VS = Q[:, 4608:5376].rearrange("p (t n) -> p t n", t=NT)
        KS = Q[:, 5376:6144]
        U = K[:, 0:4 * UW].rearrange("p (c n) -> p c n", c=4)
        UT = K[:, 4 * UW:6 * UW].rearrange("p (c n) -> p c n", c=2)
        MG = K[:].rearrange("p (k n) -> p k n", k=DK)
        SG = C[:, 0:1536].rearrange("p (a n) -> p a n", a=2)
        mtmp = C[:, 1536:3072].rearrange("p (a n) -> p a n", a=2)
        BC = {("A2", 0): Q[:, 0:1024], ("A2", 1): Q[:, 1024:2048], ("B2", 0): Q[:, 2048:3072],
              ("B2", 1): Q[:, 3072:4096], ("gt1", 0): Q[:, 4096:5120], ("gt1", 1): Q[:, 5120:6144]}
        BC["gt2", 0], BC["gt2", 1] = BC["gt1", 0], BC["gt1", 1]
        fb = C[:, 0:2048].rearrange("p (a n) -> p a n", a=2)
        junk = C[:, 2048:3072]
        otmp = C[:, 3072:4096]
        Wt = rt[:, 4 * E:6 * E].rearrange("p (a n) -> p a n", a=2)
        tabf = rt[0:1, 0:2 * TABN + 8]
        xg = C[:, 0:2 * HROW].rearrange("p (a n) -> p a n", a=2)
        s1 = C[:, 2176:2688].rearrange("p (a n) -> p a n", a=2)
        hb = C[:, 2688:3200].rearrange("p (a n) -> p a n", a=2)
        hTb = C[:, 3200:3712].rearrange("p (a n) -> p a n", a=2)
        oh = C[:, 3712:4480].bitcast(BF16).rearrange("p (a t s) -> p a t s", a=2, t=NT)
        xgT = Q[:, 0:2048].rearrange("p (a k s) -> p a k s", a=2, k=DK)
        yb = Q[:, 2048:4096].rearrange("p (a n) -> p a n", a=2)
        WSL = [K, VY]
        wgu = [w[:, 0:4096].rearrange("p (g k n) -> p g k n", g=2, k=DK) for w in WSL]
        wdn = [w[:, 4096:6144].rearrange("p (c n) -> p c n", c=2) for w in WSL]
        comb = [VY[:, 0:2048].rearrange("p (a n) -> p a n", a=2), VY[:, 2048:4096].rearrange("p (a n) -> p a n", a=2)]

        PS = stack.enter_context(nc.psum_tensor("ps", [P, 4096], F32))
        slot = [PS[:, 1024 * i:1024 * i + 1024] for i in range(3)]
        OB = [PS[:, 3072:3584], PS[:, 3584:4096]]
        m_gu = [PS[:, 0:512], PS[:, 512:1024]]
        m_tr, m_y = PS[:, 1024:2048], PS[:, 2048:3072]
        m_h, m_i = PS[:, 3072:3328], PS[:, 3584:3587]

        s_con, s_vec, s_mask = sem("s_con"), sem("s_vec"), sem("s_mask")
        s_panel = [sem(f"s_panel{i}") for i in range(RING)]
        filled = sem("filled")
        drained = {"act": sem("drained_act"), "dve": sem("drained_dve")}
        s_x, s_xs, s_xr = sem("s_x"), sem("s_xs"), sem("s_xr")
        s_csm, s_css = sem("s_csm"), sem("s_css")
        ssq_ready, var_ready, rstd_ready, xn_ready = sem("ssq_ready"), sem("var_ready"), sem("rstd_ready"), sem("xn_ready")
        rms_rec, rms_sqrt, cn_ready = sem("rms_rec"), sem("rms_sqrt"), sem("cn_ready")
        roped, rope_copied = sem("roped"), sem("rope_copied")
        max_ready, exp_ready, o_full, o_drained = sem("max_ready"), sem("exp_ready"), sem("o_full"), sem("o_drained")
        sink_sum, sink_exp = sem("sink_sum"), sem("sink_exp")
        kk_ready, u_zero, pooled = sem("kk_ready"), sem("u_zero"), sem("pooled")
        x_new, f_ready, s_h = sem("x_new"), sem("f_ready"), [sem("s_h0"), sem("s_h1")]
        w_ready, s_w = sem("w_ready"), [sem("s_w0"), sem("s_w1")]
        sh_silu, sh_ready, s_sh = sem("sh_silu"), sem("sh_ready"), [sem("s_sh0"), sem("s_sh1")]
        setup_dve, s_zero, tab_ready = sem("setup_dve"), sem("s_zero"), sem("tab_ready")
        s_turns = sem("s_turns")
        cT_zero = sem("cT_zero")
        s_row, s_hz, s_acc1, sink_neg = sem("s_row"), sem("s_hz"), sem("s_acc1"), sem("sink_neg")
        s_comb, combined, s_out = [sem("s_comb0"), sem("s_comb1")], sem("combined"), sem("s_out")
        s_gfin, fin_ready = sem("s_gfin"), sem("fin_ready")
        loops_done, layer_done = sem("loops_done"), sem("layer_done")
        L = [{n: sem(f"{n}_{l}") for n in ("wgu0", "wgu1", "wdn0", "wdn1", "gu_done", "tr_done", "hT_done", "idx_done",
                                             "dn_done", "silu_done", "h_ready", "xgT_a", "xgT_b", "hT_ev", "idx_ready",
                                             "oh_ready", "y_a", "y_b", "gat0", "gat1", "scat0", "scat1", "idx_copied", "idx_low")}
             for l in range(DEPTH)]
        chain = {e: [sem(f"chain_{e}"), 0] for e in ("act", "dve", "pool")}

        def step(e, eng, ins):
            chain[e][1] += 1
            ins.then_inc(chain[e][0], 1)
            eng.wait_ge(chain[e][0], chain[e][1])

        def after(eng, *name):
            j = names[name]
            eng.wait_ge(drained[j.drain], j.count)

        def full(l, kind):
            return l < DEPTH - 1 or kind in ("ckv", "kr", "ks")

        def pview(ps, everything, rows=P):
            return ps[0:rows, :].rearrange("p (b n) -> p b n", b=2)[:, :, 0:TOK // 2] if everything else ps[0:rows, 0:SEQ]

        def sview(buf, everything):
            return buf.rearrange("p (b n) -> p b n", b=2) if everything else buf[:, CTX:TOK]

        def attn(l, br, i):
            t, h = active(l)[i // HEADS], i % HEADS
            if br == "m":
                return t, h, 0, [(0, 0, 512), (512, 512, 256)] if t >= CT else [(0, 0, CTX)]
            if t < CT:
                return t, h, 512, [(512, 0, CTX)]
            a, b = max(CT, t - 1), min(NT - 1, t + 1)
            n = (b - a + 1) * P
            return t, h, 512 - n, [(512 - n, a * P, n), (512, 0, CTX)]

        def key_tiles(l, br, i):
            return [k // P + j for _, k, n in attn(l, br, i)[3] for j in range(n // P)]

        def exp_no(l, i):
            return (HEADS * NT if l else 0) + i + 1

        def tile_no(l, br, t):
            return (2 * NT if l else 0) + (len(active(l)) if br == "s" else 0) + active(l).index(t)

        def column(l, which, s, k):
            if which in ("A1", "A2"):
                at = l * 32 + (16 if which == "A2" else 0) + 2 * k + s
                return AB[:, at:at + 1]
            at = l * 96 + 2 * (8 * {"sh1": 0, "gt1": 2, "B2": 3, "gt2": 5}[which] + k) + s
            return modT[:, at:at + 1]

        def norm_no(l, i):
            return [0, 1 + NT, 2 + NT + len(active(1))][l] + i + 1

        def roped_no(l, what):
            return 8 * l + {"k": 1, 0: 2, 1: 3, "s": 8}[what]

        def max_no(l, i):
            return (HEADS * NT if l else 0) + i + 1

        def sink_no(l, t):
            return (NT if l else 0) + active(l).index(t) + 1

        def gate_no(n2, b, cc):
            return 6 * n2 + 2 * b + cc

        def gate_args(i):
            return i // 6, i % 6 // 2, i % 2

        def store_no(l, n):
            return 16 * ((NT // 2 if l else 0) + n // 2 + 1)

        block = stack.enter_context(nc.Block())

        def loop_end(eng):
            eng.drain().then_inc(loops_done, 1)

        @block.sync
        def _(sp):
            sp.dma_start(con[:], consts).then_inc(s_con, 16)
            sp.dma_start(K[:, 0:MASK + MASK2], mask).then_inc(s_mask, 16)
            sp.dma_start(vecs[0:8, :], c.rearrange("a (k p) -> (a k) p", p=P)).then_inc(s_vec, 16)
            sp.dma_start(vecs[8:16, :], c_ctx.rearrange("(k p) -> k p", p=P)).then_inc(s_vec, 16)
            sp.dma_start(XT[:, 0:CT, :], ctx[0].rearrange("(t p) d -> p t d", p=P)).then_inc(s_x, 16)
            sp.dma_start(XT[:, CT:NT, :], x[0].rearrange("(t p) d -> p t d", p=P)).then_inc(s_x, 16)
            for l in range(DEPTH):
                sp.wait_ge(filled, l + 1)
                at = 0
                for v in (b_mod, g_mix, g_ffn, pool_scale, g_mla_q, g_mla_kv):
                    rows = v.shape[1] // P
                    sp.dma_start(vecs[at:at + rows, :], v[l].rearrange("(k p) -> k p", p=P)).then_inc(s_vec, 16)
                    at += rows
                assert at == NVEC

            def kpn(w, a, b):
                return w[:, a:b].rearrange("(k p) n -> p k n", p=P)

            def panel_parts(key):
                kind, l = key[0], key[1]
                if kind == "mod":
                    return [(0, DK, kpn(w_mod[l], 512 * key[2], 512 * key[2] + 512))]
                if kind == "cq":
                    return [(0, DK, kpn(w_in[l], OFF_CQ, OFF_CKV))]
                if kind == "ckv":
                    return [(0, DK, kpn(w_in[l], OFF_CKV, OFF_U))]
                if kind == "qs":
                    return [(0, DK, kpn(w_in[l], OFF_QS, OFF_KS))]
                if kind == "ks":
                    return [(0, DK, kpn(w_in[l], OFF_KS, OFF_G))]
                if kind == "u":
                    return [(0, DK, kpn(w_in[l], OFF_U, OFF_QS))]
                if kind == "uq":
                    v = w_mla_uq[l].rearrange("(k p) (h n) -> k p h n", p=P, h=HEADS)
                    return [(512 * k, HEADS, v[k, :, :, 0:NOPE]) for k in range(3)] + \
                        [(1536 + 256 * k, HEADS, v[k, :, :, NOPE:NOPE + ROPE]) for k in range(3)]
                if kind == "ukv":
                    v = w_mla_ukv[l].rearrange("(k p) (h n) -> k p h n", p=P, h=HEADS)
                    return [(1024 * i + 512 * k, HEADS, v[k, :, :, 64 * i:64 * i + 64]) for i in range(2) for k in range(2)]
                if kind == "pm":
                    return [(0, 4, w_pool[l].rearrange("g c d -> c g d"))]
                if kind == "merge":
                    n, b = key[2], key[3]
                    g0 = OFF_G + b * D + 256 * n
                    br = (w_br_mla, w_br_pool, w_br_swa)[b]
                    return [(0, DK, kpn(w_in[l], g0, g0 + 256)), (2048, 4, kpn(br[l], 256 * n, 256 * n + 256))]
                if kind == "wo":
                    return [(0, DK, kpn(w_out[l], 512 * key[2], 512 * key[2] + 512))]
                if kind == "router":
                    return [(0, DK, kpn(w_router[l], 0, E))]
                if kind == "shgu":
                    return [(0, DK, kpn(w_sh_gate[l], 0, DE)), (2048, DK, kpn(w_sh_up[l], 0, DE))]
                return [(0, 2, kpn(w_sh_down[l], 0, D))]

            def load_panel(n):
                key, _ = panels[n]
                if n >= RING:
                    sp.wait_ge(filled, panels[n - RING][1].fill)
                for at, ks, src in panel_parts(key):
                    w = src.shape[2]
                    dst = ring[:, SLOT * (n % RING) + at:SLOT * (n % RING) + at + ks * w]
                    sp.dma_start(dst.rearrange("p (k n) -> p k n", k=ks), src).then_inc(s_panel[n % RING], 16)

            done = [0]

            def load_until(key):
                while done[0] <= panel_no[key]:
                    load_panel(done[0])
                    done[0] += 1

            load_until(("mod", 0, 3))
            for l in range(DEPTH):
                A = active(l)
                sp.dma_start(cs_m, rope_mla).then_inc(s_csm, 16)
                load_until(("uq", l))
                load_until(("ks", l))
                sp.wait_ge(filled, names["yT", l, "m", NT - 1].fill)
                sp.dma_start(cs_s, rope_swa).then_inc(s_css, 16)
                load_until(("wo", l, 1))
                sp.wait_ge(filled, names["b", l, 3, 2, 1].fill)
                if l == 0:
                    sp.dma_start(XT[:, 0:CT, :], ctx[0].rearrange("(t p) d -> p t d", p=P)).then_inc(s_xr, 16)
                    sp.dma_start(XT[:, CT:NT, :], x[0].rearrange("(t p) d -> p t d", p=P)).then_inc(s_xr, 16)
                else:
                    sp.dma_start(XT[:, CT:NT, :], XS[CTX:TOK, :].rearrange("(t p) d -> p t d", p=P)).then_inc(s_xr, 16)
                load_until(("shd", l))
                sl = L[l]
                sp.wait_ge(filled, names["o", l, A[-1]].fill)
                sp.wait_ge(tab_ready, l + 1)
                n_blocks = sp.value_load(tab[0:1, 2 * TABN:2 * TABN + 1], min_val=1, max_val=max_blocks(l))

                def load_gate_up(e, s):
                    for g, w in enumerate((w_exp_gate, w_exp_up)):
                        sp.dma_start(wgu[s][:, g, :, :].rearrange("p k n -> p (k n)"),
                                     w[l][bass.ds(e, 1), :, :].rearrange("e (p k) n -> (e p) (k n)", p=P))\
                            .then_inc(sl[f"wgu{s}"], 16)

                def load_down(e, s):
                    sp.dma_start(wdn[s].rearrange("p c n -> p (c n)"),
                                 w_exp_down[l][bass.ds(e, 1), :, :].rearrange("e (p c) n -> (e p) (c n)", p=P))\
                        .then_inc(sl[f"wdn{s}"], 16)

                def expert(n):
                    return sp.value_load(tab[0:1, bass.ds(n, 1)], min_val=0, max_val=E - 1)

                for n in range(2):
                    load_gate_up(expert(n), n)
                    load_down(expert(n), n)
                sp.wait_ge(sl["gu_done"], 1)
                load_gate_up(expert(2), 0)
                with sp.Fori(0, max_turns(l) // UNROLL) as m:
                    with sp.If(UNROLL * m < n_blocks):
                        for r in range(UNROLL):
                            n, s = UNROLL * m + r + 1, (r + 1) % 2
                            with sp.If(n + 2 < n_blocks):
                                sp.wait_ge(sl["gu_done"], n + 1)
                                load_gate_up(expert(n + 2), s)
                            with sp.If(n + 1 < n_blocks):
                                sp.wait_ge(sl["dn_done"], n)
                                load_down(expert(n + 1), 1 - s)
                loop_end(sp)
                sp.wait_ge(loops_done, 5 * (l + 1))
                if l == DEPTH - 1:
                    sp.dma_start(BC["A2", 0], g_final.partition_broadcast(P)).then_inc(s_gfin, 16)
                for i, t in enumerate(A):
                    g = i + (len(active(0)) if l else 0)
                    if i >= 2:
                        sp.wait_ge(combined, g - 1)
                    for a in range(2):
                        sp.dma_start(comb[i % 2][:, a, :], ACC[a][t * P:t * P + P, :]).then_inc(s_comb[i % 2], 16)
                if l < DEPTH - 1:
                    for i, t in enumerate(A):
                        sp.wait_ge(combined, i + 1)
                        sp.dma_start(XS[t * P:t * P + P, :], XT[:, t, :]).then_inc(s_xs, 16)
                else:
                    for i, t in enumerate(A):
                        sp.wait_ge(fin_ready, i + 1)
                        sp.dma_start(out[0, (t - CT) * P:(t - CT + 1) * P, :], XT[:, t, :]).then_inc(s_out, 16)
                    sp.wait_ge(s_out, 16 * len(A))

        @block.tensor
        def _(pe):
            mm = nc.tensor.matmul

            def panel(key):
                n = panel_no[key]
                per = {"merge": 2, "shgu": 2, "uq": 6, "ukv": 4}
                loads = sum(16 * per.get(panels[i][0][0], 1) for i in range(n % RING, n + 1, RING))
                pe.wait_ge(s_panel[n % RING], loads)
                return ring[:, SLOT * (n % RING):SLOT * (n % RING + 1)]

            def chunks(buf, k, w):
                return buf[:, 0:k * w].rearrange("p (k n) -> p k n", k=k)

            def project(ps, weight, src, everything, rows=P):
                pieces = [(0, 0, TOK // 2), (512, TOK // 2, TOK // 2)] if everything else [(0, CTX, SEQ)]
                for at, tok, n in pieces:
                    for k in range(len(weight)):
                        last = mm(ps[0:rows, at:at + n], weight[k], src[k][:, tok:tok + n],
                                  start=k == 0, stop=k == len(weight) - 1)
                return last

            def turn(ps, tiles):
                for at, t in tiles:
                    last = nc.tensor.transpose(ps[0:t.shape[1], at:at + t.shape[0]], t, ident[0:t.shape[0], 0:t.shape[0]])
                return last

            tiles_done = [0]

            def moe(l, part):
                sl = L[l]
                pe.wait_ge(tab_ready, l + 1)
                n_blocks = pe.value_load(tab[0:1, 2 * TABN:2 * TABN + 1], min_val=1, max_val=max_blocks(l))
                A = active(l)

                def slots_of(n, count):
                    pe.wait_ge(sl["oh_ready"], count)
                    for i, t in enumerate(A):
                        last = mm(m_i, oh[:, n % 2, t, :], tokb[:, 3 * t:3 * t + 3], start=i == 0, stop=i == len(A) - 1)
                    last.then_inc(sl["idx_done"], 1)

                def turn_tokens(s, gathered):
                    pe.wait_ge(sl[f"gat{s}"], gathered)
                    v = xg[:, s, 0:D].rearrange("s (p k) -> s k p", k=DK)
                    turn(m_tr, [(k * P, v[:, k, :]) for k in range(DK)]).then_inc(sl["tr_done"], 1)

                def gate_up(s, turns, n):
                    pe.wait_ge(sl[f"wgu{s}"], 32 * turns)
                    pe.wait_ge(sl["xgT_a"], n + 1)
                    pe.wait_ge(sl["xgT_b"], n + 1)
                    for k in range(DK):
                        last = mm(m_gu[s], xgT[:, s, k, :], wgu[s][:, :, k, :], start=k == 0, stop=k == DK - 1)
                    last.then_inc(sl["gu_done"], 1)

                def turn_hidden(s, n):
                    pe.wait_ge(sl["h_ready"], n + 1)
                    hv = hb[:, s, :].rearrange("s (p c) -> s c p", c=2)
                    turn(m_h, [(cc * P, hv[:, cc, :]) for cc in range(2)]).then_inc(sl["hT_done"], 1)

                if part == "first":
                    slots_of(0, 1)
                    pe.wait_ge(sl["idx_ready"], 1)
                    slots_of(1, 2)
                    return
                turn_tokens(0, 16)
                gate_up(0, 1, 0)
                turn_tokens(1, 16)
                slots_of(2, 3)
                turn_hidden(0, 0)
                with pe.Fori(0, max_turns(l) // UNROLL) as m:
                    with pe.If(UNROLL * m < n_blocks):
                        for r in range(UNROLL):
                            n, s = UNROLL * m + r + 1, (r + 1) % 2
                            half = UNROLL // 2 * m
                            with pe.If(n < n_blocks):
                                gate_up(s, half + (r + 1) // 2 + 1, n)
                                turn_tokens(1 - s, 16 * (half + (r + 2) // 2 + 1))
                                pe.wait_ge(sl["idx_ready"], n + 2)
                                slots_of(r + 1, n + 3)
                            with pe.If(n <= n_blocks):
                                pe.wait_ge(sl[f"wdn{1 - s}"], 16 * (half + r // 2 + 1))
                                pe.wait_ge(sl["hT_ev"], n)
                                pe.wait_ge(sl["y_a"], n)
                                pe.wait_ge(sl["y_b"], n)
                                for side in range(2):
                                    for cc in range(2):
                                        last = mm(m_y[:, 512 * side:512 * side + 512], hTb[:, 1 - s, cc * P:cc * P + P],
                                                  wdn[1 - s][:, cc, 512 * side:512 * side + 512], start=cc == 0, stop=cc == 1)
                                last.then_inc(sl["dn_done"], 1)
                            with pe.If(n < n_blocks):
                                turn_hidden(s, n)

            pe.wait_ge(s_con, 16)
            fills = []
            for job in jobs:
                kind, a = job.kind, job.args
                if job.drain:
                    ps = slot[job.slot]
                    if len(fills) >= 3:
                        pe.wait_ge(drained[fills[-3].drain], fills[-3].count)
                    fills.append(job)
                if kind == "cvec":
                    pe.wait_ge(s_vec, 32)
                    last = turn(ps, [(0, vecs[0:16, :])])
                elif kind == "vec":
                    pe.wait_ge(s_vec, 32 + 96 * (a[0] + 1))
                    last = turn(ps, [(0, vecs[0:NVEC, :])])
                elif kind == "modr":
                    w = chunks(panel(("mod",) + a), DK, 512)
                    after(pe, "cvec")
                    for k in range(DK):
                        j = k % 4
                        last = mm(ps[32 * j:32 * j + 32, 0:512], cTk[:, k, :], w[:, k, :], start=k < 4, stop=k >= 4)
                elif kind == "mod":
                    after(pe, "modr", *a)
                    for j in range(4):
                        last = mm(ps[:, 2 * j:2 * j + 2], modrow(*a)[:, j * P:j * P + P], cst("sel2"), start=True, stop=True)
                elif kind == "h":
                    l, k = a
                    pe.wait_ge(xn_ready, NT * (l + 1))
                    tiles = [((t - CT) * P, t) for t in range(CT, NT)] + [(SEQ + t * P, t) for t in range(CT)]
                    last = turn(ps, [(at, XN[:, t, k * P:k * P + P]) for at, t in tiles])
                elif kind in ("cq", "ckv", "kr", "qs", "ks"):
                    l = a[0]
                    col, width, key = {"cq": (0, 384, "cq"), "ckv": (0, 288, "ckv"), "kr": (256, 288, "ckv"),
                                       "qs": (0, 512, "qs"), "ks": (0, 256, "ks")}[kind]
                    col += P * a[1] if len(a) > 1 else 0
                    w = chunks(panel((key, l)), DK, width)
                    rows = ROPE if kind == "kr" else P
                    after(pe, "h", l, DK - 2)
                    after(pe, "h", l, DK - 1)
                    last = project(ps, [w[:, k, col:col + rows] for k in range(DK)], [hT[:, k, :] for k in range(DK)],
                                   full(l, kind), rows)
                elif kind in ("rq", "rk"):
                    l = a[0]
                    cs = (0, 1, 2) if kind == "rq" else (3, 4)
                    after(pe, *(("cq", l, 2) if kind == "rq" else ("ckv", l, 1)))
                    last = project(ps, [cst("ones") for _ in cs], [sq[:, i, :] for i in cs], full(l, kind) or kind == "rk")
                elif kind == "krp":
                    after(pe, "kr", a[0])
                    last = mm(ps[0:32, 0:SEQ], cst("perm8")[0:32, 0:32], kr[:, CTX:TOK], start=True, stop=True)
                elif kind in ("qr", "qn"):
                    l, j = a
                    pe.wait_ge(cn_ready, 2 * l + 2)
                    w = panel(("uq", l))
                    at, per = (P * j, 512) if kind == "qn" else (1536 + P * j, 256)
                    ws = [w[:, at + per * k:at + per * k + P] for k in range(3)]
                    last = project(ps, ws, [cqT[:, k, :] for k in range(3)], full(l, kind))
                elif kind == "qrp":
                    l, j = a
                    after(pe, "qr", l, j)
                    last = mm(ps[:, 0:SEQ], cst("perm8"), qr[:, j, CTX:TOK], start=True, stop=True)
                elif kind == "kn":
                    l, j = a
                    pe.wait_ge(cn_ready, 2 * l + 1)
                    w = panel(("ukv", l))
                    ws = [w[:, 512 * k + P * j:512 * k + P * j + P] for k in range(2)]
                    last = project(ps, ws, [ckvT[:, k, :] for k in range(2)], True)
                elif kind == "v":
                    l, t = a
                    w = panel(("ukv", l))
                    for k in range(2):
                        last = mm(ps[:, 0:512], ckvT[:, k, t * P:t * P + P], w[:, 1024 + 512 * k:1536 + 512 * k],
                                  start=k == 0, stop=k == 1)
                elif kind == "S":
                    l, br, i = a
                    t, h, _, parts = attn(l, br, i)
                    if i == 0:
                        if br == "m":
                            pe.wait_ge(rope_copied, 3 * (l + 1))
                            for j in range(4):
                                after(pe, "kn", l, j)
                            after(pe, "v", l, NT - 1)
                            after(pe, "v", l, NT - 2)
                            after(pe, "qn", l, 2)
                            after(pe, "qn", l, 3)
                        else:
                            pe.wait_ge(kk_ready, l + 1)
                            after(pe, "vs", l)
                    if br == "m":
                        q = QT[0:96, h, t * P:t * P + P]
                    else:
                        q = QS[64 * (h % 2):64 * (h % 2) + 64, h // 2, t * P:t * P + P]
                    for at, key, n in parts:
                        k = KT[0:96, h, key:key + n] if br == "m" else KK[64 * (h % 2):64 * (h % 2) + 64, h // 4, key:key + n]
                        last = mm(ps[:, at:at + n], q, k, start=True, stop=True)
                elif kind == "T":
                    l, br, i = a
                    if br == "m":
                        after(pe, "S", l, br, i)
                    else:
                        pe.wait_ge(exp_ready, exp_no(l, i))
                    n = len(key_tiles(l, br, i))
                    last = turn(ps, [(j * P, Pb[:, i % 2, j * P:j * P + P]) for j in range(n)])
                elif kind == "PV":
                    l, br, i = a
                    t, h = attn(l, br, i)[:2]
                    g = tiles_done[0]
                    after(pe, "T", l, br, i)
                    if h == 0 and g >= 2:
                        pe.wait_ge(o_drained, g - 1)
                    ks = key_tiles(l, br, i)
                    for j, kt in enumerate(ks):
                        v = V[:, kt, VD * h:VD * h + VD] if br == "m" else VS[:, kt, HD * (h // 4):HD * (h // 4) + HD]
                        last = mm(OB[g % 2][:, VD * h:VD * h + VD], PTb[:, i % 2, j * P:j * P + P], v,
                                  start=j == 0, stop=j == len(ks) - 1)
                    if h == HEADS - 1:
                        last.then_inc(o_full, 1)
                        tiles_done[0] += 1
                elif kind == "yT":
                    l, br, t = a
                    g = tile_no(l, br, t)
                    pe.wait_ge(o_drained, g + 1)
                    last = turn(ps, [(j * P, ytok[:, g % 2, j * P:j * P + P]) for j in range(4)])
                elif kind in ("qsp", "ksp"):
                    l = a[0]
                    after(pe, kind[:2], *a)
                    src = QS[:, a[1], :] if kind == "qsp" else KS
                    last = mm(ps[:, 0:SEQ], cst("perm16"), src[:, CTX:TOK], start=True, stop=True)
                elif kind == "vs":
                    w = chunks(panel(("ks", a[0])), DK, 256)
                    for t in range(NT):
                        for k in range(DK):
                            last = mm(ps[:, t * P:t * P + P], hT[:, k, t * P:t * P + P], w[:, k, SWKV:2 * SWKV],
                                      start=k == 0, stop=k == DK - 1)
                elif kind in ("u", "pm"):
                    l, j = a
                    if kind == "u":
                        w = chunks(panel(("u", l)), DK, 512)
                        ws, xs = [w[:, k, j * P:j * P + P] for k in range(DK)], [hT[:, k, :] for k in range(DK)]
                        at = {0: CTX, 512: 0}
                    else:
                        pe.wait_ge(pooled, 4 * l + j + 1)
                        ws, xs = [chunks(panel(("pm", l)), 4, P)[:, j, :]], [U[:, j, :]]
                        at = {0: UL, 512: UC}
                    for col, n in ((0, SEQ), (512, CTX))[:2 if l < DEPTH - 1 else 1]:
                        for k in range(len(ws)):
                            last = mm(ps[:, col:col + n], ws[k], xs[k][:, at[col]:at[col] + n],
                                      start=k == 0, stop=k == len(ws) - 1)
                elif kind in ("g", "b"):
                    l, n2, b, cc = a
                    buf = panel(("merge", l, n2, b))
                    if kind == "g":
                        w = chunks(buf, DK, 256)
                        ws, xs = [w[:, k, cc * P:cc * P + P] for k in range(DK)], [hT[:, k, :] for k in range(DK)]
                    else:
                        w = chunks(buf[:, 2048:3072], 4, 256)
                        src = (Ym, Yp, Ys)[b]
                        if n2 == 0 and cc == 0:
                            if b == 1:
                                after(pe, "pm", l, 3)
                            else:
                                after(pe, "yT", l, "ms"[b // 2], NT - 1)
                        ws, xs = [w[:, k, cc * P:cc * P + P] for k in range(4)], [src[:, k, :] for k in range(4)]
                    last = project(ps, ws, xs, full(l, kind))
                elif kind == "bc":
                    l, which, s = a
                    pe.wait_ge(setup_dve, 2 * l + 2)
                    for k in range(DK):
                        last = mm(ps[:, k * P:k * P + P], column(l, which, s, k).broadcast_to([P, P]), ident,
                                  start=True, stop=True)
                elif kind == "o":
                    l, t = a
                    for half in range(2):
                        w = chunks(panel(("wo", l, half)), DK, 512)
                        if t == active(l)[0]:
                            after(pe, "b", l, 3, 2, 1)
                        for k in range(DK):
                            last = mm(ps[:, 512 * half:512 * half + 512], MG[:, k, t * P:t * P + P], w[:, k, :],
                                      start=k == 0, stop=k == DK - 1)
                elif kind == "f":
                    l, t = a
                    n = active(l).index(t)
                    pe.wait_ge(f_ready, n + 1 + (NT if l else 0))
                    last = turn(ps, [(k * P, fb[:, n % 2, k * P:k * P + P]) for k in range(DK)])
                elif kind == "r":
                    l, t = a
                    w = chunks(panel(("router", l)), DK, E)
                    after(pe, "f", l, t)
                    for k in range(DK):
                        last = mm(ps[:, 0:E], hT[:, k, t * P:t * P + P], w[:, k, :], start=k == 0, stop=k == DK - 1)
                elif kind == "sg":
                    l, t = a
                    w = panel(("shgu", l)).rearrange("p (g k n) -> p g k n", g=2, k=DK)
                    for k in range(DK):
                        last = mm(ps[:, 0:512], hT[:, k, t * P:t * P + P], w[:, :, k, :], start=k == 0, stop=k == DK - 1)
                elif kind == "sT":
                    l, t = a
                    after(pe, "sg", l, t)
                    n = active(l).index(t)
                    last = turn(ps, [(cc * P, hb[:, n % 2, cc * P:cc * P + P]) for cc in range(2)])
                elif kind == "sd":
                    l, t = a
                    w = chunks(panel(("shd", l)), 2, D)
                    n = active(l).index(t)
                    after(pe, "sT", l, t)
                    for half in range(2):
                        for cc in range(2):
                            last = mm(ps[:, 512 * half:512 * half + 512], hTb[:, n % 2, cc * P:cc * P + P],
                                      w[:, cc, 512 * half:512 * half + 512], start=cc == 0, stop=cc == 1)
                elif kind == "pos":
                    l, t = a
                    A = active(l)
                    pe.wait_ge(w_ready, A.index(t) + 1 + (NT if l else 0))
                    for u in [v for v in A if v <= t]:
                        last = mm(ps[:, 0:E], (trib if u == t else onesb)[:], Mb[:, u * E:u * E + E], start=u == A[0], stop=u == t)
                elif kind == "cnt":
                    A = active(a[0])
                    for u in A:
                        last = mm(ps[0:E, 0:1], Mb[:, u * E:u * E + E], onesb[:, 0:1], start=u == A[0], stop=u == A[-1])
                elif kind == "end":
                    after(pe, "cnt", a[0])
                    last = mm(ps[0:E, 0:1], trib[0:E, 0:E], nbb[0:E, 0:1], start=True, stop=True)
                elif kind == "tab":
                    after(pe, "end", a[0])
                    mm(ps[0:1, 0:TABN], onesb[0:E, 0:1], Gb[0:E, :], start=True, stop=True)
                    mm(ps[0:1, 128:128 + TABN], nbb[0:E, 0:1], Gb[0:E, :], start=True, stop=True)
                    last = mm(ps[0:1, 256:257], nbb[0:E, 0:1], onesb[0:E, 0:1], start=True, stop=True)
                elif kind == "moe":
                    for before in fills[-3:]:
                        pe.wait_ge(drained[before.drain], before.count)
                    moe(a[0], "turns")
                    loop_end(pe)
                elif kind == "first":
                    moe(a[0], "first")
                if job.drain:
                    last.then_inc(filled, 1)

        @block.scalar
        def _(act):
            A_ = nc.scalar.activation

            def copy(o, i):
                return A_(o, i, ACT.Copy)

            def moe(l):
                sl = L[l]
                act.wait_ge(tab_ready, l + 1)
                n_blocks = act.value_load(tab[0:1, 2 * TABN:2 * TABN + 1], min_val=1, max_val=max_blocks(l))

                def tokens(s, count):
                    act.wait_ge(sl["tr_done"], count)
                    copy(xgT[:, s, 0:4, :], m_tr[:, 0:512].rearrange("p (k s) -> p k s", k=4)).then_inc(sl["xgT_a"], 1)

                def silu(s, count):
                    act.wait_ge(sl["gu_done"], count)
                    A_(s1[:, s, :], m_gu[s][:, 0:DE], ACT.Silu).then_inc(sl["silu_done"], 1)

                act.sem_inc(sl["y_a"], 1)
                tokens(0, 1)
                silu(0, 1)
                tokens(1, 2)
                with act.Fori(0, max_turns(l) // UNROLL) as m:
                    with act.If(UNROLL * m < n_blocks):
                        for r in range(UNROLL):
                            n, s = UNROLL * m + r + 1, (r + 1) % 2
                            with act.If(n < n_blocks):
                                silu(s, n + 1)
                                tokens(1 - s, n + 2)
                            with act.If(n <= n_blocks):
                                act.wait_ge(sl["dn_done"], n)
                                act.wait_ge(sl[f"scat{1 - s}"], 16 * (UNROLL // 2 * m + r // 2 + 1))
                                copy(yb[:, 1 - s, 0:512], m_y[:, 0:512]).then_inc(sl["y_a"], 1)

            for job in jobs:
                kind, a, ps = job.kind, job.args, slot[job.slot] if job.drain else None
                mine = job.drain == "act"
                l = a[0] if a else 0
                last = None
                if (kind, a) in (("modr", (0, 0)), ("h", (1, 0))):
                    for t in range(NT):
                        if l == 0:
                            act.wait_ge(s_x, 32)
                        else:
                            act.wait_ge(combined, t + 1)
                        ins = A_(HT[:, t * D:t * D + D], XT[:, t, :], ACT.Square, accum_out=ssq[:, t:t + 1])
                    ins.then_inc(ssq_ready, 1)
                    act.wait_ge(var_ready, norm_no(l, 0))
                    A_(rstd[:, 0:NT], ssq[:, 0:NT], ACT.Sqrt).then_inc(rstd_ready, 1)
                if mine:
                    act.wait_ge(filled, job.fill)
                if kind == "cvec":
                    act.wait_ge(cT_zero, 1)
                    last = A_(cTk[:, :, 0:2].rearrange("p k s -> p s k"), ps[:, 0:16].rearrange("p (s k) -> p s k", s=2), ACT.Silu)
                elif kind == "modr":
                    last = copy(modrow(*a), ps[:, 0:512])
                elif kind == "h" and mine:
                    k = a[1]
                    if k == 0:
                        act.wait_ge(setup_dve, 2 * l + 1)
                    for at, tok, n, s in ((0, CTX, SEQ, 0), (512, 0, CTX, 1)):
                        last = A_(hT[:, k, tok:tok + n], ps[:, at:at + n], ACT.Identity,
                                  scale=column(l, "A1", s, k), bias=column(l, "sh1", s, k))
                elif kind in ("cq", "ckv"):
                    ev = full(l, kind)
                    i = a[1] + (3 if kind == "ckv" else 0)
                    dst = cqT[:, a[1], :] if kind == "cq" else ckvT[:, a[1], :]
                    if l and kind == "ckv" and a[1] == 0:
                        act.wait_ge(s_xs, 16 * NT)
                    copy(sview(dst, ev), pview(ps, ev))
                    last = A_(sview(sq[:, i, :], ev), pview(ps, ev), ACT.Square)
                elif kind == "kr":
                    last = copy(sview(kr, True), pview(ps, True, 32))
                elif kind in ("rq", "rk"):
                    i = int(kind == "rk")
                    act.wait_ge(rms_rec, 2 * l + 2 - i)
                    v = sview(rb[:, i, :], full(l, kind) or i)
                    A_(v, v, ACT.Sqrt).then_inc(rms_sqrt, 1)
                elif kind == "krp":
                    act.wait_ge(roped, roped_no(l, "k"))
                    for h in range(HEADS):
                        ins = copy(KT[64:96, h, :], kr)
                    ins.then_inc(rope_copied, 1)
                elif kind == "qr":
                    ev = full(l, kind)
                    last = A_(sview(qr[:, a[1], :], ev), pview(ps, ev), ACT.Copy, scale=-MLA_SCALE)
                elif kind == "qrp":
                    j = a[1]
                    act.wait_ge(roped, roped_no(l, j))
                    for h in range(4 * j, 4 * j + 4):
                        ins = copy(sview(QT[64:96, h, :], full(l, kind)),
                                   sview(qr[32 * (h % 4):32 * (h % 4) + 32, j, :], full(l, kind)))
                    ins.then_inc(rope_copied, 1)
                elif kind in ("qn", "kn") and mine:
                    T_, ev = (QT, full(l, kind)) if kind == "qn" else (KT, True)
                    for hh in range(2):
                        last = A_(sview(T_[0:64, 2 * a[1] + hh, :], ev), pview(ps[64 * hh:64 * hh + 64, :], ev, 64), ACT.Copy,
                                  scale=-MLA_SCALE if kind == "qn" else 1.0)
                elif kind == "v" and mine:
                    last = copy(V[:, a[1], :], ps[:, 0:512])
                elif kind == "S":
                    _, br, i = a
                    t, h, at, parts = attn(l, br, i)
                    w = sum(n for _, _, n in parts)
                    g = tile_no(l, br, t)
                    if br == "m":
                        act.wait_ge(max_ready, max_no(l, i))
                    else:
                        after(act, "S", l, br, i)
                    if br == "m":
                        last = A_(Pb[:, i % 2, 0:w], ps[:, 0:w], ACT.Exp, scale=-1.0, bias=nb[:, 8 * (g % 2) + h:8 * (g % 2) + h + 1],
                                  accum_out=den[:, 8 * (g % 2) + h:8 * (g % 2) + h + 1])
                    else:
                        A_(Pb[:, i % 2, 0:w], Pb[:, i % 2, 0:w], ACT.Exp, scale=-1.0, bias=nb[:, 8 * (g % 2) + h:8 * (g % 2) + h + 1],
                           accum_out=den[:, 8 * (g % 2) + h:8 * (g % 2) + h + 1]).then_inc(exp_ready, 1)
                        if h == HEADS - 1:
                            act.wait_ge(sink_sum, sink_no(l, t))
                            A_(nb[:, 16 + 8 * (g % 2):24 + 8 * (g % 2)], nb[:, 16 + 8 * (g % 2):24 + 8 * (g % 2)], ACT.Exp)\
                                .then_inc(sink_exp, 1)
                elif kind == "T" and mine:
                    n = P * len(key_tiles(l, a[1], a[2]))
                    last = copy(PTb[:, a[2] % 2, 0:n], ps[:, 0:n])
                elif kind == "yT":
                    t = a[2]
                    last = copy(Y[a[1]][:, :, t * P:t * P + P], ps[:, 0:512].rearrange("p (c n) -> p c n", c=4))
                elif kind == "qs":
                    last = A_(sview(QS[:, a[1], :], full(l, kind)), pview(ps, full(l, kind)), ACT.Copy, scale=-SWA_SCALE)
                elif kind == "ks":
                    last = copy(sview(KS, True), pview(ps, True))
                elif kind == "ksp":
                    act.wait_ge(roped, roped_no(l, "s"))
                    for kv in range(2):
                        for half in range(2):
                            ins = copy(KK[64 * half:64 * half + 64, kv, :], KS[64 * kv:64 * kv + 64, :])
                    ins.then_inc(kk_ready, 1)
                elif kind == "vs":
                    last = copy(VS, ps[:, 0:TOK].rearrange("p (t n) -> p t n", t=NT))
                elif kind == "u":
                    if a[1] == 0:
                        act.wait_ge(u_zero, l + 1)
                    last = copy(U[:, a[1], UL:UL + SEQ], ps[:, 0:SEQ])
                    if l < DEPTH - 1:
                        last = copy(U[:, a[1], UC:UC + CTX], ps[:, 512:512 + CTX])
                elif kind == "g":
                    i = gate_no(*a[1:])
                    if i >= 2:
                        after(act, "b", l, *gate_args(i - 2))
                    ev = full(l, kind)
                    last = A_(sview(SG[:, i % 2, :], ev), pview(ps, ev), ACT.Sigmoid)
                elif kind == "bc":
                    if a[1] == "gt2":
                        after(act, "o", l, active(l)[-1])
                    last = copy(BC[a[1], a[2]], ps)
                elif kind == "o":
                    n = active(l).index(a[1])
                    after(act, "o", l, a[1])
                    A_(junk, XT[:, a[1], :], ACT.Square, accum_out=ssq[:, a[1]:a[1] + 1]).then_inc(ssq_ready, 1)
                    act.wait_ge(var_ready, norm_no(l, n + 1))
                    A_(rstd[:, a[1]:a[1] + 1], ssq[:, a[1]:a[1] + 1], ACT.Sqrt).then_inc(rstd_ready, 1)
                elif kind == "f":
                    last = copy(hT[:, :, a[1] * P:a[1] * P + P], ps.rearrange("p (k n) -> p k n", k=DK))
                elif kind == "r":
                    last = A_(scores[:, a[1] * E:a[1] * E + E], ps[:, 0:E], ACT.Sigmoid)
                elif kind == "sg":
                    n = active(l).index(a[1])
                    act.wait_ge(filled, job.fill)
                    A_(s1[:, n % 2, :], ps[:, 0:DE], ACT.Silu).then_inc(sh_silu, 1)
                elif kind == "sT":
                    n = active(l).index(a[1])
                    last = copy(hTb[:, n % 2, :], ps[:, 0:DE])
                elif kind == "sd":
                    n = active(l).index(a[1])
                    if n >= 2:
                        act.wait_ge(s_sh[n % 2], store_no(l, n) - 16)
                    last = copy(yb[:, n % 2, :], ps)
                elif kind == "moe":
                    moe(l)
                    loop_end(act)
                    if l == DEPTH - 1:
                        for i, t in enumerate(active(l)):
                            act.wait_ge(combined, NT + i + 1)
                            A_(junk, XT[:, t, :], ACT.Square, accum_out=ssq[:, t:t + 1]).then_inc(ssq_ready, 1)
                            act.wait_ge(var_ready, norm_no(l + 1, i))
                            A_(rstd[:, t:t + 1], ssq[:, t:t + 1], ACT.Sqrt).then_inc(rstd_ready, 1)
                if last is not None:
                    last.then_inc(drained["act"], 1)

        @block.vector
        def _(dve):
            vec = nc.vector
            tt, ts, stt = vec.tensor_tensor, vec.tensor_scalar, vec.scalar_tensor_tensor

            def link(ins):
                step("dve", dve, ins)

            def rotate(rows, ps, tables, n_rows=P):
                lat, tmp = rows[:, CTX:TOK], tmpr[0:n_rows, 0:SEQ]
                tt(tmp, ps[0:n_rows, 0:SEQ], tables[0:n_rows, 1, :], ALU.mult)
                ins = tt(lat, lat, tables[0:n_rows, 0, :], ALU.mult)
                link(ins)
                return tt(lat, lat, tmp, ALU.add)

            def inv_mean(out_, in_, n):
                link(ts(out_, in_, 1.0 / n, EPS, ALU.mult, ALU.add))
                return vec.reciprocal(out_, out_)

            def route(l, t):
                sc = scores[:, t * E:t * E + E]
                sel, t1, t2, t3 = (rt[:, i * E:i * E + E] for i in range(4))
                n = active(l).index(t)
                g8 = t1.rearrange("p (g j) -> p g j", g=GROUPS)
                gs, rank, pen, v8 = (rsm[:, 8 * i:8 * i + 8] for i in range(4))
                total, inv = rsm[:, 32:33], rsm[:, 33:34]
                after(dve, "r", l, t)
                link(tt(sel, sc, bias[:, l * E:l * E + E], ALU.add))
                for g in range(GROUPS):
                    ins = vec.max(g8[:, g, :], sel[:, 8 * g:8 * g + 8])
                link(ins)
                link(tt(gs, g8[:, :, 0], g8[:, :, 1], ALU.add))
                gj = gs.unsqueeze(1).broadcast_to([P, GROUPS, GROUPS])
                gi = gs.unsqueeze(2).broadcast_to([P, GROUPS, GROUPS])
                v2, v3 = (v.rearrange("p (g j) -> p g j", g=GROUPS) for v in (t2, t3))
                tt(v2, gj, gi, ALU.is_gt)
                link(tt(v3, gj, gi, ALU.is_equal))
                link(tt(t3, t3, cst("lower"), ALU.mult))
                link(tt(t2, t2, t3, ALU.add))
                link(vec.tensor_reduce(rank, v2, AX.X, ALU.add))
                link(ts(rank, rank, float(KEEP), None, ALU.is_lt))
                link(ts(pen, rank, -NEG, NEG, ALU.mult, ALU.add))
                vs_ = sel.rearrange("p (g j) -> p g j", g=GROUPS)
                link(tt(vs_, vs_, rank.unsqueeze(2).broadcast_to([P, GROUPS, 8]), ALU.mult))
                link(tt(vs_, vs_, pen.unsqueeze(2).broadcast_to([P, GROUPS, 8]), ALU.add))
                link(vec.max(v8, sel))
                link(vec.match_replace(t1, v8, sel, -3e38))
                link(tt(t2, t1, sel, ALU.not_equal))
                vec.tensor_copy(Mb[:, t * E:t * E + E], t2)
                link(tt(t3, sc, t2, ALU.mult))
                link(vec.tensor_reduce(total, t3, AX.X, ALU.add))
                link(vec.reciprocal(inv, total))
                if n >= 2:
                    dve.wait_ge(s_w[n % 2], store_no(l, n) - 16)
                ts(Wt[:, n % 2, :], t3, inv, ROUTED, ALU.mult, ALU.mult).then_inc(w_ready, 1)

            def moe(l, part):
                sl = L[l]
                A = active(l)
                a0 = A[0]
                n_blocks = dve.value_load(tab[0:1, 2 * TABN:2 * TABN + 1], min_val=1, max_val=max_blocks(l))

                def one_hot(n, s):
                    e = dve.value_load(tab[0:1, bass.ds(n, 1)], min_val=0, max_val=E - 1)
                    b = dve.value_load(tab[0:1, bass.ds(n + TABN, 1)], min_val=0, max_val=MAXB - 1)
                    a, _ = CONSTS["slot1"]
                    slots = con[:, bass.ds(a + b * P, P)].unsqueeze(1).broadcast_to([P, len(A), P])
                    rows = posm[:, a0 * E:NT * E].rearrange("p (t e) -> p t e", e=E)[:, :, bass.ds(e, 1)]
                    tt(oh[:, s, a0:NT, :], slots, rows.broadcast_to([P, len(A), P]), ALU.is_equal)\
                        .then_inc(sl["oh_ready"], 1)
                    return e

                def take_index(count, i4):
                    dve.wait_ge(sl["idx_done"], count)
                    vec.tensor_copy(pcol[:], m_i).then_inc(sl["idx_copied"], 1)
                    dve.wait_ge(sl["idx_copied"], count)
                    stt(idxf[:, 0:1], pcol[:, 2:3], cst("negdummy"), pcol[:, 0:1], ALU.mult, ALU.add)\
                        .then_inc(sl["idx_low"], 1)
                    dve.wait_ge(sl["idx_low"], count)
                    stt(idx[:, i4:i4 + 1], idxf[:, 0:1], cst("dummy"), pcol[:, 1:2], ALU.add, ALU.add)\
                        .then_inc(sl["idx_ready"], 1)

                def tokens(s, count):
                    dve.wait_ge(sl["tr_done"], count)
                    vec.tensor_copy(xgT[:, s, 4:8, :], m_tr[:, 512:1024].rearrange("p (k s) -> p k s", k=4))\
                        .then_inc(sl["xgT_b"], 1)

                def hidden(s, n):
                    e = dve.value_load(tab[0:1, bass.ds(n, 1)], min_val=0, max_val=E - 1)
                    dve.wait_ge(sl["silu_done"], n + 1)
                    stt(hb[:, s, :], s1[:, s, :], xg[:, s, bass.ds(e + D, 1)], m_gu[s][:, DE:2 * DE],
                        ALU.mult, ALU.mult).then_inc(sl["h_ready"], 1)

                def turned_hidden(s, n):
                    dve.wait_ge(sl["hT_done"], n + 1)
                    vec.tensor_copy(hTb[:, s, :], m_h).then_inc(sl["hT_ev"], 1)

                if part == "first":
                    one_hot(0, 0)
                    one_hot(1, 1)
                    take_index(1, 0)
                    take_index(2, 1)
                    one_hot(2, 0)
                    return
                dve.sem_inc(sl["y_b"], 1)
                tokens(0, 1)
                hidden(0, 0)
                tokens(1, 2)
                take_index(3, 2)
                turned_hidden(0, 0)
                one_hot(3, 1)
                with dve.Fori(0, max_turns(l) // UNROLL) as m:
                    with dve.If(UNROLL * m < n_blocks):
                        for r in range(UNROLL):
                            n, s = UNROLL * m + r + 1, (r + 1) % 2
                            with dve.If(n < n_blocks):
                                hidden(s, n)
                                tokens(1 - s, n + 2)
                                dve.wait_ge(sl[f"scat{s}"], 16 * (UNROLL // 2 * m + (r + 1) // 2 + 1))
                                take_index(n + 3, (r + 3) % 4)
                            with dve.If(n <= n_blocks):
                                dve.wait_ge(sl["dn_done"], n)
                                dve.wait_ge(sl[f"scat{1 - s}"], 16 * (UNROLL // 2 * m + r // 2 + 1))
                                vec.tensor_copy(yb[:, 1 - s, 512:1024], m_y[:, 512:1024]).then_inc(sl["y_b"], 1)
                            with dve.If(n < n_blocks):
                                turned_hidden(s, n)
                                one_hot(n + 3, 1 - s)

            def combine(l):
                A = active(l)
                dve.wait_ge(loops_done, 5 * (l + 1))
                for i, t in enumerate(A):
                    a = comb[i % 2]
                    per = NT // 2 if l else 0
                    dve.wait_ge(s_comb[i % 2], 32 * (per + i // 2 + 1))
                    link(tt(a[:, 0, :], a[:, 0, :], a[:, 1, :], ALU.add))
                    link(tt(a[:, 0, :], a[:, 0, :], BC["gt2", 0 if t >= CT else 1], ALU.mult))
                    tt(XT[:, t, :], XT[:, t, :], a[:, 0, :], ALU.add).then_inc(combined, 1)
                if l == DEPTH - 1:
                    dve.wait_ge(s_gfin, 16)
                    for i, t in enumerate(A):
                        dve.wait_ge(ssq_ready, norm_no(l + 1, i))
                        inv_mean(ssq[:, t:t + 1], ssq[:, t:t + 1], D).then_inc(var_ready, 1)
                        dve.wait_ge(rstd_ready, norm_no(l + 1, i))
                        stt(XT[:, t, :], XT[:, t, :], rstd[:, t:t + 1], BC["A2", 0], ALU.mult, ALU.mult)\
                            .then_inc(fin_ready, 1)

            vec.memset(cT[:], 0.0).then_inc(cT_zero, 1)
            dve.wait_ge(s_con, 16)
            vec.tensor_copy(onesb[:], cst("ones"))
            vec.tensor_copy(trib[:], cst("tri"))
            vec.tensor_copy(tokb[:], cst("tokid"))
            dve.wait_ge(s_mask, 16)
            dve.wait_ge(sink_neg, 1)
            vec.tensor_copy(masks[:], K[:, 0:MASK + MASK2])
            vec.memset(zero[:], 0.0).then_inc(s_zero, 1)
            for job in jobs:
                kind, a, ps = job.kind, job.args, slot[job.slot] if job.drain else None
                mine = job.drain == "dve"
                l = a[0] if a else 0
                last = None
                if (kind, a) in (("mod", (0, 0)), ("h", (1, 0))):
                    dve.wait_ge(ssq_ready, norm_no(l, 0))
                    inv_mean(ssq[:, 0:NT], ssq[:, 0:NT], D).then_inc(var_ready, 1)
                    dve.wait_ge(rstd_ready, norm_no(l, 0))
                    for t in range(NT):
                        ts(XN[:, t, :], XT[:, t, :], rstd[:, t:t + 1], None, ALU.mult).then_inc(xn_ready, 1)
                if mine:
                    dve.wait_ge(filled, job.fill)
                if kind == "vec":
                    last = vec.tensor_copy(vecT[:, l * NVEC:l * NVEC + NVEC], ps[:, 0:NVEC])
                elif kind == "mod":
                    if a[1] == 0:
                        after(dve, "vec", l)
                    at = l * 96 + 8 * a[1]
                    b4 = vecT[:, l * NVEC + V_B + 4 * a[1]:l * NVEC + V_B + 4 * a[1] + 4]
                    last = tt(modT[:, at:at + 8].rearrange("p (j s) -> p j s", s=2),
                              ps[:, 0:8].rearrange("p (j s) -> p j s", s=2), b4.unsqueeze(2).broadcast_to([P, 4, 2]), ALU.add)
                    if a[1] in (3, 11):
                        last.then_inc(drained["dve"], 1)
                        last = None
                        dve.wait_ge(drained["dve"], job.count)
                        i, g, m = (0, V_GM, 1) if a[1] == 3 else (1, V_GF, 4)
                        gain = vecT[:, l * NVEC + g:l * NVEC + g + DK].unsqueeze(2).broadcast_to([P, DK, 2])
                        ins = stt(AB[:, l * 32 + 16 * i:l * 32 + 16 * i + 16].rearrange("p (k s) -> p k s", s=2),
                                  modT[:, l * 96 + 16 * m:l * 96 + 16 * m + 16].rearrange("p (k s) -> p k s", s=2),
                                  1.0, gain, ALU.add, ALU.mult)
                        ins.then_inc(setup_dve, 1)
                elif kind == "h" and mine:
                    k = a[1]
                    if k == 1:
                        dve.wait_ge(setup_dve, 2 * l + 1)
                    for at, tok, n, s in ((0, CTX, SEQ, 0), (512, 0, CTX, 1)):
                        last = ts(hT[:, k, tok:tok + n], ps[:, at:at + n], column(l, "A1", s, k), column(l, "sh1", s, k),
                                  ALU.mult, ALU.add)
                elif kind in ("rq", "rk"):
                    i = int(kind == "rk")
                    ev = full(l, kind) or bool(i)
                    v = sview(rb[:, i, :], ev)
                    ts(v, pview(ps, ev), 1.0 / (KVL if i else QL), EPS, ALU.mult, ALU.add).then_inc(drained["dve"], 1)
                    dve.wait_ge(drained["dve"], job.count)
                    vec.reciprocal(v, v).then_inc(rms_rec, 1)
                    dve.wait_ge(rms_sqrt, 2 * l + 2 - i)
                    n, buf, g0 = (2, ckvT, V_GKV) if i else (3, cqT, V_GQ)
                    for k in range(n):
                        y = sview(buf[:, k, :], ev)
                        ins = stt(y, y, vecT[:, l * NVEC + g0 + k:l * NVEC + g0 + k + 1], v, ALU.mult, ALU.mult)
                    ins.then_inc(cn_ready, 1)
                elif kind == "krp":
                    dve.wait_ge(s_csm, 16 * (l + 1))
                    rotate(kr, ps, cs_m, 32).then_inc(roped, 1)
                    dve.wait_ge(roped, roped_no(l, "k"))
                elif kind == "qrp":
                    rotate(qr[:, a[1], :], ps, cs_m).then_inc(roped, 1)
                    dve.wait_ge(roped, roped_no(l, a[1]))
                elif kind in ("qsp", "ksp"):
                    if kind == "qsp" and a[1] == 0:
                        dve.wait_ge(s_css, 16 * (l + 1))
                    rotate(QS[:, a[1], :] if kind == "qsp" else KS, ps, cs_s).then_inc(roped, 1)
                    dve.wait_ge(roped, 8 * l + (4 + a[1] if kind == "qsp" else 8))
                elif kind in ("qn", "kn") and mine:
                    T_, ev = (QT, full(l, kind)) if kind == "qn" else (KT, True)
                    for hh in range(2):
                        last = ts(sview(T_[0:64, 2 * a[1] + hh, :], ev), pview(ps[64 * hh:64 * hh + 64, :], ev, 64),
                                  -MLA_SCALE if kind == "qn" else 1.0, None, ALU.mult)
                elif kind == "v" and mine:
                    last = vec.tensor_copy(V[:, a[1], :], ps[:, 0:512])
                elif kind == "S":
                    _, br, i = a
                    t, h, at, parts = attn(l, br, i)
                    w = sum(n for _, _, n in parts)
                    g = tile_no(l, br, t)
                    dve.wait_ge(filled, job.fill)
                    b1 = nb[:, 8 * (g % 2) + h:8 * (g % 2) + h + 1]
                    if br == "m":
                        vec.tensor_reduce(b1, ps[:, 0:w], AX.X, ALU.min).then_inc(max_ready, 1)
                    else:
                        if t < CT:
                            band = masks[:, MASK - CTX:MASK]
                        elif t == NT - 1:
                            band = masks[:, MASK:MASK + MASK2]
                        else:
                            band = masks[:, MASK - w:MASK]
                        ns = sink[:, (2 * l + 1) * HEADS + h:(2 * l + 1) * HEADS + h + 1]
                        vec.tensor_tensor_reduce(Pb[:, i % 2, 0:w], ps[:, at:at + w], band, 1.0, ns, ALU.add, ALU.min,
                                                 b1).then_inc(drained["dve"], 1)
                        if h == HEADS - 1:
                            dve.wait_ge(drained["dve"], job.count)
                            tt(nb[:, 16 + 8 * (g % 2):24 + 8 * (g % 2)], nb[:, 8 * (g % 2):8 * (g % 2) + 8],
                               sink[:, 2 * l * HEADS:(2 * l + 1) * HEADS], ALU.add).then_inc(sink_sum, 1)
                elif kind == "T" and mine:
                    n = P * len(key_tiles(l, a[1], a[2]))
                    last = vec.tensor_copy(PTb[:, a[2] % 2, 0:n], ps[:, 0:n])
                elif kind == "PV" and a[2] % HEADS == HEADS - 1:
                    _, br, i = a
                    t = attn(l, br, i)[0]
                    g = tile_no(l, br, t)
                    dve.wait_ge(o_full, g + 1)
                    d8, r8 = den[:, 8 * (g % 2):8 * (g % 2) + 8], rden[:, 8 * (g % 2):8 * (g % 2) + 8]
                    if br == "s":
                        dve.wait_ge(sink_exp, sink_no(l, t))
                        link(tt(d8, d8, nb[:, 16 + 8 * (g % 2):24 + 8 * (g % 2)], ALU.add))
                    link(vec.reciprocal(r8, d8))
                    tt(ytok[:, g % 2, :].rearrange("p (h n) -> p h n", h=HEADS), OB[g % 2].rearrange("p (h n) -> p h n", h=HEADS),
                       r8.unsqueeze(2).broadcast_to([P, HEADS, VD]), ALU.mult).then_inc(o_drained, 1)
                elif kind == "pm":
                    g = a[1]
                    sc = vecT[:, l * NVEC + V_PS + g:l * NVEC + V_PS + g + 1]
                    last = ts(Yp[:, g, CTX:TOK], ps[:, 0:SEQ], sc, None, ALU.mult)
                    if l < DEPTH - 1:
                        last = ts(Yp[:, g, 0:CTX], ps[:, 512:512 + CTX], sc, None, ALU.mult)
                elif kind == "b":
                    _, n2, b, cc = a
                    i = gate_no(n2, b, cc)
                    after(dve, "g", *a)
                    ev = full(l, kind)
                    gate, mrow = sview(SG[:, i % 2, :], ev), sview(MG[:, 2 * n2 + cc, :], ev)
                    if b == 0:
                        last = tt(mrow, gate, pview(ps, ev), ALU.mult)
                    else:
                        tmp = sview(mtmp[:, i % 2, :], ev)
                        link(tt(tmp, gate, pview(ps, ev), ALU.mult))
                        last = tt(mrow, mrow, tmp, ALU.add)
                elif kind == "o":
                    t = a[1]
                    n = active(l).index(t)
                    s = 0 if t >= CT else 1
                    if n == 0:
                        dve.wait_ge(s_xr, 32 if l == 0 else 48)
                        for which in ("gt1", "A2", "B2"):
                            after(dve, "bc", l, which, 0)
                            if l < DEPTH - 1:
                                after(dve, "bc", l, which, 1)
                    link(tt(otmp, ps, BC["gt1", s], ALU.mult))
                    tt(XT[:, t, :], XT[:, t, :], otmp, ALU.add).then_inc(drained["dve"], 1)
                    dve.wait_ge(ssq_ready, norm_no(l, n + 1))
                    inv_mean(ssq[:, t:t + 1], ssq[:, t:t + 1], D).then_inc(var_ready, 1)
                    dve.wait_ge(rstd_ready, norm_no(l, n + 1))
                    if n >= 2:
                        after(dve, "f", l, active(l)[n - 2])
                        dve.wait_ge(s_h[n % 2], store_no(l, n) - 16)
                    fr = fb[:, n % 2, :]
                    link(stt(fr, XT[:, t, :], rstd[:, t:t + 1], BC["A2", s], ALU.mult, ALU.mult))
                    tt(fr, fr, BC["B2", s], ALU.add).then_inc(f_ready, 1)
                elif kind == "r":
                    if a[1] < NT - 2:
                        route(l, a[1])
                elif kind == "sg":
                    n = active(l).index(a[1])
                    dve.wait_ge(sh_silu, n + 1 + (NT if l else 0))
                    last = tt(hb[:, n % 2, :], s1[:, n % 2, :], ps[:, DE:2 * DE], ALU.mult)
                    last.then_inc(drained["dve"], 1)
                    last = None
                    if n < 2:
                        route(l, NT - 2 + n)
                elif kind == "pos":
                    t = a[1]
                    last = tt(posm[:, t * E:t * E + E], ps[:, 0:E], Mb[:, t * E:t * E + E], ALU.mult)
                elif kind == "cnt":
                    link(vec.tensor_copy(endc[0:E, 0:1], ps[0:E, 0:1]))
                    link(ts(endc[0:E, 1:1 + MAXB], cst("thr", E), endc[0:E, 0:1], None, ALU.is_lt))
                    link(vec.tensor_reduce(endc[0:E, 8:9], endc[0:E, 1:1 + MAXB], AX.X, ALU.add))
                    last = vec.tensor_copy(nbb[0:E, 0:1], endc[0:E, 8:9])
                elif kind == "end":
                    link(vec.tensor_copy(endc[0:E, 9:10], ps[0:E, 0:1]))
                    last = ts(Gb[0:E, :], cst("iotan", E), endc[0:E, 9:10], None, ALU.is_ge)
                elif kind == "tab":
                    ts(tabf[0:1, 0:TABN], ps[0:1, 0:TABN], float(E - 1), None, ALU.min)
                    link(tt(tabf[0:1, TABN:2 * TABN], cst("iotan", 1), ps[0:1, 128:128 + TABN], ALU.subtract))
                    ts(tabf[0:1, TABN:2 * TABN], tabf[0:1, TABN:2 * TABN], float(MAXB - 1), None, ALU.min)
                    link(vec.tensor_copy(tabf[0:1, 2 * TABN:2 * TABN + 1], ps[0:1, 256:257]))
                    last = vec.tensor_copy(tab[0:1, 0:2 * TABN + 1], tabf[0:1, 0:2 * TABN + 1])
                    last.then_inc(drained["dve"], 1)
                    last = None
                    dve.wait_ge(drained["dve"], job.count)
                    dve.sem_inc(tab_ready, 1)
                elif kind == "moe":
                    moe(l, "turns")
                    loop_end(dve)
                    combine(l)
                elif kind == "first":
                    moe(l, "first")
                if last is not None:
                    last.then_inc(drained["dve"], 1)
                elif kind in ("krp", "qrp", "qsp", "ksp"):
                    dve.sem_inc(drained["dve"], 1)

        @block.gpsimd
        def _(pool):
            gp = nc.gpsimd

            turns = s_turns

            def link(ins):
                step("pool", pool, ins)

            for l in range(DEPTH):
                pool.dma_start(bias[:, l * E:l * E + E], router_bias[l].partition_broadcast(P)).then_inc(s_row, 16)
                pool.dma_start(sink[:, 2 * l * HEADS:(2 * l + 1) * HEADS], swa_sink[l].partition_broadcast(P)).then_inc(s_row, 16)
            pool.wait_ge(s_con, 16)
            pool.wait_ge(s_row, 32 * DEPTH)
            for l in range(DEPTH):
                ins = gp.tensor_scalar(sink[:, (2 * l + 1) * HEADS:(2 * l + 2) * HEADS],
                                       sink[:, 2 * l * HEADS:(2 * l + 1) * HEADS], -1.0, None, ALU.mult)
            ins.then_inc(sink_neg, 1)
            pool.wait_ge(s_zero, 1)
            zr = zero[:].unsqueeze(1).broadcast_to([P, 4, 256])
            pool.dma_start(H[TOK:TOK + P, 0:D].rearrange("p (a n) -> p a n", a=4), zr).then_inc(s_hz, 16)
            pool.dma_start(H[TOK:TOK + P, D:HROW], zero[:, 0:E]).then_inc(s_hz, 16)
            pool.wait_ge(s_hz, 32)
            for l in range(DEPTH):
                A, sl = active(l), L[l]
                pool.wait_ge(filled, names["yT", l, "m", NT - 1].fill)
                gp.memset(K[:, 0:4 * UW], 0.0).then_inc(u_zero, 1)
                pool.wait_ge(u_zero, l + 1)
                lo, hi = (0, UW) if l < DEPTH - 1 else (UL - 8, UW)
                for g in range(4):
                    after(pool, "u", l, g)
                    u, bufs = U[:, g, :], [UT[:, 0, :], UT[:, 1, :]]
                    link(gp.tensor_tensor(bufs[0][:, lo + 1:hi], u[:, lo:hi - 1], u[:, lo + 1:hi], ALU.add))
                    src, a, b = 0, lo + 1, hi
                    for d in (1, 2, 4)[:g]:
                        a, b = a + d, b - d
                        link(gp.tensor_tensor(bufs[1 - src][:, a:b], bufs[src][:, a - d:b - d], bufs[src][:, a + d:b + d], ALU.add))
                        src = 1 - src
                    w = bufs[src]
                    link(gp.tensor_scalar(w[:, a:b], w[:, a:b], 1.0 / (2 << g), None, ALU.mult))
                    e0 = CONSTS["edges"][0] + 16 * g
                    edge = con[:, e0:e0 + 16].rearrange("p (a n) -> p a n", a=2)
                    for start, n in ((UL, SEQ), (UC, CTX))[:2 if l < DEPTH - 1 else 1]:
                        for side in range(2):
                            v = w[:, start + side * (n - 8):start + side * (n - 8) + 8]
                            ins = gp.tensor_tensor(v, v, edge[:, side, :], ALU.mult)
                        link(ins)
                    for start, n in ((UL, SEQ), (UC, CTX))[:2 if l < DEPTH - 1 else 1]:
                        ins = gp.tensor_tensor(u[:, start:start + n], w[:, start:start + n], u[:, start:start + n], ALU.subtract)
                    ins.then_inc(pooled, 1)
                    pool.wait_ge(pooled, 4 * l + g + 1)
                for n, t in enumerate(A):
                    pool.wait_ge(f_ready, n + 1 + (NT if l else 0))
                    pool.dma_start(H[t * P:t * P + P, 0:D], fb[:, n % 2, :]).then_inc(s_h[n % 2], 16)
                    pool.dma_start(ACC[1][t * P:t * P + P, :].rearrange("p (a n) -> p a n", a=4), zr).then_inc(s_acc1, 16)
                for n, t in enumerate(A):
                    pool.wait_ge(w_ready, n + 1 + (NT if l else 0))
                    pool.dma_start(H[t * P:t * P + P, D:HROW], Wt[:, n % 2, :]).then_inc(s_w[n % 2], 16)
                for n, t in enumerate(A[:-2]):
                    after(pool, "sd", l, t)
                    pool.dma_start(ACC[0][t * P:t * P + P, :], yb[:, n % 2, :]).then_inc(s_sh[n % 2], 16)
                for s in range(2):
                    for q in (s_h, s_w):
                        pool.wait_ge(q[s], store_no(l, len(A) - 2 + s))

                def gather(s, i4, count):
                    pool.wait_ge(sl["idx_ready"], count)
                    pool.sem_inc(turns, 1)
                    pool.indirect_dma_start(xg[:, s, :], None, H, bass.IndirectOffsetOnAxis(ap=idx[:, i4:i4 + 1], axis=0))\
                        .then_inc(sl[f"gat{s}"], 16)

                def add_block(s, i4, k, before):
                    pool.wait_ge(sl["y_a"], k + 2)
                    pool.wait_ge(sl["y_b"], k + 2)
                    pool.wait_ge(sl[f"scat{s}"], 16 * (before + 1))
                    pool.sem_inc(turns, 1)
                    pool.indirect_dma_start(ACC[s], bass.IndirectOffsetOnAxis(ap=idx[:, i4:i4 + 1], axis=0),
                                            yb[:, s, :], None, compute_op=ALU.add).then_inc(sl[f"scat{s}"], 16)

                for s in range(2):
                    gather(s, s, s + 1)
                for n in (len(A) - 2, len(A) - 1):
                    after(pool, "sd", l, A[n])
                    pool.dma_start(ACC[0][A[n] * P:A[n] * P + P, :], yb[:, n % 2, :]).then_inc(s_sh[n % 2], 16)
                for s in range(2):
                    pool.wait_ge(s_sh[s], store_no(l, len(A) - 2 + s))
                pool.wait_ge(s_acc1, 16 * (NT + (len(A) if l else 0)))
                for s in range(2):
                    pool.dma_start(ACC[s][TOK:TOK + P, :].rearrange("p (a n) -> p a n", a=4), zr).then_inc(sl[f"scat{s}"], 16)
                pool.wait_ge(tab_ready, l + 1)
                n_blocks = pool.value_load(tab[0:1, 2 * TABN:2 * TABN + 1], min_val=1, max_val=max_blocks(l))
                pool.wait_ge(sl["h_ready"], 1)
                gather(0, 2, 3)
                with pool.Fori(0, max_turns(l) // UNROLL) as m:
                    with pool.If(UNROLL * m < n_blocks):
                        for r in range(UNROLL):
                            n, s = UNROLL * m + r + 1, (r + 1) % 2
                            with pool.If(n < n_blocks):
                                pool.wait_ge(sl["h_ready"], n + 1)
                                gather(s, (r + 3) % 4, n + 3)
                            with pool.If(n <= n_blocks):
                                add_block(1 - s, r, n - 1, UNROLL // 2 * m + r // 2)
                pool.wait_ge(sl["scat0"], 16 * ((n_blocks + 1) // 2) + 16)
                pool.wait_ge(sl["scat1"], 16 * (n_blocks // 2) + 16)
                pool.wait_ge(sl["gat0"], 16 * ((n_blocks + 1) // 2) + 16)
                pool.wait_ge(sl["gat1"], 16 * (n_blocks // 2) + 16)
                pool.sem_inc(turns, 1)
                loop_end(pool)


def constants():
    import numpy as np
    con = np.zeros((P, NCONST), np.float32)

    def put(name, v):
        a, b = CONSTS[name]
        con[:, a:b] = v
    i = np.arange(P)
    put("ident", np.eye(P))
    put("ones", 1.0)
    put("perm16", (i[:, None] ^ 16) == i[None, :])
    put("perm8", (i[:, None] ^ 8) == i[None, :])
    put("tri", i[:, None] <= i[None, :])
    put("tokid", np.stack([np.stack([i, np.full(P, P * t), np.ones(P)], 1) for t in range(NT)], 1).reshape(P, -1))
    put("thr", P * np.arange(MAXB))
    put("sel2", i[:, None] % 32 == np.arange(2)[None, :])
    put("iotan", np.arange(TABN))
    put("dummy", (TOK + i)[:, None])
    put("negdummy", -(TOK + i)[:, None])
    edges = np.ones((4, 2, 8))
    for g in range(4):
        w = 2 << g
        for j in range(8):
            edges[g, 0, j] = w / (j + w // 2 - max(j - w // 2, 0))
            edges[g, 1, j] = w / (min(w // 2, 8 - j) + w // 2)
    put("edges", edges.reshape(1, -1))
    put("lower", (np.arange(8)[None, :] < np.arange(8)[:, None]).reshape(1, -1))
    put("slot1", 1 + np.arange(TOK))
    prev = np.where(i[None, :] >= i[:, None], 0.0, -NEG)
    nxt = np.where(i[None, :] <= i[:, None], 0.0, -NEG)
    mask = np.concatenate([prev, np.zeros((P, P)), nxt, np.zeros((P, CTX)), prev, np.zeros((P, 3 * P))], 1)

    def rope(dim):
        n = dim // 4
        t = np.arange(SEQ)
        inv = np.float32(10000.0) ** (-np.arange(n, dtype=np.float32) / np.float32(n))
        table = np.zeros((P, 2, SEQ), np.float32)
        for p in range(P):
            part, f = p % dim // n, p % n
            pos = (t // 64 if part < 2 else t % 64).astype(np.float32)
            ang = pos * inv[f]
            table[p, 0] = np.cos(ang)
            table[p, 1] = np.sin(ang) * (-1 if part % 2 == 0 else 1)
        return table
    return {"consts": con, "mask": mask.astype(np.float32), "rope_mla": rope(ROPE), "rope_swa": rope(HD)}


_INS = ['x', 'c', 'ctx', 'c_ctx', 'w_mod', 'b_mod', 'g_mix', 'g_ffn', 'w_in', 'g_mla_q', 'g_mla_kv', 'w_mla_uq',
        'w_mla_ukv', 'w_pool', 'pool_scale', 'swa_sink', 'w_br_mla', 'w_br_pool', 'w_br_swa', 'w_out', 'w_router',
        'router_bias', 'w_exp_gate', 'w_exp_up', 'w_exp_down', 'w_sh_gate', 'w_sh_up', 'w_sh_down', 'g_final']


def kernel(**inputs):
    import numpy as np
    import concourse.bacc as bacc
    from concourse.bass_utils import run_bass_kernel_spmd
    nc = bacc.Bacc("TRN2", target_bir_lowering=False, num_devices=1)
    arrays, args = {}, []
    for name, a in [(n, inputs[n]) for n in _INS] + list(constants().items()):
        a = np.ascontiguousarray(a)
        arrays[f"in_{name}"] = a
        args.append(nc.dram_tensor(f"in_{name}", a.shape, mybir.dt.from_np(a.dtype), kind="ExternalInput").ap())
    args.append(nc.dram_tensor("out_0", (1, SEQ, D), F32, kind="ExternalOutput").ap())
    build(nc, *args)
    r = run_bass_kernel_spmd(nc, [arrays], core_ids=[0])
    return r.results[0]["out_0"]
```

```python
from contextlib import ExitStack

import concourse.bass as bass
from concourse import mybir

F32, F32R, BF16, I32 = mybir.dt.float32, mybir.dt.float32r, mybir.dt.bfloat16, mybir.dt.int32
ALU, ACT, AX = mybir.AluOpType, mybir.ActivationFunctionType, mybir.AxisListType

P = 128
D, DEPTH, SEQ, CTX = 1024, 2, 512, 256
DK = D // P
TOK = CTX + SEQ
NT, CT = TOK // P, CTX // P
EPS = 1e-6
QL, KVL, ROPE, POOLW, SWQ, SWKV = 384, 256, 32, 512, 512, 128
OFF_CQ, OFF_CKV, OFF_U, OFF_QS, OFF_KS, OFF_G = 0, 384, 672, 1184, 1696, 1952
HEADS, NOPE, VD, HD = 8, 64, 64, 64
MLA_SCALE, SWA_SCALE = (NOPE + ROPE) ** -0.5, HD ** -0.5
PIECES = 20
HALF = [2 + 2 * k for k in range(DK)]
GATE_PANELS = 3 * (D // 256)
E, DE, TOPK, GROUPS, KEEP = 64, 256, 8, 8, 4
ROUTED = 2.5
NEG = -1e30
UW = 800
UC, UL = 8, 8 + CTX + 16
MAXB = TOK // P
TABN = 120
UNROLL = 4
HROW = D + E
RING, SLOT = 3, 4096
NVEC = 73
V_B, V_GM, V_GF, V_PS, V_GQ, V_GKV = 0, 48, 56, 64, 68, 71

CONSTS = {}
_at = 0
for _name, _n in (("ident", 128), ("ones", 128), ("perm16", 128), ("perm8", 128), ("tri", 128), ("tokid", 3 * NT), ("sel2", 2),
                  ("thr", MAXB), ("iotan", TABN), ("dummy", 1), ("negdummy", 1), ("edges", 64), ("lower", 64),
                  ("slot1", TOK)):
    CONSTS[_name] = (_at, _at + _n)
    _at += _n
NCONST = _at
MASK, MASK2 = 640, 512


def active(l):
    return list(range(NT)) if l < DEPTH - 1 else list(range(CT, NT))


def max_blocks(l):
    return (len(active(l)) * P * TOPK + E * (P - 1)) // P


def max_turns(l):
    return -(-max_blocks(l) // UNROLL) * UNROLL


class Job:
    def __init__(self, kind, args, drain, slot, fill, count):
        self.kind, self.args, self.drain, self.slot, self.fill, self.count = kind, args, drain, slot, fill, count


def make_plan():
    jobs, names, panels = [], {}, []
    counts = {"act": 0, "dve": 0}

    def add(kind, *args, drain=None, panel=None):
        if drain is None:
            jobs.append(Job(kind, args, None, None, None, None))
            return
        counts[drain] += 1
        n = counts["act"] + counts["dve"]
        job = Job(kind, args, drain, (n - 1) % 3, n, counts[drain])
        jobs.append(job)
        names[(kind,) + args] = job
        for p in (panel if isinstance(panel, list) else [panel] if panel else []):
            if not panels or all(q[0] != p for q in panels):
                panels.append([p, job])
            for q in panels:
                if q[0] == p:
                    q[1] = job

    def modulation(l, p, *between):
        add("modr", l, p, drain="act", panel=("mod", l, p))
        for kind, args, kw in between:
            add(kind, *args, **kw)
        add("mod", l, p, drain="dve")

    rest = [(0, p) for p in range(4, 12)] + [(l, p) for l in range(1, DEPTH) for p in range(12)]

    def more_modulation(*between):
        if rest:
            modulation(*rest.pop(0), *between)
        else:
            for kind, args, kw in between:
                add(kind, *args, **kw)

    def attention(l, br):
        items = [(t, h) for t in active(l) for h in range(HEADS)]
        late = []
        add("S", l, br, 0, drain="act" if br == "m" else "dve")
        for i in range(len(items) + 2):
            if l == 0 and i in {"m": (3, 10, 17), "s": (16, 32)}[br]:
                more_modulation()
            if i + 1 < len(items):
                add("S", l, br, i + 1, drain="act" if br == "m" else "dve")
            if i < len(items):
                add("T", l, br, i, drain="act" if i % 2 else "dve")
            for t in late:
                add("yT", l, br, t, drain="act")
            late = []
            if 1 <= i <= len(items):
                add("PV", l, br, i - 1)
                if items[i - 1][1] == HEADS - 1:
                    late.append(items[i - 1][0])

    alt = ["act", "dve"]
    add("cvec", drain="act")
    for l in range(DEPTH):
        add("vec", l, drain="dve")
    for p in range(4):
        modulation(0, p)
    for l in range(DEPTH):
        A = active(l)

        for k in range(DK):
            add("h", l, k, drain=alt[k % 2])
        for c in range(2):
            add("ckv", l, c, drain="act", panel=("ckv", l))
        add("kr", l, drain="act", panel=("ckv", l))
        more_modulation(("rk", (l,), dict(drain="dve")))
        add("krp", l, drain="dve")
        for c in range(3):
            add("cq", l, c, drain="act", panel=("cq", l))
        more_modulation(("rq", (l,), dict(drain="dve")))
        for j in range(4):
            add("kn", l, j, drain=alt[j % 2], panel=("ukv", l))
        for t in range(NT):
            add("v", l, t, drain=alt[t % 2], panel=("ukv", l))
        more_modulation()
        for j in range(2):
            add("qr", l, j, drain="act", panel=("uq", l))
            add("qrp", l, j, drain="dve")
        for j in range(4):
            add("qn", l, j, drain=alt[j % 2], panel=("uq", l))
        attention(l, "m")
        add("ks", l, drain="act", panel=("ks", l))
        add("vs", l, drain="act", panel=("ks", l))
        add("ksp", l, drain="dve")
        for c in range(4):
            add("qs", l, c, drain="act", panel=[("qs", l), ("qs_high", l)])
            if c:
                add("qsp", l, c - 1, drain="dve")
        add("u", l, 0, drain="act", panel=("u", l))
        add("qsp", l, 3, drain="dve")
        for c in range(1, 4):
            add("u", l, c, drain="act", panel=("u", l))
        attention(l, "s")
        for g in range(4):
            add("pm", l, g, drain="dve", panel=("pm", l))
        for b in range(3):
            for n2 in range(DK // 2):
                jobs4 = [(k, (l, n2, b, c), dict(drain=e, panel=("merge", l, n2, b)))
                         for c in range(2) for k, e in (("g", "act"), ("b", "dve"))]
                if n2 == 0:
                    jobs4 = [jobs4[i] for i in ((0, 2, 1, 3) if b else (1, 0, 3, 2))]
                add(jobs4[0][0], *jobs4[0][1], **jobs4[0][2])
                more_modulation(*jobs4[1:3])
                add(jobs4[3][0], *jobs4[3][1], **jobs4[3][2])
        assert not rest
        streams = (0, 1) if l < DEPTH - 1 else (0,)
        for which in ("gt1", "A2", "B2"):
            for s in streams:
                add("bc", l, which, s, drain="act")
        for i, t in enumerate(A):
            add("o", l, t, drain="dve", panel=[("wo", l, 0), ("wo", l, 1)])
            if i:
                add("f", l, A[i - 1], drain="act")
        for s in streams:
            add("bc", l, "gt2", s, drain="act")
        add("f", l, A[-1], drain="act")
        for t in A:
            add("r", l, t, drain="act", panel=("router", l))
        for i, t in enumerate(A):
            if i == len(A) - 1:
                for u in A:
                    add("pos", l, u, drain="dve")
                add("cnt", l, drain="dve")
                add("end", l, drain="dve")
                add("tab", l, drain="dve")
                add("first", l)
            add("sg", l, t, drain="dve", panel=("shgu", l))
            for u in A[i - 1:i] + (A[-1:] if i == len(A) - 1 else []):
                add("sT", l, u, drain="act")
                add("sd", l, u, drain="act", panel=("shd", l))
        add("moe", l)
    return jobs, names, panels


def build(nc, x, c, ctx, c_ctx, w_mod, b_mod, g_mix, g_ffn, w_in, g_mla_q, g_mla_kv, w_mla_uq, w_mla_ukv, w_pool,
          pool_scale, swa_sink, w_br_mla, w_br_pool, w_br_swa, w_out, w_router, router_bias, w_exp_gate, w_exp_up,
          w_exp_down, w_sh_gate, w_sh_up, w_sh_down, g_final, consts, mask, rope_mla, rope_swa, out):
    H = nc.dram_tensor("h_rows", [TOK + P, HROW], F32, kind="Internal").ap()
    ACC = [nc.dram_tensor(f"acc{i}", [TOK + P, D], F32, kind="Internal").ap() for i in range(2)]
    XS = nc.dram_tensor("x_saved", [TOK, D], F32, kind="Internal").ap()
    jobs, names, panels = make_plan()
    panel_no = {p[0]: n for n, p in enumerate(panels)}

    with ExitStack() as stack:
        def sb(name, n, dt=F32, rows=P):
            return stack.enter_context(nc.sbuf_tensor(name, [rows, n], dt))

        def sem(name):
            return stack.enter_context(nc.semaphore(name))

        start = {}

        def region(name, n):
            t = sb(name, n)
            start[name] = nc.sbuf_base - 4 * n
            return t

        XA = region("region_x", 6144)
        HT = region("region_h", 6144)
        Q = region("region_q", 6144)
        K = region("region_k", 6144)
        VY = region("region_v", 6144)
        C = region("region_c", 4608)
        ring = region("ring", RING * SLOT)
        con = sb("con", NCONST)
        masks = sb("masks", MASK + MASK2, BF16)

        def cst(name, rows=P):
            a, b = CONSTS[name]
            return con[0:rows, a:b]
        ident = cst("ident")
        vecs = sb("vecs", P)
        cT = sb("cT", DK * 32)
        cTk = cT[:].rearrange("p (k m) -> p k m", k=DK)
        vecT = sb("vecT", DEPTH * NVEC)
        modT = sb("modT", DEPTH * 96)
        AB = sb("AB", DEPTH * 32)
        ssq, rstd = sb("ssq", 8), sb("rstd", 8)
        zero = sb("zero", 256)
        scores = sb("scores", NT * E)
        posm = sb("posm", NT * E)
        rt = sb("rt", 6 * E)
        rsm = sb("rsm", 64)
        Mb = sb("Mb", NT * E, BF16)
        onesb, trib, tokb = sb("onesb", P, BF16), sb("trib", P, BF16), sb("tokb", 3 * NT, BF16)
        nbb, Gb = sb("nbb", 2, BF16), sb("Gb", TABN, BF16)
        endc = sb("endc", 16)
        tab = sb("tab", 2 * TABN + 8, I32, 1)
        idx = sb("idx", 4, I32)
        idxf = sb("idxf", 2)
        pcol = sb("pcol", 3)
        bias = sb("bias", DEPTH * E)
        sink = sb("sink", 2 * DEPTH * HEADS)
        nb = sb("nb", 32)
        den, rden = sb("den", 16), sb("rden", 16)

        def split_view(name, n):
            return nc.alloc_sbuf_tensor_at(f"{name}_split", [P, n], F32R, offset=start[name])[:]

        XA_r, Q_r, HT_r, VY_r, C_r, ring_r = (split_view(*v) for v in (
            ("region_x", 6144), ("region_q", 6144), ("region_h", 6144), ("region_v", 6144), ("region_c", 4608),
            ("ring", RING * SLOT)))
        h_hi = XA_r.rearrange("p (k n) -> p k n", k=DK)
        h_lo = HT_r.rearrange("p (k n) -> p k n", k=DK)

        y_hi, y_lo = ({b: v.rearrange("p (c n) -> p c n", c=4) for b, v in parts.items()} for parts in (
            {1: VY_r[:, 3072:6144], 2: Q_r[:, 0:3072]}, {1: Q_r[:, 0:3072], 2: VY_r[:, 0:3072]}))

        def gate_weights(n):
            if n % 2 == 0:
                return [(0, Q_r[:, 3072:5120])]
            return [(0, Q_r[:, 5120:6144]), (4, C_r[:, 3072:4096])]

        XT = XA[:].rearrange("p (t d) -> p t d", t=NT)
        hT = HT[:].rearrange("p (k n) -> p k n", k=DK)
        layer_vecs = [K[:, P * l:P * l + P] for l in range(DEPTH)]
        mask_in = K[:, P * DEPTH:P * DEPTH + MASK + MASK2]
        cqT = C[:, 0:2304].rearrange("p (c n) -> p c n", c=3)
        ckvT = C[:, 2304:3840].rearrange("p (c n) -> p c n", c=2)
        tmp_rope = {"m": C[:, 3840:4352], "s": C[:, 0:512]}

        def modrow(l, p):
            return VY[:, 4096:4608] if (l, p) < (0, 7) else C[:, 4096:4608]
        XN = Q[:].rearrange("p (t d) -> p t d", t=NT)
        sq = XA[:, 0:3840].rearrange("p (c n) -> p c n", c=5)
        qr = XA[:, 3840:5376].rearrange("p (c n) -> p c n", c=2)
        kr = XA[0:32, 5376:6144]
        rb = Q[:, 0:1536].rearrange("p (c n) -> p c n", c=2)
        QT = Q[:].rearrange("p (h n) -> p h n", h=HEADS)
        KT = K[:].rearrange("p (h n) -> p h n", h=HEADS)
        V = VY[:, 0:3072].rearrange("p (t n) -> p t n", t=NT)
        Ym = VY[:, 3072:6144].rearrange("p (c n) -> p c n", c=4)
        cs_m = VY[:, 3072:4096].rearrange("p (a n) -> p a n", a=2)
        cs_s = VY[:, 0:1024].rearrange("p (a n) -> p a n", a=2)
        Ys = VY[:, 0:3072].rearrange("p (c n) -> p c n", c=4)
        Yp = Q[:, 0:3072].rearrange("p (c n) -> p c n", c=4)
        Y = {"m": Ym, "s": Ys}
        Pb = C[:, 0:1536].rearrange("p (a n) -> p a n", a=2)
        PTb = C[:, 1536:3072].rearrange("p (a n) -> p a n", a=2)
        ytok = C[:, 3072:4096].rearrange("p (a n) -> p a n", a=2)
        QS = Q[:, 0:3072].rearrange("p (c n) -> p c n", c=4)
        KK = Q[:, 3072:4608].rearrange("p (c n) -> p c n", c=2)
        VS = Q[:, 4608:5376].rearrange("p (t n) -> p t n", t=NT)
        KS = Q[:, 5376:6144]
        U = K[:, 0:4 * UW].rearrange("p (c n) -> p c n", c=4)
        UT = K[:, 4 * UW:6 * UW].rearrange("p (c n) -> p c n", c=2)
        MG = K[:].rearrange("p (k n) -> p k n", k=DK)
        SG = C[:, 0:1536].rearrange("p (a n) -> p a n", a=2)
        mtmp = C[:, 1536:3072].rearrange("p (a n) -> p a n", a=2)
        BC = {("A2", 0): Q[:, 0:1024], ("A2", 1): Q[:, 1024:2048], ("B2", 0): Q[:, 2048:3072],
              ("B2", 1): Q[:, 3072:4096], ("gt1", 0): Q[:, 4096:5120], ("gt1", 1): Q[:, 5120:6144]}
        BC["gt2", 0], BC["gt2", 1] = BC["gt1", 0], BC["gt1", 1]
        fb = C[:, 0:2048].rearrange("p (a n) -> p a n", a=2)
        junk = C[:, 2048:3072]
        otmp = C[:, 3072:4096]
        Wt = rt[:, 4 * E:6 * E].rearrange("p (a n) -> p a n", a=2)
        tabf = rt[0:1, 0:2 * TABN + 8]
        xg = C[:, 0:2 * HROW].rearrange("p (a n) -> p a n", a=2)
        s1 = C[:, 2176:2688].rearrange("p (a n) -> p a n", a=2)
        hb = C[:, 2688:3200].rearrange("p (a n) -> p a n", a=2)
        hTb = C[:, 3200:3712].rearrange("p (a n) -> p a n", a=2)
        oh = C[:, 3712:4480].bitcast(BF16).rearrange("p (a t s) -> p a t s", a=2, t=NT)
        xgT = Q[:, 0:2048].rearrange("p (a k s) -> p a k s", a=2, k=DK)
        yb = Q[:, 2048:4096].rearrange("p (a n) -> p a n", a=2)
        WSL = [K, VY]
        wgu = [w[:, 0:4096].rearrange("p (g k n) -> p g k n", g=2, k=DK) for w in WSL]
        wdn = [w[:, 4096:6144].rearrange("p (c n) -> p c n", c=2) for w in WSL]
        comb = [w[:, 2048 * i:2048 * i + 2048].rearrange("p (a n) -> p a n", a=2) for w in WSL for i in range(3)]

        PS = stack.enter_context(nc.psum_tensor("ps", [P, 4096], F32))
        slot = [PS[:, 1024 * i:1024 * i + 1024] for i in range(3)]
        OB = [PS[:, 3072:3584], PS[:, 3584:4096]]
        m_gu = [PS[:, 0:512], PS[:, 512:1024]]
        m_tr, m_y = PS[:, 1024:2048], PS[:, 2048:3072]
        m_h, m_i = PS[:, 3072:3328], PS[:, 3584:3587]

        s_con, s_vec, s_mask = sem("s_con"), sem("s_vec"), sem("s_mask")
        s_vecs = [sem(f"s_vecs{l}") for l in range(DEPTH)]
        s_panel = [sem(f"s_panel{i}") for i in range(RING)]
        filled = sem("filled")
        drained = {"act": sem("drained_act"), "dve": sem("drained_dve")}
        s_x, s_xs, s_xr = sem("s_x"), sem("s_xs"), sem("s_xr")
        s_csm, s_css = sem("s_csm"), sem("s_css")
        ssq_ready, var_ready, rstd_ready, xn_ready = sem("ssq_ready"), sem("var_ready"), sem("rstd_ready"), sem("xn_ready")
        pre_ssq, pre_var, pre_rstd, summed = sem("pre_ssq"), sem("pre_var"), sem("pre_rstd"), sem("summed")
        rms_rec, rms_sqrt, cn_ready = sem("rms_rec"), sem("rms_sqrt"), sem("cn_ready")
        roped, rope_copied = sem("roped"), sem("rope_copied")
        max_ready, exp_ready, o_full, o_drained = sem("max_ready"), sem("exp_ready"), sem("o_full"), sem("o_drained")
        sink_sum, sink_exp = sem("sink_sum"), sem("sink_exp")
        h_high, h_low, w_high, w_low = sem("h_high"), sem("h_low"), sem("w_high"), sem("w_low")
        y_high, y_low = sem("y_high"), sem("y_low")
        piece_high, piece_low = sem("piece_high"), sem("piece_low")
        kk_ready, u_zero, pooled = sem("kk_ready"), sem("u_zero"), sem("pooled")
        f_ready, s_h = sem("f_ready"), [sem("s_h0"), sem("s_h1")]
        w_ready, s_w = sem("w_ready"), [sem("s_w0"), sem("s_w1")]
        sh_silu, s_sh = sem("sh_silu"), [sem("s_sh0"), sem("s_sh1")]
        setup_dve, s_zero, tab_ready = sem("setup_dve"), sem("s_zero"), sem("tab_ready")
        s_turns = sem("s_turns")
        cT_zero = sem("cT_zero")
        s_row, s_hz, s_acc1, sink_neg = sem("s_row"), sem("s_hz"), sem("s_acc1"), sem("sink_neg")
        s_comb, combined, s_out = [sem(f"s_comb{i}") for i in range(NT)], sem("combined"), sem("s_out")
        s_gfin, fin_ready = sem("s_gfin"), sem("fin_ready")
        loops_done, layer_done = sem("loops_done"), sem("layer_done")
        L = [{n: sem(f"{n}_{l}") for n in ("wgu0", "wgu1", "wdn0", "wdn1", "gu_done", "tr_done", "hT_done", "idx_done",
                                             "dn_done", "silu_done", "h_ready", "xgT_a", "xgT_b", "hT_ev", "idx_ready",
                                             "oh_ready", "y_a", "y_b", "gat0", "gat1", "scat0", "scat1", "idx_copied", "idx_low")}
             for l in range(DEPTH)]
        chain = {e: [sem(f"chain_{e}"), 0] for e in ("act", "dve", "pool")}

        def step(e, eng, ins):
            chain[e][1] += 1
            ins.then_inc(chain[e][0], 1)
            eng.wait_ge(chain[e][0], chain[e][1])

        def after(eng, *name):
            j = names[name]
            eng.wait_ge(drained[j.drain], j.count)

        def full(l, kind):
            return l < DEPTH - 1 or kind in ("ckv", "kr", "ks")

        def pview(ps, everything, rows=P):
            return ps[0:rows, :].rearrange("p (b n) -> p b n", b=2)[:, :, 0:TOK // 2] if everything else ps[0:rows, 0:SEQ]

        def sview(buf, everything):
            return buf.rearrange("p (b n) -> p b n", b=2) if everything else buf[:, CTX:TOK]

        def attn(l, br, i):
            t, h = active(l)[i // HEADS], i % HEADS
            if br == "m":
                return t, h, 0, [(0, 0, 512), (512, 512, 256)] if t >= CT else [(0, 0, CTX)]
            if t < CT:
                return t, h, 512, [(512, 0, CTX)]
            a, b = max(CT, t - 1), min(NT - 1, t + 1)
            n = (b - a + 1) * P
            return t, h, 512 - n, [(512 - n, a * P, n), (512, 0, CTX)]

        def key_tiles(l, br, i):
            return [k // P + j for _, k, n in attn(l, br, i)[3] for j in range(n // P)]

        def exp_no(l, i):
            return (HEADS * NT if l else 0) + i + 1

        def tile_no(l, br, t):
            return (2 * NT if l else 0) + (len(active(l)) if br == "s" else 0) + active(l).index(t)

        def column(l, which, s, k):
            if which in ("A1", "A2"):
                at = l * 32 + (16 if which == "A2" else 0) + 2 * k + s
                return AB[:, at:at + 1]
            at = l * 96 + 2 * (8 * {"sh1": 0, "gt1": 2, "B2": 3, "gt2": 5}[which] + k) + s
            return modT[:, at:at + 1]

        def norm_no(l, i):
            return [0, NT, 1 + NT + len(active(1))][l] + i + 1

        def roped_no(l, what):
            return 8 * l + {"k": 1, 0: 2, 1: 3, "s": 4}[what]

        def max_no(l, i):
            return (HEADS * NT if l else 0) + i + 1

        def sink_no(l, t):
            return (NT if l else 0) + active(l).index(t) + 1

        def loaded(eng, key):
            n = panel_no[key]
            per = {"merge": 2, "shgu": 2, "uq": 6, "ukv": 4, "qs_high": 0}
            loads = sum(16 * per.get(panels[i][0][0], 1) for i in range(n % RING, n + 1, RING))
            eng.wait_ge(s_panel[n % RING], loads)
            return SLOT * (n % RING)

        def split_piece(l, i):
            if i < 4:
                key, at = ("ks", l), 512 * i
            else:
                key, at = (("qs", l), 512 * (i - 4)) if i < 12 else (("u", l), 512 * (i - 12))
            at += SLOT * (panel_no[key] % RING)
            if i < 4:
                high = ring_r[:, at + 2048:at + 2560]
            elif i < 12:
                h0 = SLOT * (panel_no["qs_high", l] % RING) + 512 * (i - 4)
                high = ring_r[:, h0:h0 + 512]
            else:
                k = i - 12
                high = C_r[:, 512 + 512 * k:1024 + 512 * k] if k < 4 else VY_r[:, 512 * k - 1024:512 * k - 512]
            return key, at, high

        def split_now(kind, a):
            if kind == "S" and a[1] == "m" and 18 <= a[2] < 30:
                return [a[2] - 18]
            if kind in ("qs", "qsp"):
                return {1: [12, 13, 14, 15], 2: [16, 17, 18, 19]}.get(a[1], [])
            return []

        def gate_panel(l, n2, b):
            return DK // 2 * b + n2

        def gate_key(l, i):
            return "merge", l, i % (DK // 2), i // (DK // 2)

        def gate_no(n2, b, cc):
            return DK * b + 2 * n2 + cc

        def gate_args(i):
            return i % DK // 2, i // DK, i % 2

        def store_no(l, n):
            return 16 * ((NT // 2 if l else 0) + n // 2 + 1)

        block = stack.enter_context(nc.Block())

        def loop_end(eng):
            eng.drain().then_inc(loops_done, 1)

        @block.sync
        def _(sp):
            sp.dma_start(con[:], consts).then_inc(s_con, 16)
            sp.dma_start(vecs[0:8, :], c.rearrange("a (k p) -> (a k) p", p=P)).then_inc(s_vec, 16)
            sp.dma_start(vecs[8:16, :], c_ctx.rearrange("(k p) -> k p", p=P)).then_inc(s_vec, 16)
            def load_vectors(l):
                at = 0
                for v in (b_mod, g_mix, g_ffn, pool_scale, g_mla_q, g_mla_kv):
                    rows = v.shape[1] // P
                    sp.dma_start(layer_vecs[l][at:at + rows, :], v[l].rearrange("(k p) -> k p", p=P)).then_inc(s_vecs[l], 16)
                    at += rows
                assert at == NVEC

            load_vectors(0)
            sp.dma_start(XT[:, 0:CT, :], ctx[0].rearrange("(t p) d -> p t d", p=P)).then_inc(s_x, 16)
            sp.dma_start(XT[:, CT:NT, :], x[0].rearrange("(t p) d -> p t d", p=P)).then_inc(s_x, 16)
            def kpn(w, a, b):
                return w[:, a:b].rearrange("(k p) n -> p k n", p=P)

            def panel_parts(key):
                kind, l = key[0], key[1]
                if kind == "qs_high":
                    return []
                if kind == "mod":
                    return [(0, DK, kpn(w_mod[l], 512 * key[2], 512 * key[2] + 512))]
                if kind == "cq":
                    return [(0, DK, kpn(w_in[l], OFF_CQ, OFF_CKV))]
                if kind == "ckv":
                    return [(0, DK, kpn(w_in[l], OFF_CKV, OFF_U))]
                if kind == "qs":
                    return [(0, DK, kpn(w_in[l], OFF_QS, OFF_KS))]
                if kind == "ks":
                    return [(0, DK, kpn(w_in[l], OFF_KS, OFF_G))]
                if kind == "u":
                    return [(0, DK, kpn(w_in[l], OFF_U, OFF_QS))]
                if kind == "uq":
                    v = w_mla_uq[l].rearrange("(k p) (h n) -> k p h n", p=P, h=HEADS)
                    return [(512 * k, HEADS, v[k, :, :, 0:NOPE]) for k in range(3)] + \
                        [(1536 + 256 * k, HEADS, v[k, :, :, NOPE:NOPE + ROPE]) for k in range(3)]
                if kind == "ukv":
                    v = w_mla_ukv[l].rearrange("(k p) (h n) -> k p h n", p=P, h=HEADS)
                    return [(1024 * i + 512 * k, HEADS, v[k, :, :, 64 * i:64 * i + 64]) for i in range(2) for k in range(2)]
                if kind == "pm":
                    return [(0, 4, w_pool[l].rearrange("g c d -> c g d"))]
                if kind == "merge":
                    n, b = key[2], key[3]
                    g0 = OFF_G + b * D + 256 * n
                    br = (w_br_mla, w_br_pool, w_br_swa)[b]
                    return [(0, DK, kpn(w_in[l], g0, g0 + 256)), (2048, 4, kpn(br[l], 256 * n, 256 * n + 256))]
                if kind == "wo":
                    return [(0, DK, kpn(w_out[l], 512 * key[2], 512 * key[2] + 512))]
                if kind == "router":
                    return [(0, DK, kpn(w_router[l], 0, E))]
                if kind == "shgu":
                    return [(0, DK, kpn(w_sh_gate[l], 0, DE)), (2048, DK, kpn(w_sh_up[l], 0, DE))]
                return [(0, 2, kpn(w_sh_down[l], 0, D))]

            def load_panel(n):
                key, _ = panels[n]
                if n >= RING:
                    sp.wait_ge(filled, panels[n - RING][1].fill)
                for at, ks, src in panel_parts(key):
                    w = src.shape[2]
                    dst = ring[:, SLOT * (n % RING) + at:SLOT * (n % RING) + at + ks * w]
                    sp.dma_start(dst.rearrange("p (k n) -> p k n", k=ks), src).then_inc(s_panel[n % RING], 16)

            done = [0]

            def load_until(key):
                while done[0] <= panel_no[key]:
                    load_panel(done[0])
                    done[0] += 1

            load_until(("mod", 0, 0))
            for l in range(1, DEPTH):
                load_vectors(l)
            load_until(("mod", 0, 3))
            sp.dma_start(mask_in, mask).then_inc(s_mask, 16)
            for l in range(DEPTH):
                A = active(l)
                sp.dma_start(cs_m, rope_mla).then_inc(s_csm, 16)
                load_until(("uq", l))
                load_until(("qs", l))
                sp.wait_ge(filled, names["yT", l, "m", NT - 1].fill)
                sp.dma_start(cs_s, rope_swa).then_inc(s_css, 16)
                load_until(("wo", l, 1))
                sp.wait_ge(filled, names["b", l, 3, 2, 1].fill)
                if l == 0:
                    sp.dma_start(XT[:, 0:CT, :], ctx[0].rearrange("(t p) d -> p t d", p=P)).then_inc(s_xr, 16)
                    sp.dma_start(XT[:, CT:NT, :], x[0].rearrange("(t p) d -> p t d", p=P)).then_inc(s_xr, 16)
                else:
                    sp.dma_start(XT[:, CT:NT, :], XS[CTX:TOK, :].rearrange("(t p) d -> p t d", p=P)).then_inc(s_xr, 16)
                load_until(("shd", l))
                sl = L[l]
                sp.wait_ge(filled, names["o", l, A[-1]].fill)
                sp.wait_ge(tab_ready, l + 1)
                n_blocks = sp.value_load(tab[0:1, 2 * TABN:2 * TABN + 1], min_val=1, max_val=max_blocks(l))

                def load_gate_up(e, s):
                    for g, w in enumerate((w_exp_gate, w_exp_up)):
                        sp.dma_start(wgu[s][:, g, :, :].rearrange("p k n -> p (k n)"),
                                     w[l][bass.ds(e, 1), :, :].rearrange("e (p k) n -> (e p) (k n)", p=P))\
                            .then_inc(sl[f"wgu{s}"], 16)

                def load_down(e, s):
                    sp.dma_start(wdn[s].rearrange("p c n -> p (c n)"),
                                 w_exp_down[l][bass.ds(e, 1), :, :].rearrange("e (p c) n -> (e p) (c n)", p=P))\
                        .then_inc(sl[f"wdn{s}"], 16)

                def expert(n):
                    return sp.value_load(tab[0:1, bass.ds(n, 1)], min_val=0, max_val=E - 1)

                for n in range(2):
                    load_gate_up(expert(n), n)
                    load_down(expert(n), n)
                sp.wait_ge(sl["gu_done"], 1)
                load_gate_up(expert(2), 0)
                with sp.Fori(0, max_turns(l) // UNROLL) as m:
                    with sp.If(UNROLL * m < n_blocks):
                        for r in range(UNROLL):
                            n, s = UNROLL * m + r + 1, (r + 1) % 2
                            with sp.If(n + 2 < n_blocks):
                                sp.wait_ge(sl["gu_done"], n + 1)
                                load_gate_up(expert(n + 2), s)
                            with sp.If(n + 1 < n_blocks):
                                sp.wait_ge(sl["dn_done"], n)
                                load_down(expert(n + 1), 1 - s)
                loop_end(sp)
                sp.wait_ge(loops_done, 5 * (l + 1))
                if l == DEPTH - 1:
                    sp.dma_start(BC["A2", 0], g_final.partition_broadcast(P)).then_inc(s_gfin, 16)
                for i, t in enumerate(A):
                    for a in range(2):
                        sp.dma_start(comb[i][:, a, :], ACC[a][t * P:t * P + P, :]).then_inc(s_comb[i], 16)
                if l < DEPTH - 1:
                    for i, t in enumerate(A):
                        sp.wait_ge(combined, i + 1)
                        sp.dma_start(XS[t * P:t * P + P, :], XT[:, t, :]).then_inc(s_xs, 16)
                else:
                    for i, t in enumerate(A):
                        sp.wait_ge(fin_ready, i + 1)
                        sp.dma_start(out[0, (t - CT) * P:(t - CT + 1) * P, :], XT[:, t, :]).then_inc(s_out, 16)
                    sp.wait_ge(s_out, 16 * len(A))

        @block.tensor
        def _(pe):
            mm = nc.tensor.matmul

            def panel(key):
                at = loaded(pe, key)
                return ring[:, at:at + SLOT]

            def chunks(buf, k, w):
                return buf[:, 0:k * w].rearrange("p (k n) -> p k n", k=k)

            def project(ps, weight, src, everything, rows=P):
                pieces = [(0, 0, TOK // 2), (512, TOK // 2, TOK // 2)] if everything else [(0, CTX, SEQ)]
                for at, tok, n in pieces:
                    for k in range(len(weight)):
                        last = mm(ps[0:rows, at:at + n], weight[k], src[k][:, tok:tok + n],
                                  start=k == 0, stop=k == len(weight) - 1)
                return last

            def project3(o, stationary, moving):
                for k, ((wh, wl), (xh, xl)) in enumerate(zip(stationary, moving)):
                    mm(o, wh, xh, start=k == 0, stop=False)
                    mm(o, wh, xl, start=False, stop=False)
                    last = mm(o, wl, xh, start=False, stop=k == len(stationary) - 1)
                return last

            def rows2(tok, n):
                return [(h_hi[:, k, tok:tok + n], h_lo[:, k, tok:tok + n]) for k in range(DK)]

            def weights2(l, what, col, n):
                i0, per = {"ks": (0, 2), "qs": (4, 1), "u": (12, 1)}[what]
                pe.wait_ge(piece_low, PIECES * l + {"ks": 4, "qs": 12, "u": 20}[what])
                out_ = []
                for k in range(DK):
                    _, at, high = split_piece(l, i0 + k // per)
                    c = 256 * (k % 2) * (per - 1) + col
                    out_.append((high[:, c:c + n], ring_r[:, at + c:at + c + n]))
                return out_

            def turn(ps, tiles):
                for at, t in tiles:
                    last = nc.tensor.transpose(ps[0:t.shape[1], at:at + t.shape[0]], t, ident[0:t.shape[0], 0:t.shape[0]])
                return last

            tiles_done = [0]

            def moe(l, part):
                sl = L[l]
                pe.wait_ge(tab_ready, l + 1)
                n_blocks = pe.value_load(tab[0:1, 2 * TABN:2 * TABN + 1], min_val=1, max_val=max_blocks(l))
                A = active(l)

                def slots_of(n, count):
                    pe.wait_ge(sl["oh_ready"], count)
                    for i, t in enumerate(A):
                        last = mm(m_i, oh[:, n % 2, t, :], tokb[:, 3 * t:3 * t + 3], start=i == 0, stop=i == len(A) - 1)
                    last.then_inc(sl["idx_done"], 1)

                def turn_tokens(s, gathered):
                    pe.wait_ge(sl[f"gat{s}"], gathered)
                    v = xg[:, s, 0:D].rearrange("s (p k) -> s k p", k=DK)
                    turn(m_tr, [(k * P, v[:, k, :]) for k in range(DK)]).then_inc(sl["tr_done"], 1)

                def gate_up(s, turns, n):
                    pe.wait_ge(sl[f"wgu{s}"], 32 * turns)
                    pe.wait_ge(sl["xgT_a"], n + 1)
                    pe.wait_ge(sl["xgT_b"], n + 1)
                    for k in range(DK):
                        last = mm(m_gu[s], xgT[:, s, k, :], wgu[s][:, :, k, :], start=k == 0, stop=k == DK - 1)
                    last.then_inc(sl["gu_done"], 1)

                def turn_hidden(s, n):
                    pe.wait_ge(sl["h_ready"], n + 1)
                    hv = hb[:, s, :].rearrange("s (p c) -> s c p", c=2)
                    turn(m_h, [(cc * P, hv[:, cc, :]) for cc in range(2)]).then_inc(sl["hT_done"], 1)

                if part == "first":
                    slots_of(0, 1)
                    pe.wait_ge(sl["idx_ready"], 1)
                    slots_of(1, 2)
                    return
                turn_tokens(0, 16)
                gate_up(0, 1, 0)
                turn_tokens(1, 16)
                slots_of(2, 3)
                turn_hidden(0, 0)
                with pe.Fori(0, max_turns(l) // UNROLL) as m:
                    with pe.If(UNROLL * m < n_blocks):
                        for r in range(UNROLL):
                            n, s = UNROLL * m + r + 1, (r + 1) % 2
                            half = UNROLL // 2 * m
                            with pe.If(n < n_blocks):
                                gate_up(s, half + (r + 1) // 2 + 1, n)
                                turn_tokens(1 - s, 16 * (half + (r + 2) // 2 + 1))
                                pe.wait_ge(sl["idx_ready"], n + 2)
                                slots_of(r + 1, n + 3)
                            with pe.If(n <= n_blocks):
                                pe.wait_ge(sl[f"wdn{1 - s}"], 16 * (half + r // 2 + 1))
                                pe.wait_ge(sl["hT_ev"], n)
                                pe.wait_ge(sl["y_a"], n)
                                pe.wait_ge(sl["y_b"], n)
                                for side in range(2):
                                    for cc in range(2):
                                        last = mm(m_y[:, 512 * side:512 * side + 512], hTb[:, 1 - s, cc * P:cc * P + P],
                                                  wdn[1 - s][:, cc, 512 * side:512 * side + 512], start=cc == 0, stop=cc == 1)
                                last.then_inc(sl["dn_done"], 1)
                            with pe.If(n < n_blocks):
                                turn_hidden(s, n)

            pe.wait_ge(s_con, 16)
            fills = []
            for job in jobs:
                kind, a = job.kind, job.args
                if job.drain:
                    ps = slot[job.slot]
                    if len(fills) >= 3:
                        pe.wait_ge(drained[fills[-3].drain], fills[-3].count)
                    fills.append(job)
                if kind == "cvec":
                    pe.wait_ge(s_vec, 32)
                    last = turn(ps, [(0, vecs[0:16, :])])
                elif kind == "vec":
                    pe.wait_ge(s_vecs[a[0]], 96)
                    last = turn(ps, [(0, layer_vecs[a[0]][0:NVEC, :])])
                elif kind == "modr":
                    w = chunks(panel(("mod",) + a), DK, 512)
                    after(pe, "cvec")
                    for k in range(DK):
                        j = k % 4
                        last = mm(ps[32 * j:32 * j + 32, 0:512], cTk[:, k, :], w[:, k, :], start=k < 4, stop=k >= 4)
                elif kind == "mod":
                    after(pe, "modr", *a)
                    for j in range(4):
                        last = mm(ps[:, 2 * j:2 * j + 2], modrow(*a)[:, j * P:j * P + P], cst("sel2"), start=True, stop=True)
                elif kind == "h":
                    l, k = a
                    pe.wait_ge(xn_ready, NT * (l + 1))
                    tiles = [((t - CT) * P, t) for t in range(CT, NT)] + [(SEQ + t * P, t) for t in range(CT)]
                    last = turn(ps, [(at, XN[:, t, k * P:k * P + P]) for at, t in tiles])
                elif kind in ("qs", "ks"):
                    l = a[0]
                    pe.wait_ge(h_low, DK * (l + 1))
                    w = weights2(l, kind, P * a[1] if kind == "qs" else 0, P)
                    for col, tok, n in [(0, 0, TOK // 2), (512, TOK // 2, TOK // 2)] if full(l, kind) else [(0, CTX, SEQ)]:
                        last = project3(ps[:, col:col + n], w, rows2(tok, n))
                elif kind in ("cq", "ckv", "kr"):
                    l = a[0]
                    col, width, key = {"cq": (0, 384, "cq"), "ckv": (0, 288, "ckv"), "kr": (256, 288, "ckv")}[kind]
                    col += P * a[1] if len(a) > 1 else 0
                    w = chunks(panel((key, l)), DK, width)
                    rows = ROPE if kind == "kr" else P
                    after(pe, "h", l, DK - 2)
                    after(pe, "h", l, DK - 1)
                    last = project(ps, [w[:, k, col:col + rows] for k in range(DK)], [hT[:, k, :] for k in range(DK)],
                                   full(l, kind), rows)
                elif kind in ("rq", "rk"):
                    l = a[0]
                    cs = (0, 1, 2) if kind == "rq" else (3, 4)
                    after(pe, *(("cq", l, 2) if kind == "rq" else ("ckv", l, 1)))
                    last = project(ps, [cst("ones") for _ in cs], [sq[:, i, :] for i in cs], full(l, kind) or kind == "rk")
                elif kind == "krp":
                    after(pe, "kr", a[0])
                    last = mm(ps[0:32, 0:SEQ], cst("perm8")[0:32, 0:32], kr[:, CTX:TOK], start=True, stop=True)
                elif kind in ("qr", "qn"):
                    l, j = a
                    pe.wait_ge(cn_ready, 2 * l + 2)
                    w = panel(("uq", l))
                    at, per = (P * j, 512) if kind == "qn" else (1536 + P * j, 256)
                    ws = [w[:, at + per * k:at + per * k + P] for k in range(3)]
                    last = project(ps, ws, [cqT[:, k, :] for k in range(3)], full(l, kind))
                elif kind == "qrp":
                    l, j = a
                    after(pe, "qr", l, j)
                    last = mm(ps[:, 0:SEQ], cst("perm8"), qr[:, j, CTX:TOK], start=True, stop=True)
                elif kind == "kn":
                    l, j = a
                    pe.wait_ge(cn_ready, 2 * l + 1)
                    w = panel(("ukv", l))
                    ws = [w[:, 512 * k + P * j:512 * k + P * j + P] for k in range(2)]
                    last = project(ps, ws, [ckvT[:, k, :] for k in range(2)], True)
                elif kind == "v":
                    l, t = a
                    w = panel(("ukv", l))
                    for k in range(2):
                        last = mm(ps[:, 0:512], ckvT[:, k, t * P:t * P + P], w[:, 1024 + 512 * k:1536 + 512 * k],
                                  start=k == 0, stop=k == 1)
                elif kind == "S":
                    l, br, i = a
                    t, h, _, parts = attn(l, br, i)
                    if i == 0:
                        if br == "m":
                            pe.wait_ge(rope_copied, 3 * (l + 1))
                            for j in range(4):
                                after(pe, "kn", l, j)
                            after(pe, "v", l, NT - 1)
                            after(pe, "v", l, NT - 2)
                            after(pe, "qn", l, 2)
                            after(pe, "qn", l, 3)
                        else:
                            pe.wait_ge(kk_ready, l + 1)
                            after(pe, "vs", l)
                    if br == "m":
                        q = QT[0:96, h, t * P:t * P + P]
                    else:
                        q = QS[64 * (h % 2):64 * (h % 2) + 64, h // 2, t * P:t * P + P]
                    for at, key, n in parts:
                        k = KT[0:96, h, key:key + n] if br == "m" else KK[64 * (h % 2):64 * (h % 2) + 64, h // 4, key:key + n]
                        last = mm(ps[:, at:at + n], q, k, start=True, stop=True)
                elif kind == "T":
                    l, br, i = a
                    if br == "m":
                        after(pe, "S", l, br, i)
                    else:
                        pe.wait_ge(exp_ready, exp_no(l, i))
                    n = len(key_tiles(l, br, i))
                    last = turn(ps, [(j * P, Pb[:, i % 2, j * P:j * P + P]) for j in range(n)])
                elif kind == "PV":
                    l, br, i = a
                    t, h = attn(l, br, i)[:2]
                    g = tiles_done[0]
                    after(pe, "T", l, br, i)
                    if h == 0 and g >= 2:
                        pe.wait_ge(o_drained, g - 1)
                    ks = key_tiles(l, br, i)
                    for j, kt in enumerate(ks):
                        v = V[:, kt, VD * h:VD * h + VD] if br == "m" else VS[:, kt, HD * (h // 4):HD * (h // 4) + HD]
                        last = mm(OB[g % 2][:, VD * h:VD * h + VD], PTb[:, i % 2, j * P:j * P + P], v,
                                  start=j == 0, stop=j == len(ks) - 1)
                    if h == HEADS - 1:
                        last.then_inc(o_full, 1)
                        tiles_done[0] += 1
                elif kind == "yT":
                    l, br, t = a
                    g = tile_no(l, br, t)
                    pe.wait_ge(o_drained, g + 1)
                    last = turn(ps, [(j * P, ytok[:, g % 2, j * P:j * P + P]) for j in range(4)])
                elif kind in ("qsp", "ksp"):
                    l = a[0]
                    after(pe, kind[:2], *a)
                    src = QS[:, a[1], :] if kind == "qsp" else KS
                    last = mm(ps[:, 0:SEQ], cst("perm16"), src[:, CTX:TOK], start=True, stop=True)
                elif kind == "vs":
                    w = weights2(a[0], "ks", SWKV, SWKV)
                    for t in range(NT):
                        last = project3(ps[:, t * P:t * P + P], rows2(t * P, P), w)
                elif kind in ("u", "pm"):
                    l, j = a
                    streams = ((0, SEQ), (512, CTX))[:2 if l < DEPTH - 1 else 1]
                    if kind == "u":
                        w = weights2(l, "u", j * P, P)
                        for col, n in streams:
                            last = project3(ps[:, col:col + n], w, rows2(0 if col else CTX, n))
                    else:
                        pe.wait_ge(pooled, 4 * l + j + 1)
                        w = chunks(panel(("pm", l)), 4, P)[:, j, :]
                        for col, n in streams:
                            at = UC if col else UL
                            last = mm(ps[:, col:col + n], w, U[:, j, at:at + n], start=True, stop=True)
                elif kind in ("g", "b"):
                    l, n2, b, cc = a
                    buf = panel(("merge", l, n2, b))
                    if kind == "g":
                        i = gate_panel(l, n2, b)
                        pe.wait_ge(w_low, GATE_PANELS * l + i + 1)
                        at = SLOT * (panel_no["merge", l, n2, b] % RING) + cc * P
                        w = []
                        for k0, piece in gate_weights(i):
                            for k in range(piece.shape[1] // 256):
                                lo = at + 256 * (k0 + k)
                                w.append((piece[:, 256 * k + cc * P:256 * k + cc * P + P], ring_r[:, lo:lo + P]))
                        for col, tok, n in [(0, 0, TOK // 2), (512, TOK // 2, TOK // 2)] if full(l, kind) else [(0, CTX, SEQ)]:
                            last = project3(ps[:, col:col + n], w, rows2(tok, n))
                    elif b == 0:
                        w = chunks(buf[:, 2048:3072], 4, 256)
                        if n2 == cc == 0:
                            after(pe, "yT", l, "m", NT - 1)
                        last = project(ps, [w[:, k, cc * P:cc * P + P] for k in range(4)], [Ym[:, k, :] for k in range(4)],
                                       full(l, kind))
                    else:
                        pe.wait_ge(y_low, 8 * l + 4 * b)
                        pe.wait_ge(w_low, GATE_PANELS * l + gate_panel(l, n2, b) + 1)
                        at = SLOT * (panel_no["merge", l, n2, b] % RING) + cc * P
                        w = [(ring_r[:, at + 3072 + 256 * k:at + 3072 + 256 * k + P],
                              ring_r[:, at + 2048 + 256 * k:at + 2048 + 256 * k + P]) for k in range(4)]
                        for col, tok, n in [(0, 0, TOK // 2), (512, TOK // 2, TOK // 2)] if full(l, kind) else [(0, CTX, SEQ)]:
                            y = [(y_hi[b][:, k, tok:tok + n], y_lo[b][:, k, tok:tok + n]) for k in range(4)]
                            last = project3(ps[:, col:col + n], w, y)
                elif kind == "bc":
                    l, which, s = a
                    pe.wait_ge(setup_dve, 2 * l + 2)
                    for k in range(DK):
                        last = mm(ps[:, k * P:k * P + P], column(l, which, s, k).broadcast_to([P, P]), ident,
                                  start=True, stop=True)
                elif kind == "o":
                    l, t = a
                    for half in range(2):
                        w = chunks(panel(("wo", l, half)), DK, 512)
                        if t == active(l)[0]:
                            after(pe, "b", l, 3, 2, 1)
                        for k in range(DK):
                            last = mm(ps[:, 512 * half:512 * half + 512], MG[:, k, t * P:t * P + P], w[:, k, :],
                                      start=k == 0, stop=k == DK - 1)
                elif kind == "f":
                    l, t = a
                    n = active(l).index(t)
                    pe.wait_ge(f_ready, n + 1 + (NT if l else 0))
                    last = turn(ps, [(k * P, fb[:, n % 2, k * P:k * P + P]) for k in range(DK)])
                elif kind == "r":
                    l, t = a
                    w = chunks(panel(("router", l)), DK, E)
                    after(pe, "f", l, t)
                    for k in range(DK):
                        last = mm(ps[:, 0:E], hT[:, k, t * P:t * P + P], w[:, k, :], start=k == 0, stop=k == DK - 1)
                elif kind == "sg":
                    l, t = a
                    w = panel(("shgu", l)).rearrange("p (g k n) -> p g k n", g=2, k=DK)
                    for k in range(DK):
                        last = mm(ps[:, 0:512], hT[:, k, t * P:t * P + P], w[:, :, k, :], start=k == 0, stop=k == DK - 1)
                elif kind == "sT":
                    l, t = a
                    after(pe, "sg", l, t)
                    n = active(l).index(t)
                    last = turn(ps, [(cc * P, hb[:, n % 2, cc * P:cc * P + P]) for cc in range(2)])
                elif kind == "sd":
                    l, t = a
                    w = chunks(panel(("shd", l)), 2, D)
                    n = active(l).index(t)
                    after(pe, "sT", l, t)
                    for half in range(2):
                        for cc in range(2):
                            last = mm(ps[:, 512 * half:512 * half + 512], hTb[:, n % 2, cc * P:cc * P + P],
                                      w[:, cc, 512 * half:512 * half + 512], start=cc == 0, stop=cc == 1)
                elif kind == "pos":
                    l, t = a
                    A = active(l)
                    pe.wait_ge(w_ready, A.index(t) + 1 + (NT if l else 0))
                    for u in [v for v in A if v <= t]:
                        last = mm(ps[:, 0:E], (trib if u == t else onesb)[:], Mb[:, u * E:u * E + E], start=u == A[0], stop=u == t)
                elif kind == "cnt":
                    A = active(a[0])
                    for u in A:
                        last = mm(ps[0:E, 0:1], Mb[:, u * E:u * E + E], onesb[:, 0:1], start=u == A[0], stop=u == A[-1])
                elif kind == "end":
                    after(pe, "cnt", a[0])
                    last = mm(ps[0:E, 0:1], trib[0:E, 0:E], nbb[0:E, 0:1], start=True, stop=True)
                elif kind == "tab":
                    after(pe, "end", a[0])
                    mm(ps[0:1, 0:TABN], onesb[0:E, 0:1], Gb[0:E, :], start=True, stop=True)
                    mm(ps[0:1, 128:128 + TABN], nbb[0:E, 0:1], Gb[0:E, :], start=True, stop=True)
                    last = mm(ps[0:1, 256:257], nbb[0:E, 0:1], onesb[0:E, 0:1], start=True, stop=True)
                elif kind == "moe":
                    for before in fills[-3:]:
                        pe.wait_ge(drained[before.drain], before.count)
                    moe(a[0], "turns")
                    loop_end(pe)
                elif kind == "first":
                    moe(a[0], "first")
                if job.drain:
                    last.then_inc(filled, 1)

        @block.scalar
        def _(act):
            A_ = nc.scalar.activation

            def copy(o, i):
                return A_(o, i, ACT.Copy)

            def copy_scaled(o, i, factor):
                return A_(o, i, ACT.Copy, scale=factor)

            def moe(l):
                sl = L[l]
                act.wait_ge(tab_ready, l + 1)
                n_blocks = act.value_load(tab[0:1, 2 * TABN:2 * TABN + 1], min_val=1, max_val=max_blocks(l))

                def tokens(s, count):
                    act.wait_ge(sl["tr_done"], count)
                    copy(xgT[:, s, 0:4, :], m_tr[:, 0:512].rearrange("p (k s) -> p k s", k=4)).then_inc(sl["xgT_a"], 1)

                def silu(s, count):
                    act.wait_ge(sl["gu_done"], count)
                    A_(s1[:, s, :], m_gu[s][:, 0:DE], ACT.Silu).then_inc(sl["silu_done"], 1)

                act.sem_inc(sl["y_a"], 1)
                tokens(0, 1)
                silu(0, 1)
                tokens(1, 2)
                with act.Fori(0, max_turns(l) // UNROLL) as m:
                    with act.If(UNROLL * m < n_blocks):
                        for r in range(UNROLL):
                            n, s = UNROLL * m + r + 1, (r + 1) % 2
                            with act.If(n < n_blocks):
                                silu(s, n + 1)
                                tokens(1 - s, n + 2)
                            with act.If(n <= n_blocks):
                                act.wait_ge(sl["dn_done"], n)
                                act.wait_ge(sl[f"scat{1 - s}"], 16 * (UNROLL // 2 * m + r // 2 + 1))
                                copy(yb[:, 1 - s, 0:512], m_y[:, 0:512]).then_inc(sl["y_a"], 1)

            def weights_high(l, i):
                at = loaded(act, gate_key(l, i))
                if i == 0:
                    act.wait_ge(filled, names["yT", l, "s", NT - 1].fill)
                for k0, piece in gate_weights(i):
                    ins = copy(piece, ring[:, at + 256 * k0:at + 256 * k0 + piece.shape[1]])
                if gate_key(l, i)[3]:
                    ins = copy(ring_r[:, at + 3072:at + 4096], ring[:, at + 2048:at + 3072])
                ins.then_inc(w_high, 1)

            for job in jobs:
                kind, a, ps = job.kind, job.args, slot[job.slot] if job.drain else None
                mine = job.drain == "act"
                l = a[0] if a else 0
                last = None
                if kind == "modr" and a == (0, 0):
                    for t in range(NT):
                        act.wait_ge(s_x, 32)
                        ins = A_(HT[:, t * D:t * D + D], XT[:, t, :], ACT.Square, accum_out=ssq[:, t:t + 1])
                    ins.then_inc(ssq_ready, 1)
                    act.wait_ge(var_ready, norm_no(l, 0))
                    A_(rstd[:, 0:NT], ssq[:, 0:NT], ACT.Sqrt).then_inc(rstd_ready, 1)
                if kind == "pm" and a[1] == 0:
                    weights_high(l, 0)
                if mine:
                    act.wait_ge(filled, job.fill)
                if kind == "cvec":
                    act.wait_ge(cT_zero, 1)
                    last = A_(cTk[:, :, 0:2].rearrange("p k s -> p s k"), ps[:, 0:16].rearrange("p (s k) -> p s k", s=2), ACT.Silu)
                elif kind == "modr":
                    last = copy(modrow(*a), ps[:, 0:512])
                elif kind == "h" and mine:
                    k = a[1]
                    if k == 0:
                        act.wait_ge(setup_dve, 2 * l + 1)
                    for at, tok, n, s in ((0, CTX, SEQ, 0), (512, 0, CTX, 1)):
                        last = A_(hT[:, k, tok:tok + n], ps[:, at:at + n], ACT.Identity,
                                  scale=column(l, "A1", s, k), bias=column(l, "sh1", s, k))
                elif kind in ("cq", "ckv"):
                    ev = full(l, kind)
                    i = a[1] + (3 if kind == "ckv" else 0)
                    dst = cqT[:, a[1], :] if kind == "cq" else ckvT[:, a[1], :]
                    if l and kind == "ckv" and a[1] == 0:
                        act.wait_ge(s_xs, 16 * NT)
                    copy(sview(dst, ev), pview(ps, ev))
                    last = A_(sview(sq[:, i, :], ev), pview(ps, ev), ACT.Square)
                elif kind == "kr":
                    last = copy(sview(kr, True), pview(ps, True, 32))
                elif kind in ("rq", "rk"):
                    i = int(kind == "rk")
                    act.wait_ge(rms_rec, 2 * l + 2 - i)
                    v = sview(rb[:, i, :], full(l, kind) or i)
                    A_(v, v, ACT.Sqrt).then_inc(rms_sqrt, 1)
                elif kind == "krp":
                    act.wait_ge(roped, roped_no(l, "k"))
                    for h in range(HEADS):
                        ins = copy(KT[64:96, h, :], kr)
                    ins.then_inc(rope_copied, 1)
                elif kind == "qr":
                    ev = full(l, kind)
                    last = A_(sview(qr[:, a[1], :], ev), pview(ps, ev), ACT.Copy, scale=-MLA_SCALE)
                elif kind == "qrp":
                    j = a[1]
                    act.wait_ge(roped, roped_no(l, j))
                    for h in range(4 * j, 4 * j + 4):
                        ins = copy(sview(QT[64:96, h, :], full(l, kind)),
                                   sview(qr[32 * (h % 4):32 * (h % 4) + 32, j, :], full(l, kind)))
                    ins.then_inc(rope_copied, 1)
                elif kind in ("qn", "kn") and mine:
                    T_, ev = (QT, full(l, kind)) if kind == "qn" else (KT, True)
                    for hh in range(2):
                        last = A_(sview(T_[0:64, 2 * a[1] + hh, :], ev), pview(ps[64 * hh:64 * hh + 64, :], ev, 64), ACT.Copy,
                                  scale=-MLA_SCALE if kind == "qn" else 1.0)
                elif kind == "v" and mine:
                    last = copy(V[:, a[1], :], ps[:, 0:512])
                elif kind == "S":
                    _, br, i = a
                    t, h, at, parts = attn(l, br, i)
                    w = sum(n for _, _, n in parts)
                    g = tile_no(l, br, t)
                    if br == "m":
                        act.wait_ge(max_ready, max_no(l, i))
                    else:
                        after(act, "S", l, br, i)
                    if br == "m":
                        last = A_(Pb[:, i % 2, 0:w], ps[:, 0:w], ACT.Exp, scale=-1.0, bias=nb[:, 8 * (g % 2) + h:8 * (g % 2) + h + 1],
                                  accum_out=den[:, 8 * (g % 2) + h:8 * (g % 2) + h + 1])
                    else:
                        A_(Pb[:, i % 2, 0:w], Pb[:, i % 2, 0:w], ACT.Exp, scale=-1.0, bias=nb[:, 8 * (g % 2) + h:8 * (g % 2) + h + 1],
                           accum_out=den[:, 8 * (g % 2) + h:8 * (g % 2) + h + 1]).then_inc(exp_ready, 1)
                        if h == HEADS - 1:
                            act.wait_ge(sink_sum, sink_no(l, t))
                            A_(nb[:, 16 + 8 * (g % 2):24 + 8 * (g % 2)], nb[:, 16 + 8 * (g % 2):24 + 8 * (g % 2)], ACT.Exp)\
                                .then_inc(sink_exp, 1)
                elif kind == "T" and mine:
                    n = P * len(key_tiles(l, a[1], a[2]))
                    last = copy(PTb[:, a[2] % 2, 0:n], ps[:, 0:n])
                elif kind == "yT":
                    t = a[2]
                    last = copy(Y[a[1]][:, :, t * P:t * P + P], ps[:, 0:512].rearrange("p (c n) -> p c n", c=4))
                elif kind == "qs":
                    last = A_(sview(QS[:, a[1], :], full(l, kind)), pview(ps, full(l, kind)), ACT.Copy, scale=-SWA_SCALE)
                elif kind == "ks":
                    last = copy(sview(KS, True), pview(ps, True))
                elif kind == "ksp":
                    act.wait_ge(roped, roped_no(l, "s"))
                    for kv in range(2):
                        for half in range(2):
                            ins = copy(KK[64 * half:64 * half + 64, kv, :], KS[64 * kv:64 * kv + 64, :])
                    ins.then_inc(kk_ready, 1)
                elif kind == "vs":
                    last = copy(VS, ps[:, 0:TOK].rearrange("p (t n) -> p t n", t=NT))
                elif kind == "u":
                    if a[1] == 0:
                        act.wait_ge(u_zero, l + 1)
                    last = copy(U[:, a[1], UL:UL + SEQ], ps[:, 0:SEQ])
                    if l < DEPTH - 1:
                        last = copy(U[:, a[1], UC:UC + CTX], ps[:, 512:512 + CTX])
                elif kind == "g":
                    i = gate_no(*a[1:])
                    if i >= 2:
                        after(act, "b", l, *gate_args(i - 2))
                    ev = full(l, kind)
                    A_(sview(SG[:, i % 2, :], ev), pview(ps, ev), ACT.Sigmoid).then_inc(drained["act"], 1)
                    if a[1] == a[3] == 0 and a[2]:
                        after(act, "pm", l, 3)
                        t0 = 0 if full(l, kind) else CTX
                        for k in range(4):
                            copy(y_hi[a[2]][:, k, t0:TOK], (Ym, Yp, Ys)[a[2]][:, k, t0:TOK]).then_inc(y_high, 1)
                    i = gate_panel(*a[:3])
                    if a[3] == 0 and i + 1 < GATE_PANELS:
                        weights_high(l, i + 1)
                elif kind == "bc":
                    if a[1] == "gt2":
                        after(act, "o", l, active(l)[-1])
                    last = copy(BC[a[1], a[2]], ps)
                elif kind == "o":
                    n = active(l).index(a[1])
                    after(act, "o", l, a[1])
                    A_(junk, XT[:, a[1], :], ACT.Square, accum_out=ssq[:, a[1]:a[1] + 1]).then_inc(ssq_ready, 1)
                    act.wait_ge(var_ready, norm_no(l, n + 1))
                    A_(rstd[:, a[1]:a[1] + 1], ssq[:, a[1]:a[1] + 1], ACT.Sqrt).then_inc(rstd_ready, 1)
                elif kind == "f":
                    last = copy(hT[:, :, a[1] * P:a[1] * P + P], ps.rearrange("p (k n) -> p k n", k=DK))
                elif kind == "r":
                    last = A_(scores[:, a[1] * E:a[1] * E + E], ps[:, 0:E], ACT.Sigmoid)
                elif kind == "sg":
                    n = active(l).index(a[1])
                    act.wait_ge(filled, job.fill)
                    A_(s1[:, n % 2, :], ps[:, 0:DE], ACT.Silu).then_inc(sh_silu, 1)
                elif kind == "sT":
                    n = active(l).index(a[1])
                    last = copy(hTb[:, n % 2, :], ps[:, 0:DE])
                elif kind == "sd":
                    n = active(l).index(a[1])
                    if n >= 2:
                        act.wait_ge(s_sh[n % 2], store_no(l, n) - 16)
                    last = copy(yb[:, n % 2, :], ps)
                elif kind == "moe":
                    moe(l)
                    loop_end(act)
                    if l < DEPTH - 1:
                        def normed(t):
                            act.wait_ge(pre_rstd, NT * l + t + 1)
                            copy_scaled(XN[:, t, :], XT[:, t, :], rstd[:, t:t + 1]).then_inc(xn_ready, 1)

                        for t in range(NT):
                            act.wait_ge(combined, t + 1)
                            A_(junk, XT[:, t, :], ACT.Square, accum_out=ssq[:, t:t + 1]).then_inc(pre_ssq, 1)
                            act.wait_ge(pre_var, NT * l + t + 1)
                            A_(rstd[:, t:t + 1], ssq[:, t:t + 1], ACT.Sqrt).then_inc(pre_rstd, 1)
                            if t < 4:
                                normed(t)
                        act.wait_ge(combined, NT)
                        for t in range(4, NT):
                            normed(t)
                    else:
                        for i, t in enumerate(active(l)):
                            act.wait_ge(combined, NT + i + 1)
                            A_(junk, XT[:, t, :], ACT.Square, accum_out=ssq[:, t:t + 1]).then_inc(ssq_ready, 1)
                            act.wait_ge(var_ready, norm_no(l + 1, i))
                            A_(rstd[:, t:t + 1], ssq[:, t:t + 1], ACT.Sqrt).then_inc(rstd_ready, 1)
                if last is not None:
                    last.then_inc(drained["act"], 1)
                if kind == "S" and a[1] == "m" and a[2] in HALF:
                    k = HALF.index(a[2])
                    copy(h_hi[:, k, :], hT[:, k, :]).then_inc(h_high, 1)
                for i in split_now(kind, a) if kind != "qsp" else ():
                    key, at, high = split_piece(l, i)
                    loaded(act, key)
                    if i == 4:
                        act.wait_ge(filled, panels[panel_no["qs_high", l] - RING][1].fill)
                    elif i == 12:
                        act.wait_ge(filled, names["yT", l, "m", NT - 1].fill)
                    copy(high, ring[:, at:at + 512]).then_inc(piece_high, 1)

        @block.vector
        def _(dve):
            vec = nc.vector
            tt, ts, stt = vec.tensor_tensor, vec.tensor_scalar, vec.scalar_tensor_tensor

            def link(ins):
                step("dve", dve, ins)

            def rotate(rows, ps, tables, br, n_rows=P):
                lat, tmp = rows[:, CTX:TOK], tmp_rope[br][0:n_rows, 0:SEQ]
                tt(tmp, ps[0:n_rows, 0:SEQ], tables[0:n_rows, 1, :], ALU.mult)
                ins = tt(lat, lat, tables[0:n_rows, 0, :], ALU.mult)
                link(ins)
                return tt(lat, lat, tmp, ALU.add)

            def weights_low(l, i):
                at = SLOT * (panel_no[gate_key(l, i)] % RING)
                dve.wait_ge(w_high, GATE_PANELS * l + i + 1)
                for k0, piece in gate_weights(i):
                    a, b = at + 256 * k0, at + 256 * k0 + piece.shape[1]
                    ins = tt(ring_r[:, a:b], ring[:, a:b], piece, ALU.subtract)
                if gate_key(l, i)[3]:
                    a, b, c = at + 2048, at + 3072, at + 4096
                    ins = tt(ring_r[:, a:b], ring[:, a:b], ring_r[:, b:c], ALU.subtract)
                ins.then_inc(w_low, 1)

            def inv_mean(out_, in_, n):
                link(ts(out_, in_, 1.0 / n, EPS, ALU.mult, ALU.add))
                return vec.reciprocal(out_, out_)

            def route(l, t):
                sc = scores[:, t * E:t * E + E]
                sel, t1, t2, t3 = (rt[:, i * E:i * E + E] for i in range(4))
                n = active(l).index(t)
                g8 = t1.rearrange("p (g j) -> p g j", g=GROUPS)
                gs, rank, pen, v8 = (rsm[:, 8 * i:8 * i + 8] for i in range(4))
                total, inv = rsm[:, 32:33], rsm[:, 33:34]
                after(dve, "r", l, t)
                link(tt(sel, sc, bias[:, l * E:l * E + E], ALU.add))
                for g in range(GROUPS):
                    ins = vec.max(g8[:, g, :], sel[:, 8 * g:8 * g + 8])
                link(ins)
                link(tt(gs, g8[:, :, 0], g8[:, :, 1], ALU.add))
                gj = gs.unsqueeze(1).broadcast_to([P, GROUPS, GROUPS])
                gi = gs.unsqueeze(2).broadcast_to([P, GROUPS, GROUPS])
                v2, v3 = (v.rearrange("p (g j) -> p g j", g=GROUPS) for v in (t2, t3))
                tt(v2, gj, gi, ALU.is_gt)
                link(tt(v3, gj, gi, ALU.is_equal))
                link(tt(t3, t3, cst("lower"), ALU.mult))
                link(tt(t2, t2, t3, ALU.add))
                link(vec.tensor_reduce(rank, v2, AX.X, ALU.add))
                link(ts(rank, rank, float(KEEP), None, ALU.is_lt))
                link(ts(pen, rank, -NEG, NEG, ALU.mult, ALU.add))
                vs_ = sel.rearrange("p (g j) -> p g j", g=GROUPS)
                link(tt(vs_, vs_, rank.unsqueeze(2).broadcast_to([P, GROUPS, 8]), ALU.mult))
                link(tt(vs_, vs_, pen.unsqueeze(2).broadcast_to([P, GROUPS, 8]), ALU.add))
                link(vec.max(v8, sel))
                link(vec.match_replace(t1, v8, sel, -3e38))
                link(tt(t2, t1, sel, ALU.not_equal))
                vec.tensor_copy(Mb[:, t * E:t * E + E], t2)
                link(tt(t3, sc, t2, ALU.mult))
                link(vec.tensor_reduce(total, t3, AX.X, ALU.add))
                link(vec.reciprocal(inv, total))
                if n >= 2:
                    dve.wait_ge(s_w[n % 2], store_no(l, n) - 16)
                ts(Wt[:, n % 2, :], t3, inv, ROUTED, ALU.mult, ALU.mult).then_inc(w_ready, 1)

            def moe(l, part):
                sl = L[l]
                A = active(l)
                a0 = A[0]
                n_blocks = dve.value_load(tab[0:1, 2 * TABN:2 * TABN + 1], min_val=1, max_val=max_blocks(l))

                def one_hot(n, s):
                    e = dve.value_load(tab[0:1, bass.ds(n, 1)], min_val=0, max_val=E - 1)
                    b = dve.value_load(tab[0:1, bass.ds(n + TABN, 1)], min_val=0, max_val=MAXB - 1)
                    a, _ = CONSTS["slot1"]
                    slots = con[:, bass.ds(a + b * P, P)].unsqueeze(1).broadcast_to([P, len(A), P])
                    rows = posm[:, a0 * E:NT * E].rearrange("p (t e) -> p t e", e=E)[:, :, bass.ds(e, 1)]
                    tt(oh[:, s, a0:NT, :], slots, rows.broadcast_to([P, len(A), P]), ALU.is_equal)\
                        .then_inc(sl["oh_ready"], 1)
                    return e

                def take_index(count, i4):
                    dve.wait_ge(sl["idx_done"], count)
                    vec.tensor_copy(pcol[:], m_i).then_inc(sl["idx_copied"], 1)
                    dve.wait_ge(sl["idx_copied"], count)
                    stt(idxf[:, 0:1], pcol[:, 2:3], cst("negdummy"), pcol[:, 0:1], ALU.mult, ALU.add)\
                        .then_inc(sl["idx_low"], 1)
                    dve.wait_ge(sl["idx_low"], count)
                    stt(idx[:, i4:i4 + 1], idxf[:, 0:1], cst("dummy"), pcol[:, 1:2], ALU.add, ALU.add)\
                        .then_inc(sl["idx_ready"], 1)

                def tokens(s, count):
                    dve.wait_ge(sl["tr_done"], count)
                    vec.tensor_copy(xgT[:, s, 4:8, :], m_tr[:, 512:1024].rearrange("p (k s) -> p k s", k=4))\
                        .then_inc(sl["xgT_b"], 1)

                def hidden(s, n):
                    e = dve.value_load(tab[0:1, bass.ds(n, 1)], min_val=0, max_val=E - 1)
                    dve.wait_ge(sl["silu_done"], n + 1)
                    stt(hb[:, s, :], s1[:, s, :], xg[:, s, bass.ds(e + D, 1)], m_gu[s][:, DE:2 * DE],
                        ALU.mult, ALU.mult).then_inc(sl["h_ready"], 1)

                def turned_hidden(s, n):
                    dve.wait_ge(sl["hT_done"], n + 1)
                    vec.tensor_copy(hTb[:, s, :], m_h).then_inc(sl["hT_ev"], 1)

                if part == "first":
                    one_hot(0, 0)
                    one_hot(1, 1)
                    take_index(1, 0)
                    take_index(2, 1)
                    one_hot(2, 0)
                    return
                dve.sem_inc(sl["y_b"], 1)
                tokens(0, 1)
                hidden(0, 0)
                tokens(1, 2)
                take_index(3, 2)
                turned_hidden(0, 0)
                one_hot(3, 1)
                with dve.Fori(0, max_turns(l) // UNROLL) as m:
                    with dve.If(UNROLL * m < n_blocks):
                        for r in range(UNROLL):
                            n, s = UNROLL * m + r + 1, (r + 1) % 2
                            with dve.If(n < n_blocks):
                                hidden(s, n)
                                tokens(1 - s, n + 2)
                                dve.wait_ge(sl[f"scat{s}"], 16 * (UNROLL // 2 * m + (r + 1) // 2 + 1))
                                take_index(n + 3, (r + 3) % 4)
                            with dve.If(n <= n_blocks):
                                dve.wait_ge(sl["dn_done"], n)
                                dve.wait_ge(sl[f"scat{1 - s}"], 16 * (UNROLL // 2 * m + r // 2 + 1))
                                vec.tensor_copy(yb[:, 1 - s, 512:1024], m_y[:, 512:1024]).then_inc(sl["y_b"], 1)
                            with dve.If(n < n_blocks):
                                turned_hidden(s, n)
                                one_hot(n + 3, 1 - s)

            def combine(l):
                A = active(l)

                def finish(i):
                    t = A[i]
                    if l < DEPTH - 1:
                        dve.wait_ge(pre_ssq, NT * l + i + 1)
                        inv_mean(ssq[:, t:t + 1], ssq[:, t:t + 1], D).then_inc(pre_var, 1)
                        return
                    dve.wait_ge(ssq_ready, norm_no(l + 1, i))
                    inv_mean(ssq[:, t:t + 1], ssq[:, t:t + 1], D).then_inc(var_ready, 1)
                    dve.wait_ge(s_gfin, 16)
                    dve.wait_ge(rstd_ready, norm_no(l + 1, i))
                    stt(XT[:, t, :], XT[:, t, :], rstd[:, t:t + 1], BC["A2", 0], ALU.mult, ALU.mult)\
                        .then_inc(fin_ready, 1)

                for i, t in enumerate(A):
                    a = comb[i]
                    dve.wait_ge(summed, i + 1 + (NT if l else 0))
                    link(tt(a[:, 0, :], a[:, 0, :], BC["gt2", 0 if t >= CT else 1], ALU.mult))
                    tt(XT[:, t, :], XT[:, t, :], a[:, 0, :], ALU.add).then_inc(combined, 1)
                    if i:
                        finish(i - 1)
                finish(len(A) - 1)

            vec.memset(cT[:], 0.0).then_inc(cT_zero, 1)
            dve.wait_ge(s_con, 16)
            vec.tensor_copy(onesb[:], cst("ones"))
            vec.tensor_copy(trib[:], cst("tri"))
            vec.tensor_copy(tokb[:], cst("tokid"))
            vec.memset(zero[:], 0.0).then_inc(s_zero, 1)
            for job in jobs:
                kind, a, ps = job.kind, job.args, slot[job.slot] if job.drain else None
                mine = job.drain == "dve"
                l = a[0] if a else 0
                last = None
                if kind == "mod" and a == (0, 0):
                    dve.wait_ge(ssq_ready, norm_no(l, 0))
                    inv_mean(ssq[:, 0:NT], ssq[:, 0:NT], D).then_inc(var_ready, 1)
                    dve.wait_ge(rstd_ready, norm_no(l, 0))
                    for t in range(NT):
                        ts(XN[:, t, :], XT[:, t, :], rstd[:, t:t + 1], None, ALU.mult).then_inc(xn_ready, 1)
                if kind == "b" and a[1:] == (0, 0, 0):
                    weights_low(l, 0)
                elif kind == "g" and a[1] == a[3] == 0 and a[2]:
                    t0 = 0 if full(l, kind) else CTX
                    for k in range(4):
                        dve.wait_ge(y_high, 8 * l + 4 * (a[2] - 1) + k + 1)
                        tt(y_lo[a[2]][:, k, t0:TOK], (Ym, Yp, Ys)[a[2]][:, k, t0:TOK], y_hi[a[2]][:, k, t0:TOK],
                           ALU.subtract).then_inc(y_low, 1)
                if mine:
                    dve.wait_ge(filled, job.fill)
                if kind == "h" and a == (0, 1):
                    dve.wait_ge(s_mask, 16)
                    dve.wait_ge(sink_neg, 1)
                    vec.tensor_copy(masks[:], mask_in)
                if kind == "vec":
                    last = vec.tensor_copy(vecT[:, l * NVEC:l * NVEC + NVEC], ps[:, 0:NVEC])
                elif kind == "mod":
                    if a[1] == 0:
                        after(dve, "vec", l)
                    at = l * 96 + 8 * a[1]
                    b4 = vecT[:, l * NVEC + V_B + 4 * a[1]:l * NVEC + V_B + 4 * a[1] + 4]
                    last = tt(modT[:, at:at + 8].rearrange("p (j s) -> p j s", s=2),
                              ps[:, 0:8].rearrange("p (j s) -> p j s", s=2), b4.unsqueeze(2).broadcast_to([P, 4, 2]), ALU.add)
                    if a[1] in (3, 11):
                        last.then_inc(drained["dve"], 1)
                        last = None
                        dve.wait_ge(drained["dve"], job.count)
                        i, g, m = (0, V_GM, 1) if a[1] == 3 else (1, V_GF, 4)
                        gain = vecT[:, l * NVEC + g:l * NVEC + g + DK].unsqueeze(2).broadcast_to([P, DK, 2])
                        ins = stt(AB[:, l * 32 + 16 * i:l * 32 + 16 * i + 16].rearrange("p (k s) -> p k s", s=2),
                                  modT[:, l * 96 + 16 * m:l * 96 + 16 * m + 16].rearrange("p (k s) -> p k s", s=2),
                                  1.0, gain, ALU.add, ALU.mult)
                        ins.then_inc(setup_dve, 1)
                elif kind == "h" and mine:
                    k = a[1]
                    if k == 1:
                        dve.wait_ge(setup_dve, 2 * l + 1)
                    for at, tok, n, s in ((0, CTX, SEQ, 0), (512, 0, CTX, 1)):
                        last = ts(hT[:, k, tok:tok + n], ps[:, at:at + n], column(l, "A1", s, k), column(l, "sh1", s, k),
                                  ALU.mult, ALU.add)
                elif kind in ("rq", "rk"):
                    i = int(kind == "rk")
                    ev = full(l, kind) or bool(i)
                    v = sview(rb[:, i, :], ev)
                    ts(v, pview(ps, ev), 1.0 / (KVL if i else QL), EPS, ALU.mult, ALU.add).then_inc(drained["dve"], 1)
                    dve.wait_ge(drained["dve"], job.count)
                    vec.reciprocal(v, v).then_inc(rms_rec, 1)
                    dve.wait_ge(rms_sqrt, 2 * l + 2 - i)
                    n, buf, g0 = (2, ckvT, V_GKV) if i else (3, cqT, V_GQ)
                    for k in range(n):
                        y = sview(buf[:, k, :], ev)
                        ins = stt(y, y, vecT[:, l * NVEC + g0 + k:l * NVEC + g0 + k + 1], v, ALU.mult, ALU.mult)
                    ins.then_inc(cn_ready, 1)
                elif kind == "krp":
                    dve.wait_ge(s_csm, 16 * (l + 1))
                    rotate(kr, ps, cs_m, "m", 32).then_inc(roped, 1)
                    dve.wait_ge(roped, roped_no(l, "k"))
                elif kind == "qrp":
                    rotate(qr[:, a[1], :], ps, cs_m, "m").then_inc(roped, 1)
                    dve.wait_ge(roped, roped_no(l, a[1]))
                elif kind in ("qsp", "ksp"):
                    if kind == "ksp":
                        dve.wait_ge(s_css, 16 * (l + 1))
                    rotate(QS[:, a[1], :] if kind == "qsp" else KS, ps, cs_s, "s").then_inc(roped, 1)
                    dve.wait_ge(roped, 8 * l + (5 + a[1] if kind == "qsp" else 4))
                elif kind in ("qn", "kn") and mine:
                    T_, ev = (QT, full(l, kind)) if kind == "qn" else (KT, True)
                    for hh in range(2):
                        last = ts(sview(T_[0:64, 2 * a[1] + hh, :], ev), pview(ps[64 * hh:64 * hh + 64, :], ev, 64),
                                  -MLA_SCALE if kind == "qn" else 1.0, None, ALU.mult)
                elif kind == "v" and mine:
                    last = vec.tensor_copy(V[:, a[1], :], ps[:, 0:512])
                elif kind == "S":
                    _, br, i = a
                    t, h, at, parts = attn(l, br, i)
                    w = sum(n for _, _, n in parts)
                    g = tile_no(l, br, t)
                    dve.wait_ge(filled, job.fill)
                    b1 = nb[:, 8 * (g % 2) + h:8 * (g % 2) + h + 1]
                    if br == "m":
                        vec.tensor_reduce(b1, ps[:, 0:w], AX.X, ALU.min).then_inc(max_ready, 1)
                    else:
                        if t < CT:
                            band = masks[:, MASK - CTX:MASK]
                        elif t == NT - 1:
                            band = masks[:, MASK:MASK + MASK2]
                        else:
                            band = masks[:, MASK - w:MASK]
                        ns = sink[:, (2 * l + 1) * HEADS + h:(2 * l + 1) * HEADS + h + 1]
                        vec.tensor_tensor_reduce(Pb[:, i % 2, 0:w], ps[:, at:at + w], band, 1.0, ns, ALU.add, ALU.min,
                                                 b1).then_inc(drained["dve"], 1)
                        if h == HEADS - 1:
                            dve.wait_ge(drained["dve"], job.count)
                            tt(nb[:, 16 + 8 * (g % 2):24 + 8 * (g % 2)], nb[:, 8 * (g % 2):8 * (g % 2) + 8],
                               sink[:, 2 * l * HEADS:(2 * l + 1) * HEADS], ALU.add).then_inc(sink_sum, 1)
                elif kind == "T" and mine:
                    n = P * len(key_tiles(l, a[1], a[2]))
                    last = vec.tensor_copy(PTb[:, a[2] % 2, 0:n], ps[:, 0:n])
                elif kind == "PV" and a[2] % HEADS == HEADS - 1:
                    _, br, i = a
                    t = attn(l, br, i)[0]
                    g = tile_no(l, br, t)
                    dve.wait_ge(o_full, g + 1)
                    d8, r8 = den[:, 8 * (g % 2):8 * (g % 2) + 8], rden[:, 8 * (g % 2):8 * (g % 2) + 8]
                    if br == "s":
                        dve.wait_ge(sink_exp, sink_no(l, t))
                        link(tt(d8, d8, nb[:, 16 + 8 * (g % 2):24 + 8 * (g % 2)], ALU.add))
                    link(vec.reciprocal(r8, d8))
                    tt(ytok[:, g % 2, :].rearrange("p (h n) -> p h n", h=HEADS), OB[g % 2].rearrange("p (h n) -> p h n", h=HEADS),
                       r8.unsqueeze(2).broadcast_to([P, HEADS, VD]), ALU.mult).then_inc(o_drained, 1)
                elif kind == "pm":
                    g = a[1]
                    sc = vecT[:, l * NVEC + V_PS + g:l * NVEC + V_PS + g + 1]
                    last = ts(Yp[:, g, CTX:TOK], ps[:, 0:SEQ], sc, None, ALU.mult)
                    if l < DEPTH - 1:
                        last = ts(Yp[:, g, 0:CTX], ps[:, 512:512 + CTX], sc, None, ALU.mult)
                elif kind == "b":
                    _, n2, b, cc = a
                    i = gate_no(n2, b, cc)
                    after(dve, "g", *a)
                    ev = full(l, kind)
                    gate, mrow = sview(SG[:, i % 2, :], ev), sview(MG[:, 2 * n2 + cc, :], ev)
                    if b == 0:
                        last = tt(mrow, gate, pview(ps, ev), ALU.mult)
                    else:
                        tmp = sview(mtmp[:, i % 2, :], ev)
                        link(tt(tmp, gate, pview(ps, ev), ALU.mult))
                        last = tt(mrow, mrow, tmp, ALU.add)
                    i = gate_panel(*a[:3])
                    if cc == 0 and i + 1 < GATE_PANELS:
                        last.then_inc(drained["dve"], 1)
                        last = None
                        weights_low(l, i + 1)
                elif kind == "o":
                    t = a[1]
                    n = active(l).index(t)
                    s = 0 if t >= CT else 1
                    if n == 0:
                        dve.wait_ge(s_xr, 32 if l == 0 else 48)
                        for which in ("gt1", "A2", "B2"):
                            after(dve, "bc", l, which, 0)
                            if l < DEPTH - 1:
                                after(dve, "bc", l, which, 1)
                    link(tt(otmp, ps, BC["gt1", s], ALU.mult))
                    tt(XT[:, t, :], XT[:, t, :], otmp, ALU.add).then_inc(drained["dve"], 1)
                    dve.wait_ge(ssq_ready, norm_no(l, n + 1))
                    inv_mean(ssq[:, t:t + 1], ssq[:, t:t + 1], D).then_inc(var_ready, 1)
                    dve.wait_ge(rstd_ready, norm_no(l, n + 1))
                    if n >= 2:
                        after(dve, "f", l, active(l)[n - 2])
                        dve.wait_ge(s_h[n % 2], store_no(l, n) - 16)
                    fr = fb[:, n % 2, :]
                    link(stt(fr, XT[:, t, :], rstd[:, t:t + 1], BC["A2", s], ALU.mult, ALU.mult))
                    tt(fr, fr, BC["B2", s], ALU.add).then_inc(f_ready, 1)
                elif kind == "r":
                    if a[1] < NT - 2:
                        route(l, a[1])
                elif kind == "sg":
                    n = active(l).index(a[1])
                    dve.wait_ge(sh_silu, n + 1 + (NT if l else 0))
                    last = tt(hb[:, n % 2, :], s1[:, n % 2, :], ps[:, DE:2 * DE], ALU.mult)
                    last.then_inc(drained["dve"], 1)
                    last = None
                    if n < 2:
                        route(l, NT - 2 + n)
                elif kind == "pos":
                    t = a[1]
                    last = tt(posm[:, t * E:t * E + E], ps[:, 0:E], Mb[:, t * E:t * E + E], ALU.mult)
                elif kind == "cnt":
                    link(vec.tensor_copy(endc[0:E, 0:1], ps[0:E, 0:1]))
                    link(ts(endc[0:E, 1:1 + MAXB], cst("thr", E), endc[0:E, 0:1], None, ALU.is_lt))
                    link(vec.tensor_reduce(endc[0:E, 8:9], endc[0:E, 1:1 + MAXB], AX.X, ALU.add))
                    last = vec.tensor_copy(nbb[0:E, 0:1], endc[0:E, 8:9])
                elif kind == "end":
                    link(vec.tensor_copy(endc[0:E, 9:10], ps[0:E, 0:1]))
                    last = ts(Gb[0:E, :], cst("iotan", E), endc[0:E, 9:10], None, ALU.is_ge)
                elif kind == "tab":
                    ts(tabf[0:1, 0:TABN], ps[0:1, 0:TABN], float(E - 1), None, ALU.min)
                    link(tt(tabf[0:1, TABN:2 * TABN], cst("iotan", 1), ps[0:1, 128:128 + TABN], ALU.subtract))
                    ts(tabf[0:1, TABN:2 * TABN], tabf[0:1, TABN:2 * TABN], float(MAXB - 1), None, ALU.min)
                    link(vec.tensor_copy(tabf[0:1, 2 * TABN:2 * TABN + 1], ps[0:1, 256:257]))
                    last = vec.tensor_copy(tab[0:1, 0:2 * TABN + 1], tabf[0:1, 0:2 * TABN + 1])
                    last.then_inc(drained["dve"], 1)
                    last = None
                    dve.wait_ge(drained["dve"], job.count)
                    dve.sem_inc(tab_ready, 1)
                elif kind == "moe":
                    moe(l, "turns")
                    loop_end(dve)
                    combine(l)
                elif kind == "first":
                    moe(l, "first")
                if last is not None:
                    last.then_inc(drained["dve"], 1)
                elif kind in ("krp", "qrp", "qsp", "ksp"):
                    dve.sem_inc(drained["dve"], 1)
                if kind == "T" and a[1] == "m" and a[2] in HALF:
                    k = HALF.index(a[2])
                    dve.wait_ge(h_high, DK * l + k + 1)
                    tt(h_lo[:, k, :], hT[:, k, :], h_hi[:, k, :], ALU.subtract).then_inc(h_low, 1)
                for i in split_now("S" if kind == "T" else kind, a) if kind in ("T", "qsp") else ():
                    _, at, high = split_piece(l, i)
                    dve.wait_ge(piece_high, PIECES * l + i + 1)
                    tt(ring_r[:, at:at + 512], ring[:, at:at + 512], high, ALU.subtract).then_inc(piece_low, 1)

        @block.gpsimd
        def _(pool):
            gp = nc.gpsimd

            turns = s_turns

            def link(ins):
                step("pool", pool, ins)

            for l in range(DEPTH):
                pool.dma_start(bias[:, l * E:l * E + E], router_bias[l].partition_broadcast(P)).then_inc(s_row, 16)
                pool.dma_start(sink[:, 2 * l * HEADS:(2 * l + 1) * HEADS], swa_sink[l].partition_broadcast(P)).then_inc(s_row, 16)
            pool.wait_ge(s_con, 16)
            pool.wait_ge(s_row, 32 * DEPTH)
            for l in range(DEPTH):
                ins = gp.tensor_scalar(sink[:, (2 * l + 1) * HEADS:(2 * l + 2) * HEADS],
                                       sink[:, 2 * l * HEADS:(2 * l + 1) * HEADS], -1.0, None, ALU.mult)
            ins.then_inc(sink_neg, 1)
            pool.wait_ge(s_zero, 1)
            after(pool, "h", 0, 0)
            zr = zero[:].unsqueeze(1).broadcast_to([P, 4, 256])
            pool.dma_start(H[TOK:TOK + P, 0:D].rearrange("p (a n) -> p a n", a=4), zr).then_inc(s_hz, 16)
            pool.dma_start(H[TOK:TOK + P, D:HROW], zero[:, 0:E]).then_inc(s_hz, 16)
            pool.wait_ge(s_hz, 32)
            for l in range(DEPTH):
                A, sl = active(l), L[l]
                pool.wait_ge(filled, names["yT", l, "m", NT - 1].fill)
                gp.memset(K[:, 0:4 * UW], 0.0).then_inc(u_zero, 1)
                pool.wait_ge(u_zero, l + 1)
                lo, hi = (0, UW) if l < DEPTH - 1 else (UL - 8, UW)
                for g in range(4):
                    after(pool, "u", l, g)
                    u, bufs = U[:, g, :], [UT[:, 0, :], UT[:, 1, :]]
                    link(gp.tensor_tensor(bufs[0][:, lo + 1:hi], u[:, lo:hi - 1], u[:, lo + 1:hi], ALU.add))
                    src, a, b = 0, lo + 1, hi
                    for d in (1, 2, 4)[:g]:
                        a, b = a + d, b - d
                        link(gp.tensor_tensor(bufs[1 - src][:, a:b], bufs[src][:, a - d:b - d], bufs[src][:, a + d:b + d], ALU.add))
                        src = 1 - src
                    w = bufs[src]
                    link(gp.tensor_scalar(w[:, a:b], w[:, a:b], 1.0 / (2 << g), None, ALU.mult))
                    e0 = CONSTS["edges"][0] + 16 * g
                    edge = con[:, e0:e0 + 16].rearrange("p (a n) -> p a n", a=2)
                    for start, n in ((UL, SEQ), (UC, CTX))[:2 if l < DEPTH - 1 else 1]:
                        for side in range(2):
                            v = w[:, start + side * (n - 8):start + side * (n - 8) + 8]
                            ins = gp.tensor_tensor(v, v, edge[:, side, :], ALU.mult)
                        link(ins)
                    for start, n in ((UL, SEQ), (UC, CTX))[:2 if l < DEPTH - 1 else 1]:
                        ins = gp.tensor_tensor(u[:, start:start + n], w[:, start:start + n], u[:, start:start + n], ALU.subtract)
                    ins.then_inc(pooled, 1)
                    pool.wait_ge(pooled, 4 * l + g + 1)
                for n, t in enumerate(A):
                    pool.wait_ge(f_ready, n + 1 + (NT if l else 0))
                    pool.dma_start(H[t * P:t * P + P, 0:D], fb[:, n % 2, :]).then_inc(s_h[n % 2], 16)
                    pool.dma_start(ACC[1][t * P:t * P + P, :].rearrange("p (a n) -> p a n", a=4), zr).then_inc(s_acc1, 16)
                for n, t in enumerate(A):
                    pool.wait_ge(w_ready, n + 1 + (NT if l else 0))
                    pool.dma_start(H[t * P:t * P + P, D:HROW], Wt[:, n % 2, :]).then_inc(s_w[n % 2], 16)
                for n, t in enumerate(A[:-2]):
                    after(pool, "sd", l, t)
                    pool.dma_start(ACC[0][t * P:t * P + P, :], yb[:, n % 2, :]).then_inc(s_sh[n % 2], 16)
                for s in range(2):
                    for q in (s_h, s_w):
                        pool.wait_ge(q[s], store_no(l, len(A) - 2 + s))

                def gather(s, i4, count):
                    pool.wait_ge(sl["idx_ready"], count)
                    pool.sem_inc(turns, 1)
                    pool.indirect_dma_start(xg[:, s, :], None, H, bass.IndirectOffsetOnAxis(ap=idx[:, i4:i4 + 1], axis=0))\
                        .then_inc(sl[f"gat{s}"], 16)

                def add_block(s, i4, k, before):
                    pool.wait_ge(sl["y_a"], k + 2)
                    pool.wait_ge(sl["y_b"], k + 2)
                    pool.wait_ge(sl[f"scat{s}"], 16 * (before + 1))
                    pool.sem_inc(turns, 1)
                    pool.indirect_dma_start(ACC[s], bass.IndirectOffsetOnAxis(ap=idx[:, i4:i4 + 1], axis=0),
                                            yb[:, s, :], None, compute_op=ALU.add).then_inc(sl[f"scat{s}"], 16)

                for s in range(2):
                    gather(s, s, s + 1)
                for n in (len(A) - 2, len(A) - 1):
                    after(pool, "sd", l, A[n])
                    pool.dma_start(ACC[0][A[n] * P:A[n] * P + P, :], yb[:, n % 2, :]).then_inc(s_sh[n % 2], 16)
                for s in range(2):
                    pool.wait_ge(s_sh[s], store_no(l, len(A) - 2 + s))
                pool.wait_ge(s_acc1, 16 * (NT + (len(A) if l else 0)))
                for s in range(2):
                    pool.dma_start(ACC[s][TOK:TOK + P, :].rearrange("p (a n) -> p a n", a=4), zr).then_inc(sl[f"scat{s}"], 16)
                pool.wait_ge(tab_ready, l + 1)
                n_blocks = pool.value_load(tab[0:1, 2 * TABN:2 * TABN + 1], min_val=1, max_val=max_blocks(l))
                pool.wait_ge(sl["h_ready"], 1)
                gather(0, 2, 3)
                with pool.Fori(0, max_turns(l) // UNROLL) as m:
                    with pool.If(UNROLL * m < n_blocks):
                        for r in range(UNROLL):
                            n, s = UNROLL * m + r + 1, (r + 1) % 2
                            with pool.If(n < n_blocks):
                                pool.wait_ge(sl["h_ready"], n + 1)
                                gather(s, (r + 3) % 4, n + 3)
                            with pool.If(n <= n_blocks):
                                add_block(1 - s, r, n - 1, UNROLL // 2 * m + r // 2)
                pool.wait_ge(sl["scat0"], 16 * ((n_blocks + 1) // 2) + 16)
                pool.wait_ge(sl["scat1"], 16 * (n_blocks // 2) + 16)
                pool.wait_ge(sl["gat0"], 16 * ((n_blocks + 1) // 2) + 16)
                pool.wait_ge(sl["gat1"], 16 * (n_blocks // 2) + 16)
                pool.sem_inc(turns, 1)
                loop_end(pool)
                for i, t in enumerate(A):
                    a = comb[i]
                    pool.wait_ge(s_comb[i], 32 * (l + 1))
                    gp.tensor_tensor(a[:, 0, :], a[:, 0, :], a[:, 1, :], ALU.add).then_inc(summed, 1)


def constants():
    import numpy as np
    con = np.zeros((P, NCONST), np.float32)

    def put(name, v):
        a, b = CONSTS[name]
        con[:, a:b] = v
    i = np.arange(P)
    put("ident", np.eye(P))
    put("ones", 1.0)
    put("perm16", (i[:, None] ^ 16) == i[None, :])
    put("perm8", (i[:, None] ^ 8) == i[None, :])
    put("tri", i[:, None] <= i[None, :])
    put("tokid", np.stack([np.stack([i, np.full(P, P * t), np.ones(P)], 1) for t in range(NT)], 1).reshape(P, -1))
    put("thr", P * np.arange(MAXB))
    put("sel2", i[:, None] % 32 == np.arange(2)[None, :])
    put("iotan", np.arange(TABN))
    put("dummy", (TOK + i)[:, None])
    put("negdummy", -(TOK + i)[:, None])
    edges = np.ones((4, 2, 8))
    for g in range(4):
        w = 2 << g
        for j in range(8):
            edges[g, 0, j] = w / (j + w // 2 - max(j - w // 2, 0))
            edges[g, 1, j] = w / (min(w // 2, 8 - j) + w // 2)
    put("edges", edges.reshape(1, -1))
    put("lower", (np.arange(8)[None, :] < np.arange(8)[:, None]).reshape(1, -1))
    put("slot1", 1 + np.arange(TOK))
    prev = np.where(i[None, :] >= i[:, None], 0.0, -NEG)
    nxt = np.where(i[None, :] <= i[:, None], 0.0, -NEG)
    mask = np.concatenate([prev, np.zeros((P, P)), nxt, np.zeros((P, CTX)), prev, np.zeros((P, 3 * P))], 1)

    def rope(dim):
        n = dim // 4
        t = np.arange(SEQ)
        inv = np.float32(10000.0) ** (-np.arange(n, dtype=np.float32) / np.float32(n))
        table = np.zeros((P, 2, SEQ), np.float32)
        for p in range(P):
            part, f = p % dim // n, p % n
            pos = (t // 64 if part < 2 else t % 64).astype(np.float32)
            ang = pos * inv[f]
            table[p, 0] = np.cos(ang)
            table[p, 1] = np.sin(ang) * (-1 if part % 2 == 0 else 1)
        return table
    return {"consts": con, "mask": mask.astype(np.float32), "rope_mla": rope(ROPE), "rope_swa": rope(HD)}


_INS = ['x', 'c', 'ctx', 'c_ctx', 'w_mod', 'b_mod', 'g_mix', 'g_ffn', 'w_in', 'g_mla_q', 'g_mla_kv', 'w_mla_uq',
        'w_mla_ukv', 'w_pool', 'pool_scale', 'swa_sink', 'w_br_mla', 'w_br_pool', 'w_br_swa', 'w_out', 'w_router',
        'router_bias', 'w_exp_gate', 'w_exp_up', 'w_exp_down', 'w_sh_gate', 'w_sh_up', 'w_sh_down', 'g_final']


def kernel(**inputs):
    import numpy as np
    import concourse.bacc as bacc
    from concourse.bass_utils import run_bass_kernel_spmd
    nc = bacc.Bacc("TRN2", target_bir_lowering=False, num_devices=1)
    arrays, args = {}, []
    for name, a in [(n, inputs[n]) for n in _INS] + list(constants().items()):
        a = np.ascontiguousarray(a)
        arrays[f"in_{name}"] = a
        args.append(nc.dram_tensor(f"in_{name}", a.shape, mybir.dt.from_np(a.dtype), kind="ExternalInput").ap())
    args.append(nc.dram_tensor("out_0", (1, SEQ, D), F32, kind="ExternalOutput").ap())
    build(nc, *args)
    r = run_bass_kernel_spmd(nc, [arrays], core_ids=[0])
    return r.results[0]["out_0"]
```
